# Optimizing a Trainium2 kernel written in Bass

```python
import math
import jax, jax.numpy as jnp
from jax import lax
import numpy as np

D_MODEL = 1024
BATCH = 1
SEQ = 256
DEPTH = 1
DEC_BATCH = 8
DEC_SEQ = 1
PAST_LEN = 1024
PAGE_SIZE = 128

SSD_EXPAND = 2
D_INNER = SSD_EXPAND * D_MODEL
SSD_HEAD_DIM = 64
SSD_HEADS = D_INNER // SSD_HEAD_DIM
SSD_GROUPS = 8
SSD_HEADS_PER_GROUP = SSD_HEADS // SSD_GROUPS
D_STATE = 128
CONV_W = 4
CONV_DIM = D_INNER + 2 * SSD_GROUPS * D_STATE
SSD_CHUNK = 128
ATT_HEADS = 16
ATT_HEAD_DIM = 64
ATT_WIDTH = ATT_HEADS * ATT_HEAD_DIM
KV_HEADS = 4
KV_REP = ATT_HEADS // KV_HEADS
IDX_HEADS = 8
IDX_DIM = 64
TOPK_KEYS_MAX = 256
Q_BLOCK = 128
NUM_BUCKETS = 32
MAX_DISTANCE = 128
PEER_HEADS = 8
PEER_N_KEYS = 128
PEER_EXPERTS = PEER_N_KEYS * PEER_N_KEYS
PEER_KEY_DIM = 256
PEER_HALF = PEER_KEY_DIM // 2
PEER_TOPK = 16
PEER_BLOCK = 128
EPS = 1e-6
IN_SPLITS = (D_INNER, CONV_DIM, SSD_HEADS,
             ATT_WIDTH, KV_HEADS * ATT_HEAD_DIM, KV_HEADS * ATT_HEAD_DIM,
             IDX_HEADS * IDX_DIM, IDX_DIM, IDX_HEADS,
             D_MODEL, D_MODEL)
IN_COLS = sum(IN_SPLITS)

kernel_name = 'hybrid_ssd_dsa_peer_step'

F32 = jnp.float32

def rms_norm(x, g):
    xf = x.astype(F32)
    y = xf * lax.rsqrt(jnp.mean(xf * xf, axis=-1, keepdims=True) + EPS)
    return (y * g.astype(F32)).astype(x.dtype)

def split_cols(proj):
    offs = np.cumsum(np.array(IN_SPLITS))[:-1].tolist()
    return jnp.split(proj, offs, axis=-1)

def causal_dwconv(xpad, w, b):
    out = lax.conv_general_dilated(xpad, w[:, None, :], window_strides=(1,), padding='VALID',
                                   dimension_numbers=('NWC', 'WIO', 'NWC'),
                                   feature_group_count=xpad.shape[-1])
    return jax.nn.silu(out + b)

def t5_bucket(dist):
    n = jnp.maximum(dist, 0)
    max_exact = NUM_BUCKETS // 2
    nf = jnp.maximum(n, 1).astype(F32)
    large = max_exact + (jnp.log(nf / max_exact) / math.log(MAX_DISTANCE / max_exact)
                         * (NUM_BUCKETS - max_exact)).astype(jnp.int32)
    large = jnp.minimum(large, NUM_BUCKETS - 1)
    return jnp.where(n < max_exact, n, large)

def indexer_topk(iq, iw, ik, q_pos, n_sel):
    s = jnp.einsum('bthd,bsd->bths', iq, ik, preferred_element_type=F32) * IDX_DIM ** -0.5
    score = jnp.einsum('bth,bths->bts', iw.astype(F32), jax.nn.relu(s))
    k_pos = jnp.arange(ik.shape[1])
    score = jnp.where(k_pos[None, None, :] <= q_pos[None, :, None], score, -jnp.inf)
    _, idx = lax.top_k(score, n_sel)
    return idx

def sparse_attention(q, k_sel, v_sel, q_pos, idx, rel_bias):
    B, T = q.shape[:2]
    K = idx.shape[-1]
    qg = q.reshape(B, T, KV_HEADS, KV_REP, ATT_HEAD_DIM)
    logits = jnp.einsum('btgrd,btkgd->btgrk', qg, k_sel, preferred_element_type=F32) * ATT_HEAD_DIM ** -0.5
    dist = q_pos[None, :, None] - idx
    bias = rel_bias.astype(F32)[t5_bucket(dist)]
    bias = bias.reshape(B, T, K, KV_HEADS, KV_REP).transpose(0, 1, 3, 4, 2)
    valid = (dist >= 0)[:, :, None, None, :]
    p = jax.nn.softmax(jnp.where(valid, logits + bias, -jnp.inf), axis=-1)
    out = jnp.einsum('btgrk,btkgd->btgrd', p.astype(v_sel.dtype), v_sel)
    return out.reshape(B, T, ATT_WIDTH)

def gather_rows(rows, ids):
    return jax.vmap(lambda r, i: r[i])(rows, ids)

def attn_inputs(q_raw, k_raw, v_raw, iq_raw, iw_raw, p):
    B, T = q_raw.shape[:2]
    q = rms_norm(q_raw.reshape(B, T, ATT_HEADS, ATT_HEAD_DIM), p['q_norm_g'])
    k = rms_norm(k_raw.reshape(B, T, KV_HEADS, ATT_HEAD_DIM), p['k_norm_g'])
    v = v_raw.reshape(B, T, KV_HEADS, ATT_HEAD_DIM)
    iq = iq_raw.reshape(B, T, IDX_HEADS, IDX_DIM)
    iw = iw_raw * IDX_HEADS ** -0.5
    return q, k, v, iq, iw

def attention_prompt(q, k, v, iq, ik, iw, rel_bias):
    B, T = q.shape[:2]
    n_sel = min(TOPK_KEYS_MAX, T // 4)
    nb = T // Q_BLOCK

    def blocks(a):
        return jnp.moveaxis(a.reshape(B, nb, Q_BLOCK, *a.shape[2:]), 1, 0)

    pos = jnp.arange(T).reshape(nb, Q_BLOCK)

    def one_block(inp):
        qb, iqb, iwb, posb = inp
        idx = indexer_topk(iqb, iwb, ik, posb, n_sel)
        return sparse_attention(qb, gather_rows(k, idx), gather_rows(v, idx), posb, idx, rel_bias)

    out = lax.map(one_block, (blocks(q), blocks(iq), blocks(iw), pos))
    return jnp.moveaxis(out, 0, 1).reshape(B, T, ATT_WIDTH)

def attention_sample(q, k, v, iq, ik, iw, rel_bias, cache_k, cache_v, cache_ik, page_table):
    DB, DS = q.shape[:2]
    past = page_table.shape[1] * PAGE_SIZE
    n_sel = min(TOPK_KEYS_MAX, (past + DS) // 4)
    rows = (page_table[:, :, None] * PAGE_SIZE
            + jnp.arange(PAGE_SIZE, dtype=jnp.int32)[None, None, :]).reshape(DB, past)
    pool_k = cache_k.reshape(-1, KV_HEADS, ATT_HEAD_DIM)
    pool_v = cache_v.reshape(-1, KV_HEADS, ATT_HEAD_DIM)
    pool_ik = cache_ik.reshape(-1, IDX_DIM)
    ik_all = jnp.concatenate([pool_ik[rows], ik], axis=1)
    q_pos = past + jnp.arange(DS)
    idx = indexer_topk(iq, iw, ik_all, q_pos, n_sel)
    is_new = (idx >= past)[..., None, None]
    prow = jnp.take_along_axis(rows, jnp.minimum(idx, past - 1).reshape(DB, -1), axis=1).reshape(idx.shape)
    nidx = jnp.clip(idx - past, 0, DS - 1)
    k_sel = jnp.where(is_new, gather_rows(k, nidx), pool_k[prow])
    v_sel = jnp.where(is_new, gather_rows(v, nidx), pool_v[prow])
    return sparse_attention(q, k_sel, v_sel, q_pos, idx, rel_bias)

def ssd_inputs(xbc_conv, dt_raw, p):
    B, T = xbc_conv.shape[:2]
    x, bm, cm = jnp.split(xbc_conv, [D_INNER, D_INNER + SSD_GROUPS * D_STATE], axis=-1)
    x = x.reshape(B, T, SSD_GROUPS, SSD_HEADS_PER_GROUP, SSD_HEAD_DIM)
    bm = bm.reshape(B, T, SSD_GROUPS, D_STATE)
    cm = cm.reshape(B, T, SSD_GROUPS, D_STATE)
    dt = jax.nn.softplus((dt_raw + p['dt_bias']).astype(F32)).reshape(B, T, SSD_GROUPS, SSD_HEADS_PER_GROUP)
    A = -jnp.exp(p['a_log'].astype(F32)).reshape(SSD_GROUPS, SSD_HEADS_PER_GROUP)
    return x, bm, cm, dt, A

def ssd_chunked(xs, dt, A, bm, cm):
    B, T = xs.shape[:2]
    nc = T // SSD_CHUNK

    def to_chunks(a):
        return jnp.moveaxis(a.reshape(B, nc, SSD_CHUNK, *a.shape[2:]), 1, 0)

    causal = jnp.tril(jnp.ones((SSD_CHUNK, SSD_CHUNK), dtype=bool))[None, :, :, None, None]

    def step(h, inp):
        xc, dtc, bc, cc = inp
        acum = jnp.cumsum(dtc * A, axis=1)
        seg = acum[:, :, None] - acum[:, None, :]
        lmat = jnp.exp(jnp.where(causal, seg, -jnp.inf))
        cb = jnp.einsum('btgn,bsgn->btsg', cc, bc, preferred_element_type=F32)
        y = jnp.einsum('btsg,btsgr,bsgr,bsgrp->btgrp', cb, lmat, dtc, xc)
        y = y + jnp.einsum('btgn,bgrpn,btgr->btgrp', cc, h, jnp.exp(acum))
        decay = jnp.exp(acum[:, -1:] - acum) * dtc
        h = h * jnp.exp(acum[:, -1])[..., None, None] + jnp.einsum('bsgn,bsgr,bsgrp->bgrpn', bc, decay, xc)
        return h, y

    h0 = jnp.zeros((B, SSD_GROUPS, SSD_HEADS_PER_GROUP, SSD_HEAD_DIM, D_STATE), F32)
    hT, ys = lax.scan(step, h0, (to_chunks(xs), to_chunks(dt), to_chunks(bm), to_chunks(cm)))
    return jnp.moveaxis(ys, 0, 1).reshape(xs.shape), hT

def ssd_recurrent(xs, dt, A, bm, cm, h0):
    def step(h, inp):
        xt, dtt, bt, ct = inp
        h = h * jnp.exp(dtt * A)[..., None, None] + jnp.einsum('bgr,bgrp,bgn->bgrpn', dtt, xt, bt)
        y = jnp.einsum('bgn,bgrpn->bgrp', ct, h)
        return h, y

    seq = (jnp.moveaxis(xs, 1, 0), jnp.moveaxis(dt, 1, 0), jnp.moveaxis(bm, 1, 0), jnp.moveaxis(cm, 1, 0))
    hT, ys = lax.scan(step, h0, seq)
    return jnp.moveaxis(ys, 0, 1), hT

def ssd_output(y, xs, z, p):
    B, T = z.shape[:2]
    d = p['d_skip'].astype(F32).reshape(SSD_GROUPS, SSD_HEADS_PER_GROUP, 1)
    y = (y + d * xs).reshape(B, T, D_INNER) * jax.nn.silu(z.astype(F32))
    yg = y.reshape(B, T, SSD_GROUPS, D_INNER // SSD_GROUPS)
    yg = yg * lax.rsqrt(jnp.mean(yg * yg, axis=-1, keepdims=True) + EPS)
    return (yg.reshape(B, T, D_INNER) * p['ssd_norm_g'].astype(F32)).astype(z.dtype)

def peer(h, p):
    n = h.shape[0]
    q = (h @ p['peer_wq']).reshape(n, PEER_HEADS, 2, PEER_HALF)
    s = jnp.einsum('nhcd,chkd->nhck', q, p['peer_keys'], preferred_element_type=F32)
    s1, i1 = lax.top_k(s[:, :, 0], PEER_TOPK)
    s2, i2 = lax.top_k(s[:, :, 1], PEER_TOPK)
    cand_s = (s1[..., :, None] + s2[..., None, :]).reshape(n, PEER_HEADS, PEER_TOPK * PEER_TOPK)
    cand_i = (i1[..., :, None] * PEER_N_KEYS + i2[..., None, :]).reshape(n, PEER_HEADS, PEER_TOPK * PEER_TOPK)
    top_s, pos = lax.top_k(cand_s, PEER_TOPK)
    eidx = jnp.take_along_axis(cand_i, pos, axis=-1)
    g = jax.nn.softmax(top_s, axis=-1)
    act = jax.nn.gelu(jnp.einsum('nd,nhkd->nhk', h, p['peer_u'][eidx], preferred_element_type=F32))
    return jnp.einsum('nhk,nhkd->nd', (g * act).astype(h.dtype), p['peer_v'][eidx])

def mixer_projection(x, p):
    return split_cols(rms_norm(x, p['norm1_g']) @ p['w_in'])

def merge_and_channel(x, y_ssd, y_att, g_a, g_b, p, blocked):
    merged = (jax.nn.sigmoid(g_a) * (y_ssd @ p['w_branch_a'])
              + jax.nn.sigmoid(g_b) * (y_att @ p['w_branch_b']))
    x = x + merged @ p['w_out']
    h = rms_norm(x, p['norm2_g'])
    B, T, _ = h.shape
    hf = h.reshape(B * T, D_MODEL)
    if blocked:
        out = lax.map(lambda hb: peer(hb, p), hf.reshape(-1, PEER_BLOCK, D_MODEL)).reshape(B * T, D_MODEL)
    else:
        out = peer(hf, p)
    return x + out.reshape(B, T, D_MODEL)

def layer_prompt(x, p, rel_bias):
    z, xbc, dt_raw, q_raw, k_raw, v_raw, iq_raw, ik, iw_raw, g_a, g_b = mixer_projection(x, p)
    B = x.shape[0]
    xpad = jnp.concatenate([jnp.zeros((B, CONV_W - 1, CONV_DIM), xbc.dtype), xbc], axis=1)
    conv_state = xpad[:, -(CONV_W - 1):]
    xs, bm, cm, dt, A = ssd_inputs(causal_dwconv(xpad, p['conv_w'], p['conv_b']), dt_raw, p)
    y, hT = ssd_chunked(xs, dt, A, bm, cm)
    y_ssd = ssd_output(y, xs, z, p)
    q, k, v, iq, iw = attn_inputs(q_raw, k_raw, v_raw, iq_raw, iw_raw, p)
    y_att = attention_prompt(q, k, v, iq, ik, iw, rel_bias)
    out = merge_and_channel(x, y_ssd, y_att, g_a, g_b, p, True)
    ssm_state = hT.reshape(B, SSD_HEADS, SSD_HEAD_DIM, D_STATE).astype(x.dtype)
    return out, (k, v, ik, ssm_state, conv_state)

def layer_sample(x, p, rel_bias, cache_k, cache_v, cache_ik, page_table, state_ssm, state_conv):
    z, xbc, dt_raw, q_raw, k_raw, v_raw, iq_raw, ik, iw_raw, g_a, g_b = mixer_projection(x, p)
    DB = x.shape[0]
    xcat = jnp.concatenate([state_conv.astype(xbc.dtype), xbc], axis=1)
    conv_state = xcat[:, -(CONV_W - 1):]
    xs, bm, cm, dt, A = ssd_inputs(causal_dwconv(xcat, p['conv_w'], p['conv_b']), dt_raw, p)
    h0 = state_ssm.astype(F32).reshape(DB, SSD_GROUPS, SSD_HEADS_PER_GROUP, SSD_HEAD_DIM, D_STATE)
    y, hT = ssd_recurrent(xs, dt, A, bm, cm, h0)
    y_ssd = ssd_output(y, xs, z, p)
    q, k, v, iq, iw = attn_inputs(q_raw, k_raw, v_raw, iq_raw, iw_raw, p)
    y_att = attention_sample(q, k, v, iq, ik, iw, rel_bias, cache_k, cache_v, cache_ik, page_table)
    out = merge_and_channel(x, y_ssd, y_att, g_a, g_b, p, False)
    ssm_state = hT.reshape(DB, SSD_HEADS, SSD_HEAD_DIM, D_STATE).astype(state_ssm.dtype)
    return out, (k, v, ik, ssm_state, conv_state)

def setup_inputs(seed: int = 0) -> dict:
    key = jax.random.key(seed)
    ks = jax.random.split(key, 32)
    n_pages = PAST_LEN // PAGE_SIZE
    n_pool = (DEC_BATCH * n_pages * 5) // 4

    def nrm(k, shape, scale):
        return scale * jax.random.normal(k, shape, F32)

    dt0 = jnp.exp(jax.random.uniform(ks[13], (DEPTH, SSD_HEADS), F32, math.log(1e-3), math.log(1e-1)))
    return {
        'x_prompt': nrm(ks[0], (BATCH, SEQ, D_MODEL), 1.0),
        'x_sample': nrm(ks[1], (DEC_BATCH, DEC_SEQ, D_MODEL), 1.0),
        'cache_k': nrm(ks[2], (DEPTH, n_pool, PAGE_SIZE, KV_HEADS, ATT_HEAD_DIM), 1.0),
        'cache_v': nrm(ks[3], (DEPTH, n_pool, PAGE_SIZE, KV_HEADS, ATT_HEAD_DIM), 1.0),
        'cache_idx_k': nrm(ks[4], (DEPTH, n_pool, PAGE_SIZE, IDX_DIM), 1.0),
        'state_ssm': nrm(ks[5], (DEPTH, DEC_BATCH, SSD_HEADS, SSD_HEAD_DIM, D_STATE), 0.1),
        'state_conv': nrm(ks[6], (DEPTH, DEC_BATCH, CONV_W - 1, CONV_DIM), 1.0),
        'page_table': jax.random.permutation(ks[7], n_pool)[:DEC_BATCH * n_pages]
                      .reshape(DEC_BATCH, n_pages).astype(jnp.int32),
        'rel_bias': nrm(ks[8], (NUM_BUCKETS, ATT_HEADS), 0.5),
        'norm1_g': 1.0 + nrm(ks[9], (DEPTH, D_MODEL), 0.02),
        'w_in': nrm(ks[10], (DEPTH, D_MODEL, IN_COLS), D_MODEL ** -0.5),
        'conv_w': nrm(ks[11], (DEPTH, CONV_W, CONV_DIM), CONV_W ** -0.5),
        'conv_b': nrm(ks[12], (DEPTH, CONV_DIM), 0.02),
        'dt_bias': dt0 + jnp.log(-jnp.expm1(-dt0)),
        'a_log': jnp.log(jax.random.uniform(ks[14], (DEPTH, SSD_HEADS), F32, 1.0, 16.0)),
        'd_skip': 1.0 + nrm(ks[15], (DEPTH, SSD_HEADS), 0.1),
        'ssd_norm_g': 1.0 + nrm(ks[16], (DEPTH, D_INNER), 0.02),
        'q_norm_g': 1.0 + nrm(ks[17], (DEPTH, ATT_HEAD_DIM), 0.02),
        'k_norm_g': 1.0 + nrm(ks[18], (DEPTH, ATT_HEAD_DIM), 0.02),
        'w_branch_a': nrm(ks[19], (DEPTH, D_INNER, D_MODEL), D_INNER ** -0.5),
        'w_branch_b': nrm(ks[20], (DEPTH, ATT_WIDTH, D_MODEL), ATT_WIDTH ** -0.5),
        'w_out': nrm(ks[21], (DEPTH, D_MODEL, D_MODEL), D_MODEL ** -0.5),
        'norm2_g': 1.0 + nrm(ks[22], (DEPTH, D_MODEL), 0.02),
        'peer_wq': nrm(ks[23], (DEPTH, D_MODEL, PEER_HEADS * PEER_KEY_DIM), D_MODEL ** -0.5),
        'peer_keys': nrm(ks[24], (DEPTH, 2, PEER_HEADS, PEER_N_KEYS, PEER_HALF), PEER_HALF ** -0.5),
        'peer_u': nrm(ks[25], (DEPTH, PEER_EXPERTS, D_MODEL), D_MODEL ** -0.5),
        'peer_v': nrm(ks[26], (DEPTH, PEER_EXPERTS, D_MODEL), PEER_HEADS ** -0.5),
    }

def reference(x_prompt, x_sample, cache_k, cache_v, cache_idx_k, state_ssm, state_conv, page_table,
              rel_bias, norm1_g, w_in, conv_w, conv_b, dt_bias, a_log, d_skip, ssd_norm_g,
              q_norm_g, k_norm_g, w_branch_a, w_branch_b, w_out, norm2_g,
              peer_wq, peer_keys, peer_u, peer_v):
    yp, ys = x_prompt, x_sample
    new_p, new_s = [], []
    for l in range(DEPTH):
        p = dict(norm1_g=norm1_g[l], w_in=w_in[l], conv_w=conv_w[l], conv_b=conv_b[l],
                 dt_bias=dt_bias[l], a_log=a_log[l], d_skip=d_skip[l], ssd_norm_g=ssd_norm_g[l],
                 q_norm_g=q_norm_g[l], k_norm_g=k_norm_g[l], w_branch_a=w_branch_a[l],
                 w_branch_b=w_branch_b[l], w_out=w_out[l], norm2_g=norm2_g[l],
                 peer_wq=peer_wq[l], peer_keys=peer_keys[l], peer_u=peer_u[l], peer_v=peer_v[l])
        yp, sp = layer_prompt(yp, p, rel_bias)
        ys, ss = layer_sample(ys, p, rel_bias, cache_k[l], cache_v[l], cache_idx_k[l], page_table,
                              state_ssm[l], state_conv[l])
        new_p.append(sp)
        new_s.append(ss)

    def stk(group, i):
        return jnp.stack([st[i] for st in group], axis=0)

    return (yp, ys,
            stk(new_p, 0), stk(new_p, 1), stk(new_p, 2), stk(new_p, 3), stk(new_p, 4),
            stk(new_s, 0), stk(new_s, 1), stk(new_s, 2), stk(new_s, 3), stk(new_s, 4))


_drawn_inputs = setup_inputs


def setup_inputs(seed=0):
    import zlib

    import numpy as np

    out = dict(_drawn_inputs(seed))
    spreads = {}
    factors = {'ssd_norm_g': 8.316,
     'q_norm_g': 35.494,
     'k_norm_g': 8.203,
     'norm2_g': 11.423,
     'rel_bias': 4.615}
    for name, (base, spread) in spreads.items():
        noise = np.random.default_rng([zlib.crc32(name.encode()), seed]).standard_normal(out[name].shape)
        drawn = base * np.exp(spread * noise) if base else spread * noise
        out[name] = __import__('jax').numpy.asarray(drawn.astype(out[name].dtype))
    for name, factor in factors.items():
        out[name] = (out[name] * factor).astype(out[name].dtype)
    return out
```

```python
from contextlib import ExitStack

import concourse.bass as bass
from concourse import mybir
import numpy as np

ALU = mybir.AluOpType
ACT = mybir.ActivationFunctionType
AX = mybir.AxisListType
F32 = mybir.dt.float32
I32 = mybir.dt.int32
U32 = mybir.dt.uint32

P = 128
D_MODEL, D_INNER, CONV_DIM = 1024, 2048, 4096
KD = D_MODEL // P
KI = D_INNER // P
KC = CONV_DIM // P
TP, TS = 256, 8
T = TP + TS
CW = 4
RAW = 3 + TP + 4 * TS
CV = RAW - 3
SAMP0 = 3 + TP
HEADS, KVH, REP, HD = 16, 4, 4, 64
IH = 8
SSDH, GROUPS, NST = 32, 8, 128
PAGES, PG = 8, 128
PAST = PAGES * PG
NKS = PAST + 1
SEL_P, SEL_S = 64, 256
NB = 32
PH, PK, TOPK = 8, 128, 16
NEXP = PK * PK
EPS = 1e-6
NEG = -1.0e30
LOW = -3.0e38

N_Z, N_XBC, N_ATT, N_GATE = KI, KC, 16, 16
N_TILES = N_Z + N_XBC + N_ATT + N_GATE + 1
Q0, K0, V0, IQ0 = 0, 8, 10, 12
IW_P, DT_P = 64, 96
WSLOTS = 4

C_ID, C_ONES, C_J, C_TRI, C_BLK, C_NEGT, C_SELLO, C_SELHI, C_END = (P * i for i in range(9))
CX_N = 256
BIAS_N = 384


def tensors(nc, ctx, **shapes):
    return [ctx.enter_context(nc.sbuf_tensor(n, [s[0], *s[1:]], F32)) for n, s in shapes.items()]


class Kept:
    pass


IN_NAMES = ("d_alog", "d_cb", "d_cik", "d_ck", "d_cst", "d_cv", "d_cw", "d_cx", "d_dskip", "d_dtb", "d_g1",
            "d_g2", "d_gqk", "d_gssd", "d_hot", "d_hots", "d_keys", "d_old", "d_pages", "d_rel",
            "d_relbh", "d_spread", "d_state", "d_uv", "d_w_ab", "d_w_in", "d_w_out", "d_wq", "d_xT")


def signals(nc, ctx, prefix=""):
    made = []

    def close():
        nc.clear_and_free_semaphores(made)
        nc.all_engine_barrier()
    ctx.callback(close)

    def sem(name):
        made.append(nc.alloc_semaphore(prefix + name))
        return made[-1]
    return sem


def norm_in(nc, k):
    with ExitStack() as ctx:
        sem = signals(nc, ctx)
        xsq, g1, rms = tensors(nc, ctx, n1_xsq=(P, KD, T), n1_g=(P, KD), n1_rms=(P, T))
        ps = ctx.enter_context(nc.psum_tensor("n1_ps", [P, 512], F32))
        x_loaded, c_loaded, squared, summed, rooted, inverted, done = (sem(n) for n in (
            "n1_x", "n1_c", "n1_sq", "n1_sum", "n1_root", "n1_inv", "n1_done"))
        block = ctx.enter_context(nc.Block())

        @block.sync
        def _(sp):
            sp.dma_start(k.xT[:], k.d_xT[:]).then_inc(x_loaded, 16)
            sp.dma_start(k.cst[:], k.d_cst[:]).then_inc(c_loaded, 16)
            sp.dma_start(k.cx[:], k.d_cx[:]).then_inc(c_loaded, 16)
            sp.dma_start(g1[:], k.d_g1[:]).then_inc(c_loaded, 16)
            sp.wait_ge(c_loaded, 48)

        @block.scalar
        def _(act):
            act.wait_ge(x_loaded, 16)
            act.activation(xsq[:], k.xT[:], ACT.Square).then_inc(squared, 1)
            act.wait_ge(c_loaded, 48)
            act.wait_ge(summed, 1)
            act.activation(rms[:], ps[:, 0:T], ACT.Sqrt, scale=1.0 / D_MODEL, bias=k.eps).then_inc(rooted, 1)

        @block.tensor
        def _(pe):
            pe.wait_ge(c_loaded, 48)
            pe.wait_ge(squared, 1)
            for c in range(KD):
                mm = pe.matmul(ps[:, 0:T], k.ones, xsq[:, c, :], start=c == 0, stop=c == KD - 1)
            mm.then_inc(summed, 1)

        @block.vector
        def _(dve):
            dve.wait_ge(rooted, 1)
            dve.reciprocal(rms[:], rms[:]).then_inc(inverted, 1)
            dve.wait_ge(inverted, 1)
            dve.wait_ge(c_loaded, 48)
            for c in range(KD):
                dve.scalar_tensor_tensor(out=k.xn[:, c, :], in0=k.xT[:, c, :], scalar=g1[:, c:c + 1],
                                         in1=rms[:], op0=ALU.mult, op1=ALU.mult).then_inc(done, 1)
            dve.wait_ge(done, KD)


def project_in(nc, k):
    with ExitStack() as ctx:
        sem = signals(nc, ctx)
        w, raw, cv, cw, cb, old, tail_p, tail_s = tensors(
            nc, ctx, pi_w=(P, WSLOTS, KD * P), pi_raw=(P, WSLOTS, RAW), pi_cv=(P, WSLOTS, CV),
            pi_cw=(P, KC, CW), pi_cb=(P, KC), pi_old=(P, KC, TS, 3), pi_tail_p=(P, KC, 3),
            pi_tail_s=(P, KC, TS, 3))
        ps = ctx.enter_context(nc.psum_tensor("pi_ps", [P, WSLOTS, 512], F32))
        w_loaded = [sem(f"pi_w{s}") for s in range(WSLOTS)]
        c_loaded, zeroed, multiplied, evacuated, filled, saved, tap, convolved, stored = (sem(n) for n in (
            "pi_c", "pi_zero", "pi_mm", "pi_evac", "pi_fill", "pi_saved", "pi_tap", "pi_conv", "pi_store"))
        stored_cv = sem("pi_silu")
        block = ctx.enter_context(nc.Block())

        def blocks(t):
            return t[:, SAMP0:SAMP0 + 4 * TS].rearrange("p (b j) -> p b j", j=4)

        @block.sync
        def _(sp):
            def load(i, s):
                sp.dma_start(w[:, s, :], k.d_w_in[bass.ds(i * WSLOTS + s, 1)].rearrange("a p n -> p (a n)")
                             ).then_inc(w_loaded[s], 16)
            for s in range(WSLOTS):
                load(0, s)
            with sp.Fori(1, N_TILES // WSLOTS) as i:
                for s in range(WSLOTS):
                    sp.wait_ge(multiplied, (i - 1) * WSLOTS + s + 1)
                    load(i, s)
            sp.wait_ge(multiplied, N_TILES - WSLOTS)
            sp.dma_start(w[:, 0, :], k.d_w_in[N_TILES - 1]).then_inc(w_loaded[0], 16)
            sp.wait_ge(saved, KC)
            sp.dma_start(k.o_conv_p[:], tail_p[:]).then_inc(stored, 16)
            sp.dma_start(k.o_conv_s[:], tail_s[:]).then_inc(stored, 16)
            sp.wait_ge(stored, 32)

        @block.tensor
        def _(pe):
            def tile(i, s, first):
                pe.wait_ge(w_loaded[s], (i + 1) * 16)
                if not first:
                    pe.wait_ge(evacuated, (i - 1) * WSLOTS + s + 1)
                for c in range(KD):
                    mm = pe.matmul(ps[:, s, 0:T], w[:, s, c * P:(c + 1) * P], k.xn[:, c, :],
                                   start=c == 0, stop=c == KD - 1)
                mm.then_inc(multiplied, 1)
            for s in range(WSLOTS):
                tile(0, s, True)
            with pe.Fori(1, N_TILES // WSLOTS) as i:
                for s in range(WSLOTS):
                    tile(i, s, False)
            tile(N_TILES // WSLOTS, 0, False)

        @block.scalar
        def _(act):
            act.dma_start(cw[:], k.d_cw[:]).then_inc(c_loaded, 16)
            act.dma_start(cb[:], k.d_cb[:]).then_inc(c_loaded, 16)
            act.dma_start(old[:], k.d_old[:]).then_inc(c_loaded, 16)
            with act.Fori(0, N_Z // WSLOTS) as i:
                for s in range(WSLOTS):
                    act.wait_ge(multiplied, i * WSLOTS + s + 1)
                    act.activation(k.zs[:, bass.ds(i * WSLOTS + s, 1), :], ps[:, s:s + 1, 0:T],
                                   ACT.Silu).then_inc(evacuated, 1)

            def silu(n, s):
                act.wait_ge(convolved, n + 1)
                act.activation(k.xbc[:, bass.ds(n, 1), :], cv[:, s:s + 1, :], ACT.Silu).then_inc(stored_cv, 1)

            def raw_tile(i, s, first):
                n = i * WSLOTS + s
                act.wait_ge(multiplied, n + N_Z + 1)
                if not first:
                    act.wait_ge(convolved, n - WSLOTS + 1)
                    act.wait_ge(saved, n - WSLOTS + 1)
                act.activation(raw[:, s, 3:3 + TP], ps[:, s, 0:TP], ACT.Copy)
                act.activation(blocks(raw[:, s])[:, :, 3], ps[:, s, TP:T], ACT.Copy).then_inc(evacuated, 1)
            for s in range(WSLOTS):
                raw_tile(0, s, True)
                if s:
                    silu(s - 1, s - 1)
            with act.Fori(1, N_XBC // WSLOTS) as i:
                for s in range(WSLOTS):
                    raw_tile(i, s, False)
                    silu(i * WSLOTS + s - 1, (s - 1) % WSLOTS)
            silu(N_XBC - 1, WSLOTS - 1)
            with act.Fori(0, N_ATT // WSLOTS) as i:
                for s in range(WSLOTS):
                    act.wait_ge(multiplied, i * WSLOTS + s + 1 + N_Z + N_XBC)
                    act.activation(k.att[:, bass.ds(i * WSLOTS + s, 1), :], ps[:, s:s + 1, 0:T],
                                   ACT.Copy).then_inc(evacuated, 1)
            with act.Fori(0, N_GATE // WSLOTS) as i:
                for s in range(WSLOTS):
                    act.wait_ge(multiplied, i * WSLOTS + s + 1 + N_Z + N_XBC + N_ATT)
                    act.activation(k.gate[:, bass.ds(i * WSLOTS + s, 1), :], ps[:, s:s + 1, 0:T],
                                   ACT.Sigmoid).then_inc(evacuated, 1)
            act.wait_ge(multiplied, N_TILES)
            act.activation(k.misc[:], ps[:, 0, 0:T], ACT.Copy).then_inc(evacuated, 1)
            act.wait_ge(evacuated, N_TILES)
            act.wait_ge(stored_cv, N_XBC)

        @block.gpsimd
        def _(pool):
            for s in range(WSLOTS):
                pool.memset(raw[:, s, 0:3], 0.0).then_inc(zeroed, 1)
            pool.wait_ge(c_loaded, 48)

            def tile(i, s, first):
                n = i * WSLOTS + s
                if not first:
                    pool.wait_ge(convolved, n - WSLOTS + 1)
                    pool.wait_ge(saved, n - WSLOTS + 1)
                pool.tensor_copy(blocks(raw[:, s])[:, :, 0:3].rearrange("p b j -> p b j"),
                                 old[:, bass.ds(n, 1)].rearrange("p a b j -> p (a b) j")).then_inc(filled, 1)
                pool.wait_ge(evacuated, n + N_Z + 1)
                pool.wait_ge(filled, n + 1)
                pool.tensor_copy(tail_p[:, bass.ds(n, 1), :], raw[:, s:s + 1, TP:TP + 3])
                pool.tensor_copy(tail_s[:, bass.ds(n, 1)].rearrange("p a b j -> p (a b) j"),
                                 blocks(raw[:, s])[:, :, 1:4]).then_inc(saved, 1)
            for s in range(WSLOTS):
                tile(0, s, True)
            with pool.Fori(1, N_XBC // WSLOTS) as i:
                for s in range(WSLOTS):
                    tile(i, s, False)
            pool.wait_ge(saved, N_XBC)

        @block.vector
        def _(dve):
            dve.wait_ge(c_loaded, 48)
            dve.wait_ge(zeroed, WSLOTS)

            def tile(i, s, first):
                n = i * WSLOTS + s
                dve.wait_ge(evacuated, n + N_Z + 1)
                dve.wait_ge(filled, n + 1)
                if not first:
                    dve.wait_ge(stored_cv, n - WSLOTS + 1)
                dve.tensor_scalar(cv[:, s, :], raw[:, s, 0:CV], cw[:, bass.ds(n, 1), 0].rearrange("p a -> p a"),
                                  cb[:, bass.ds(n, 1)], ALU.mult, ALU.add).then_inc(tap, 1)
                for j in range(1, CW):
                    dve.wait_ge(tap, n * (CW - 1) + j)
                    dve.scalar_tensor_tensor(out=cv[:, s, :], in0=raw[:, s, j:j + CV],
                                             scalar=cw[:, bass.ds(n, 1), j].rearrange("p a -> p a"), in1=cv[:, s, :],
                                             op0=ALU.mult, op1=ALU.add
                                             ).then_inc(tap if j < CW - 1 else convolved, 1)
            for s in range(WSLOTS):
                tile(0, s, True)
            with dve.Fori(1, N_XBC // WSLOTS) as i:
                for s in range(WSLOTS):
                    tile(i, s, False)


def prepare_attention(nc, k):
    with ExitStack() as ctx:
        sem = signals(nc, ctx)
        sq, rms, gqk, table, rel = tensors(nc, ctx, pa_sq=(P, 10, T), pa_rms=(P, 10, T), pa_g=(P, 2),
                                           pa_table=(HEADS, BIAS_N), pa_rel=(NB, HEADS))
        hot, = tensors(nc, ctx, pa_hot=(NB, BIAS_N))
        ps = ctx.enter_context(nc.psum_tensor("pa_ps", [P, 4, 512], F32))
        tr = ctx.enter_context(nc.psum_tensor("pa_tr", [P, 3, 512], F32))
        pt = ctx.enter_context(nc.psum_tensor("pa_pt", [P, 512], F32))
        (c_loaded, squared, summed, rooted, inverted, normed, turned, copied, tabled, table_out, spread,
         stored, doubled, copied_table) = (sem("pa_" + n) for n in (
             "c", "sq", "sum", "root", "inv", "normed", "turned", "copied", "tab", "tabout", "spread",
             "stored", "dup", "tabcp"))
        block = ctx.enter_context(nc.Block())
        NQ, NK = 8, 2

        @block.sync
        def _(sp):
            sp.dma_start(gqk[:], k.d_gqk[:]).then_inc(c_loaded, 16)
            sp.dma_start(rel[:], k.d_rel[:]).then_inc(c_loaded, 16)
            sp.dma_start(hot[:], k.d_hot[:]).then_inc(c_loaded, 16)
            sp.dma_start(k.ikd[0:HD, :], k.misc[0:HD, :]).then_inc(doubled, 16)
            sp.dma_start(k.ikd[HD:P, :], k.misc[0:HD, :]).then_inc(doubled, 16)
            sp.dma_start(k.o_ik[:], k.misc[0:HD, :]).then_inc(stored, 16)
            sp.dma_start(k.o_v[:], k.att[:, V0:V0 + 2, :]).then_inc(stored, 16)
            sp.wait_ge(copied_table, 1)
            sp.dma_start(k.s_table[:], table[:]).then_inc(table_out, 16)
            sp.wait_ge(table_out, 16)
            hankel = bass.AP(tensor=k.s_table.tensor, offset=0, ap=[[1, P], [BIAS_N, HEADS], [1, TP]])
            sp.dma_start(k.hankel[:], hankel).then_inc(spread, 16)
            sp.wait_ge(normed, NQ + NK)
            sp.dma_start(k.o_k[:], k.att[:, K0:K0 + 2, :]).then_inc(stored, 16)
            sp.wait_ge(spread, 16)
            sp.wait_ge(doubled, 32)
            sp.wait_ge(stored, 48)

        @block.scalar
        def _(act):
            act.activation(sq[:], k.att[:, 0:NQ + NK, :], ACT.Square).then_inc(squared, 1)
            for n in range(NQ + NK):
                act.wait_ge(summed, n + 1)
                if n < NQ:
                    act.activation(rms[:, n, :], ps[:, n % 4, 0:T], ACT.Sqrt, bias=k.eps64).then_inc(rooted, 1)
                else:
                    act.activation(rms[:, n, :], ps[:, n % 4, 0:T], ACT.Sqrt, scale=1.0 / HD,
                                   bias=k.eps).then_inc(rooted, 1)

        @block.tensor
        def _(pe):
            pe.wait_ge(c_loaded, 48)
            pe.matmul(pt[0:HEADS, 0:BIAS_N], rel[:], hot[:], start=True, stop=True).then_inc(tabled, 1)
            for c, at in enumerate((0, P, TP)):
                n = P if at < TP else TS
                for i, src in enumerate((k.att[:, V0, at:at + n], k.att[:, V0 + 1, at:at + n],
                                         k.misc[:, at:at + n])):
                    mm = pe.transpose(tr[0:n, c, i * P:(i + 1) * P], src, k.ident)
                mm.then_inc(turned, 1)
            pe.wait_ge(squared, 1)
            for n in range(NQ + NK):
                if n >= 4:
                    pe.wait_ge(rooted, n - 3)
                pe.matmul(ps[:, n % 4, 0:T], k.block, sq[:, n, :], start=True, stop=True).then_inc(summed, 1)

        @block.vector
        def _(dve):
            dve.wait_ge(tabled, 1)
            dve.tensor_copy(table[:], pt[0:HEADS, 0:BIAS_N]).then_inc(copied_table, 1)
            for c in range(2):
                dve.wait_ge(turned, c + 1)
                dve.tensor_copy(k.vnat[:, c, :], tr[:, c, 0:2 * P]).then_inc(copied, 1)
                dve.tensor_copy(k.mnat[:, c, :], tr[:, c, 2 * P:3 * P]).then_inc(copied, 1)
            dve.wait_ge(turned, 3)
            dve.tensor_copy(k.vnew[:], tr[0:TS, 2, 0:2 * P]).then_inc(copied, 1)
            dve.wait_ge(copied, 5)
            for n in range(NQ + NK):
                dve.wait_ge(rooted, n + 1)
                dve.reciprocal(rms[:, n, :], rms[:, n, :]).then_inc(inverted, 1)
                dve.wait_ge(inverted, n + 1)
                g = gqk[:, 0:1] if n < NQ else gqk[:, 1:2]
                dve.scalar_tensor_tensor(out=k.att[:, n, :], in0=k.att[:, n, :], scalar=g, in1=rms[:, n, :],
                                         op0=ALU.mult, op1=ALU.mult).then_inc(normed, 1)
            dve.wait_ge(normed, NQ + NK)


def choose_prompt(nc, k):
    with ExitStack() as ctx:
        sem = signals(nc, ctx)
        r, iw = tensors(nc, ctx, cp_r=(P, 4, TP), cp_iw=(P, 2, IH))
        score, = tensors(nc, ctx, cp_score=(P, 2, TP))
        top, = tensors(nc, ctx, cp_top=(P, 2, 8))
        ps = ctx.enter_context(nc.psum_tensor("cp_ps", [P, 4, 512], F32))
        weighed, multiplied, rectified, added, cut, found, replaced, masked, final = (sem("cp_" + n) for n in (
            "w", "mm", "relu", "add", "cut", "max", "rep", "mask", "final"))
        block = ctx.enter_context(nc.Block())
        steps = [(i, h) for i in range(2) for h in range(IH)]
        width = lambda i: P * (i + 1)

        @block.tensor
        def _(pe):
            for n, (i, h) in enumerate(steps):
                if n >= 4:
                    pe.wait_ge(rectified, n - 3)
                half = slice(h % 2 * HD, h % 2 * HD + HD)
                pe.matmul(ps[:, n % 4, 0:width(i)], k.att[half, IQ0 + h // 2, i * P:(i + 1) * P],
                          k.ikd[half, 0:width(i)], start=True, stop=True).then_inc(multiplied, 1)

        @block.scalar
        def _(act):
            for n, (i, h) in enumerate(steps):
                act.wait_ge(multiplied, n + 1)
                if n >= 4:
                    act.wait_ge(added, n - 3)
                act.activation(r[:, n % 4, 0:width(i)], ps[:, n % 4, 0:width(i)], ACT.Relu,
                               scale=HD ** -0.5).then_inc(rectified, 1)

        @block.vector
        def _(dve):
            dve.tensor_scalar(iw[:], k.mnat[:, :, IW_P:IW_P + IH], IH ** -0.5, None, ALU.mult).then_inc(weighed, 1)
            dve.wait_ge(weighed, 1)
            for n, (i, h) in enumerate(steps):
                dve.wait_ge(rectified, n + 1)
                s = score[:, i, 0:width(i)]
                if h == 0:
                    dve.tensor_scalar(s, r[:, n % 4, 0:width(i)], iw[:, i, h:h + 1], None, ALU.mult
                                      ).then_inc(added, 1)
                else:
                    dve.wait_ge(added, n)
                    dve.scalar_tensor_tensor(out=s, in0=r[:, n % 4, 0:width(i)], scalar=iw[:, i, h:h + 1], in1=s,
                                             op0=ALU.mult, op1=ALU.add).then_inc(added, 1)
            for step in range(SEL_P // 8):
                for i in range(2):
                    s = score[:, i, 0:width(i)]
                    n = 2 * step + i
                    if step == 0:
                        dve.wait_ge(cut, i + 1)
                    else:
                        dve.wait_ge(replaced, n - 1)
                    dve.max(top[:, i, :], s).then_inc(found, 1)
                    dve.wait_ge(found, n + 1)
                    dve.match_replace(s, top[:, i, :], s, LOW).then_inc(replaced, 1)
            for i in range(2):
                dve.wait_ge(replaced, SEL_P // 4 - 1 + i)
                dve.tensor_scalar(k.negp[:, i, 0:width(i)], score[:, i, 0:width(i)], LOW, NEG,
                                  ALU.not_equal, ALU.mult).then_inc(masked, 1)

        @block.gpsimd
        def _(pool):
            for i in range(2):
                pool.wait_ge(added, IH * (i + 1))
                s = score[:, i, i * P:(i + 1) * P]
                pool.affine_select(out=s, in_=s, compare_op=ALU.is_ge, fill=-1.0e38, base=0,
                                   pattern=[[-1, P]], channel_multiplier=1).then_inc(cut, 1)
            for i in range(2):
                pool.wait_ge(masked, i + 1)
                s = k.negp[:, i, i * P:(i + 1) * P]
                pool.affine_select(out=s, in_=s, compare_op=ALU.is_ge, fill=NEG, base=0,
                                   pattern=[[-1, P]], channel_multiplier=1).then_inc(final, 1)
            pool.wait_ge(final, 2)


def attend_prompt(nc, k):
    with ExitStack() as ctx:
        sem = signals(nc, ctx)
        lg, pr, prt, st = tensors(nc, ctx, ap_l=(P, 2, TP), ap_p=(P, 2, TP), ap_pt=(P, 2, TP), ap_st=(P, 2, 4))
        psl = ctx.enter_context(nc.psum_tensor("ap_psl", [P, 2, 512], F32))
        pst = ctx.enter_context(nc.psum_tensor("ap_pst", [P, 2, 512], F32))
        pso = ctx.enter_context(nc.psum_tensor("ap_pso", [P, 2, 512], F32))
        logits, maxed, negated, expd, inverted, normed, turned, copied, mixed, out = (sem("ap_" + n) for n in (
            "logit", "max", "neg", "exp", "inv", "norm", "turn", "copy", "mix", "out"))
        block = ctx.enter_context(nc.Block())
        steps = [(i, j, half, r) for i in range(2) for j in range(2) for half in range(2) for r in range(REP)]
        N = len(steps)
        width = lambda i: P * (i + 1)

        @block.tensor
        def _(pe):
            for m in range(N + 2):
                if m < N:
                    i, j, half, r = steps[m]
                    if m >= 2:
                        pe.wait_ge(maxed, m - 1)
                    rows = slice(half * HD, half * HD + HD)
                    o = psl[:, m % 2, 0:width(i)]
                    pe.matmul(o, k.att[rows, 4 * j + r, i * P:(i + 1) * P], k.att[rows, K0 + j, 0:width(i)],
                              start=True, stop=False)
                    pe.matmul(o, k.flip, k.hankel[:, 8 * j + 4 * half + r, TP - width(i):TP],
                              start=False, stop=True).then_inc(logits, 1)
                if 1 <= m <= N:
                    n = m - 1
                    i = steps[n][0]
                    pe.wait_ge(normed, n + 1)
                    if n >= 2:
                        pe.wait_ge(copied, n - 1)
                    for c in range(i + 1):
                        mm = pe.transpose(pst[:, n % 2, c * P:(c + 1) * P], pr[:, n % 2, c * P:(c + 1) * P], k.ident)
                    mm.then_inc(turned, 1)
                if m >= 2:
                    n = m - 2
                    i, j = steps[n][0:2]
                    pe.wait_ge(copied, n + 1)
                    if n >= 2:
                        pe.wait_ge(out, n - 1)
                    for c in range(i + 1):
                        mm = pe.matmul(pso[:, n % 2, 0:P], k.vnat[:, c, j * P:(j + 1) * P],
                                       prt[:, n % 2, c * P:(c + 1) * P], start=c == 0, stop=c == i)
                    mm.then_inc(mixed, 1)

        @block.vector
        def _(dve):
            for m in range(N + 1):
                if m < N:
                    i = steps[m][0]
                    w = width(i)
                    dve.wait_ge(logits, m + 1)
                    if m >= 2:
                        dve.wait_ge(expd, m - 1)
                    dve.tensor_tensor_reduce(lg[:, m % 2, 0:w], psl[:, m % 2, 0:w], k.negp[:, i, 0:w], 1.0, LOW,
                                             ALU.add, ALU.max, st[:, m % 2, 0:1]).then_inc(maxed, 1)
                    dve.wait_ge(maxed, m + 1)
                    dve.tensor_scalar(st[:, m % 2, 1:2], st[:, m % 2, 0:1], -1.0, None, ALU.mult
                                      ).then_inc(negated, 1)
                if m >= 1:
                    n = m - 1
                    w = width(steps[n][0])
                    dve.wait_ge(expd, n + 1)
                    dve.reciprocal(st[:, n % 2, 3:4], st[:, n % 2, 2:3]).then_inc(inverted, 1)
                    dve.wait_ge(inverted, n + 1)
                    dve.tensor_scalar(pr[:, n % 2, 0:w], pr[:, n % 2, 0:w], st[:, n % 2, 3:4], None, ALU.mult
                                      ).then_inc(normed, 1)

        @block.scalar
        def _(act):
            for m in range(N + 2):
                if m < N:
                    w = width(steps[m][0])
                    act.wait_ge(negated, m + 1)
                    if m >= 2:
                        act.wait_ge(turned, m - 1)
                    act.activation(pr[:, m % 2, 0:w], lg[:, m % 2, 0:w], ACT.Exp, bias=st[:, m % 2, 1:2],
                                   accum_out=st[:, m % 2, 2:3]).then_inc(expd, 1)
                if 1 <= m <= N:
                    n = m - 1
                    w = width(steps[n][0])
                    act.wait_ge(turned, n + 1)
                    if n >= 2:
                        act.wait_ge(mixed, n - 1)
                    act.activation(prt[:, n % 2, 0:w], pst[:, n % 2, 0:w], ACT.Copy).then_inc(copied, 1)
                if m >= 2:
                    n = m - 2
                    i, j, half, r = steps[n]
                    rows = slice(half * HD, half * HD + HD)
                    act.wait_ge(mixed, n + 1)
                    act.activation(k.yatt[rows, 4 * j + r, i * P:(i + 1) * P], pso[rows, n % 2, 0:P], ACT.Copy
                                   ).then_inc(out, 1)
            act.wait_ge(out, N)


def time_steps(nc, k):
    NP_, ALL = 2 * SSDH, 2 * SSDH + TS
    with ExitStack() as ctx:
        sem = signals(nc, ctx)
        bias, alog, x, a, e, u, l, seg, both = tensors(nc, ctx, **{"ts_" + n: (P, ALL) for n in "bias alog x a e u l".split()},
                                                       ts_seg=(P, NP_), ts_both=(P, 2 * TS))
        spread, = tensors(nc, ctx, ts_spread=(P, D_INNER))
        ps = ctx.enter_context(nc.psum_tensor("ts_ps", [P, 512], F32))
        px = ctx.enter_context(nc.psum_tensor("ts_px", [P, 512], F32))
        c_loaded, cleared, step_v, step_a, cumulated, widened, last = (sem("ts_" + n) for n in (
            "c", "clear", "v", "a", "cum", "wide", "last"))
        block = ctx.enter_context(nc.Block())
        rows = slice(DT_P, P)

        @block.sync
        def _(sp):
            sp.dma_start(bias[:], k.d_dtb[:]).then_inc(c_loaded, 16)
            sp.dma_start(alog[:], k.d_alog[:]).then_inc(c_loaded, 16)
            sp.dma_start(spread[:], k.d_spread[:]).then_inc(c_loaded, 16)
            sp.dma_start(k.dskip[:], k.d_dskip[:]).then_inc(c_loaded, 16)

        @block.vector
        def _(dve):
            dve.memset(x[:], 0.0).then_inc(cleared, 1)
            dve.wait_ge(cleared, 1)
            dve.wait_ge(c_loaded, 64)
            dve.tensor_tensor(x[:, 0:NP_].rearrange("p (c h) -> p c h", c=2), k.mnat[:, :, DT_P:P],
                              bias[:, 0:NP_].rearrange("p (c h) -> p c h", c=2), ALU.add)
            dve.tensor_tensor(x[rows, NP_:ALL], k.misc[rows, TP:T], bias[rows, NP_:ALL], ALU.add).then_inc(step_v, 1)
            dve.wait_ge(step_a, 2)
            dve.tensor_scalar(u[:], e[:], 1.0, None, ALU.add).then_inc(step_v, 1)
            dve.wait_ge(step_v, 2)
            dve.scalar_tensor_tensor(out=a[:], in0=u[:], scalar=-1.0, in1=e[:], op0=ALU.add, op1=ALU.subtract
                                     ).then_inc(step_v, 1)
            dve.wait_ge(step_v, 3)
            dve.reciprocal(e[:], u[:]).then_inc(step_v, 1)
            dve.wait_ge(step_v, 4)
            dve.tensor_tensor(e[:], a[:], e[:], ALU.mult).then_inc(step_v, 1)
            dve.wait_ge(step_a, 3)
            dve.wait_ge(step_v, 5)
            dve.tensor_tensor(l[:], l[:], e[:], ALU.subtract).then_inc(step_v, 1)
            dve.wait_ge(step_v, 6)
            dve.scalar_tensor_tensor(out=k.dt[:], in0=x[:], scalar=0.0, in1=l[:], op0=ALU.max, op1=ALU.add
                                     ).then_inc(step_v, 1)
            dve.wait_ge(step_a, 4)
            dve.wait_ge(step_v, 7)
            dve.scalar_tensor_tensor(out=k.dA[:], in0=k.dt[:], scalar=-1.0, in1=alog[:], op0=ALU.mult, op1=ALU.mult
                                     ).then_inc(step_v, 1)
            dve.tensor_copy(both[rows, 0:TS], k.dt[rows, NP_:ALL]).then_inc(step_v, 1)
            dve.wait_ge(cumulated, 1)
            dve.tensor_scalar(k.nac[:], ps[:, 0:NP_], -1.0, None, ALU.mult).then_inc(step_v, 1)
            dve.wait_ge(step_v, 10)
            dve.tensor_tensor(seg[:], k.nac[:], ps[:, NP_:2 * NP_], ALU.add).then_inc(step_v, 1)
            dve.wait_ge(step_a, 6)
            dve.tensor_tensor(k.dec[:], seg[:], k.dt[:, 0:NP_], ALU.mult).then_inc(last, 1)
            dve.wait_ge(widened, 1)
            dve.tensor_copy(k.ex[:], px[:, 0:KI * 2 * TS].rearrange("p (c n) -> p c n", c=KI)).then_inc(last, 1)
            dve.wait_ge(last, 2)

        @block.scalar
        def _(act):
            act.wait_ge(step_v, 1)
            act.activation(a[:], x[:], ACT.Abs).then_inc(step_a, 1)
            act.wait_ge(step_a, 1)
            act.activation(e[:], a[:], ACT.Exp, scale=-1.0).then_inc(step_a, 1)
            act.wait_ge(step_v, 2)
            act.activation(l[:], u[:], ACT.Ln).then_inc(step_a, 1)
            act.wait_ge(c_loaded, 64)
            act.activation(alog[:], alog[:], ACT.Exp).then_inc(step_a, 1)
            act.wait_ge(step_v, 9)
            act.activation(both[rows, TS:2 * TS], k.dA[rows, NP_:ALL], ACT.Exp).then_inc(step_a, 1)
            act.wait_ge(step_v, 11)
            act.activation(seg[:], seg[:], ACT.Exp).then_inc(step_a, 1)
            act.activation(k.etot[:], ps[:, NP_:2 * NP_], ACT.Exp).then_inc(step_a, 1)
            act.wait_ge(step_a, 7)

        @block.tensor
        def _(pe):
            pe.wait_ge(step_v, 8)
            pe.matmul(ps[:, 0:NP_], k.tri, k.dA[:, 0:NP_], start=True, stop=True)
            pe.matmul(ps[:, NP_:2 * NP_], k.ones, k.dA[:, 0:NP_], start=True, stop=True).then_inc(cumulated, 1)
            pe.wait_ge(step_v, 9)
            pe.wait_ge(step_a, 5)
            for c in range(KI):
                mm = pe.matmul(px[:, c * 2 * TS:(c + 1) * 2 * TS], spread[rows, c * P:(c + 1) * P], both[rows, :],
                               start=True, stop=True, tile_position=(DT_P, 0))
            mm.then_inc(widened, 1)


def ssd_chunk(nc, k, c):
    t0 = c * P
    with ExitStack() as ctx:
        sem = signals(nc, ctx, f"sc{c}_")
        xdt, xdec, bnat, cb, lm, em, mx, ea, ce = tensors(
            nc, ctx, **{f"sc{c}_{n}": s for n, s in dict(
                xdt=(P, D_INNER), xdec=(P, D_INNER), bnat=(P, GROUPS, P), cb=(P, GROUPS, P), lm=(P, 2, 4, P),
                em=(P, 2, 4, P), mx=(P, 2, 4, P), ea=(P, 2, 4, P), ce=(P, 2, 4, P)).items()})
        tr = ctx.enter_context(nc.psum_tensor(f"sc{c}_tr", [P, 2, 512], F32))
        pl = ctx.enter_context(nc.psum_tensor(f"sc{c}_pl", [P, 2, 4, P], F32))
        py = ctx.enter_context(nc.psum_tensor(f"sc{c}_py", [P, 2, 512], F32))
        ph = ctx.enter_context(nc.psum_tensor(f"sc{c}_ph", [P, 512], F32))
        (turned, drained_v, drained_a, crossed, crossed_out, cumulated, lm_ready, ea_ready, em_ready, mixed,
         carried, y_done, y_skip, y_out, h_done, h_scaled, h_out) = (sem(n) for n in (
             "turn", "drv", "dra", "cross", "crossout", "cum", "lm", "ea", "em", "mix", "ce", "y", "yskip", "yout", "h",
             "hsc", "hout"))
        block = ctx.enter_context(nc.Block())
        heads = lambda a, h0, n: a[:, c * SSDH + h0:c * SSDH + h0 + n]

        @block.tensor
        def _(pe):
            for n in range(6):
                if 2 <= n < 6:
                    pe.wait_ge(drained_v, n - 1) if n < 6 else None
                for i in range(4):
                    mm = pe.transpose(tr[:, n % 2, i * P:(i + 1) * P], k.xbc[:, 4 * n + i, t0:t0 + P], k.ident)
                mm.then_inc(turned, 1)
            for n in range(2):
                pe.wait_ge(drained_a, n + 1)
                for i in range(4):
                    g = 4 * n + i
                    mm = pe.matmul(tr[:, n, i * P:(i + 1) * P], k.xbc[:, KI + g, t0:t0 + P],
                                   k.xbc[:, KI + GROUPS + g, t0:t0 + P], start=True, stop=True)
                mm.then_inc(crossed, 1)

            def outputs(g):
                pe.wait_ge(mixed, g + 1)
                if c:
                    pe.wait_ge(carried, g + 1)
                if g >= 2:
                    pe.wait_ge(y_skip, g - 1)
                for r in range(4):
                    h = 4 * g + r
                    o = py[r % 2 * HD:r % 2 * HD + HD, g % 2, r // 2 * P:(r // 2 + 1) * P]
                    mm = pe.matmul(o, xdt[:, h * HD:(h + 1) * HD], mx[:, g % 2, r, :], start=True, stop=c == 0)
                    if c:
                        mm = pe.matmul(o, k.hT[:, h * HD:(h + 1) * HD], ce[:, g % 2, r, :], start=False, stop=True)
                mm.then_inc(y_done, 1)

            for g in range(GROUPS):
                if g >= 2:
                    pe.wait_ge(lm_ready, g - 1)
                    if c:
                        pe.wait_ge(ea_ready, g - 1)
                for r in range(4):
                    dah = heads(k.dA, 4 * g + r, 1).broadcast_to([P, P])
                    mm = pe.matmul(pl[:, g % 2, r, :], dah, k.tri, start=True, stop=True)
                mm.then_inc(cumulated, 1)
                if g:
                    outputs(g - 1)
                    pe.wait_ge(h_out, g)
                else:
                    pe.wait_ge(drained_v, 4)
                pe.matmul(ph[:, 0:4 * HD], bnat[:, g, :], xdec[:, g * 4 * HD:(g + 1) * 4 * HD],
                          start=True, stop=True).then_inc(h_done, 1)
            outputs(GROUPS - 1)

        @block.scalar
        def _(act):
            for n in range(2):
                act.wait_ge(turned, 5 + n)
                act.activation(bnat[:, 4 * n:4 * n + 4, :].rearrange("p g n -> p (g n)"), tr[:, n, :], ACT.Copy
                               ).then_inc(drained_a, 1)
            for n in range(2):
                act.wait_ge(crossed, n + 1)
                act.activation(cb[:, 4 * n:4 * n + 4, :].rearrange("p g n -> p (g n)"), tr[:, n, :], ACT.Copy
                               ).then_inc(crossed_out, 1)
            for g in range(GROUPS):
                act.wait_ge(lm_ready, g + 1)
                if c:
                    if g >= 2:
                        act.wait_ge(carried, g - 1)
                    act.activation(ea[:, g % 2], pl[:, g % 2], ACT.Exp).then_inc(ea_ready, 1)
                if g >= 2:
                    act.wait_ge(mixed, g - 1)
                for r in range(4):
                    e = act.activation(em[:, g % 2, r, :], lm[:, g % 2, r, :], ACT.Exp, bias=heads(k.nac, 4 * g + r, 1))
                e.then_inc(em_ready, 1)
                if c == 0:
                    act.wait_ge(h_done, g + 1)
                    act.activation(k.hT[:, g * 4 * HD:(g + 1) * 4 * HD], ph[:, 0:4 * HD], ACT.Copy).then_inc(h_out, 1)

        @block.vector
        def _(dve):
            for n in range(4):
                dve.wait_ge(turned, n + 1)
                for out, f in ((xdt, k.dt), (xdec, k.dec)):
                    o = dve.tensor_tensor(out[:, n * 512:(n + 1) * 512].rearrange("p (h d) -> p h d", d=HD),
                                          tr[:, n % 2, :].rearrange("p (h d) -> p h d", d=HD),
                                          heads(f, 8 * n, 8).unsqueeze(2).broadcast_to([P, 8, HD]), ALU.mult)
                o.then_inc(drained_v, 1)

            def finish(g):
                dve.wait_ge(y_done, g + 1)
                if g:
                    dve.wait_ge(y_out, g)
                for i in range(2):
                    o = dve.scalar_tensor_tensor(out=k.Y[:, 2 * g + i, t0:t0 + P], in0=k.xbc[:, 2 * g + i, t0:t0 + P],
                                                 scalar=k.dskip[:, 2 * g + i:2 * g + i + 1],
                                                 in1=py[:, g % 2, i * P:(i + 1) * P], op0=ALU.mult, op1=ALU.add)
                o.then_inc(y_skip, 1)
                if c:
                    hg = k.hT[:, g * 4 * HD:(g + 1) * 4 * HD]
                    dve.wait_ge(h_done, g + 1)
                    dve.tensor_tensor(hg.rearrange("p (h d) -> p h d", d=HD), hg.rearrange("p (h d) -> p h d", d=HD),
                                      heads(k.etot, 4 * g, 4).unsqueeze(2).broadcast_to([P, 4, HD]), ALU.mult
                                      ).then_inc(h_scaled, 1)
                    dve.wait_ge(h_scaled, g + 1)
                    dve.tensor_tensor(hg, hg, ph[:, 0:4 * HD], ALU.add).then_inc(h_out, 1)
                dve.wait_ge(y_skip, g + 1)
                yg = k.Y[:, 2 * g:2 * g + 2, t0:t0 + P]
                dve.tensor_tensor(yg, yg, k.zs[:, 2 * g:2 * g + 2, t0:t0 + P], ALU.mult).then_inc(y_out, 1)

            for g in range(GROUPS):
                dve.wait_ge(cumulated, g + 1)
                if g >= 2:
                    dve.wait_ge(em_ready, g - 1)
                dve.tensor_tensor(lm[:, g % 2], pl[:, g % 2], k.negt.unsqueeze(1).broadcast_to([P, 4, P]), ALU.add
                                  ).then_inc(lm_ready, 1)
                if g == 0:
                    dve.wait_ge(crossed_out, 2)
                if g:
                    finish(g - 1)
                if c:
                    dve.wait_ge(ea_ready, g + 1)
                    ct = k.xbc[:, KI + GROUPS + g, t0:t0 + P].unsqueeze(1).broadcast_to([P, 4, P])
                    dve.tensor_tensor(ce[:, g % 2], ea[:, g % 2], ct, ALU.mult).then_inc(carried, 1)
                dve.wait_ge(em_ready, g + 1)
                dve.tensor_tensor(mx[:, g % 2], em[:, g % 2], cb[:, g, :].unsqueeze(1).broadcast_to([P, 4, P]),
                                  ALU.mult).then_inc(mixed, 1)
            finish(GROUPS - 1)
            dve.wait_ge(y_out, GROUPS)

        stored = sem("store")
        if c:
            @block.sync
            def _(sp):
                sp.wait_ge(h_out, GROUPS)
                sp.dma_start(k.o_ssm_p[:], k.hT[:]).then_inc(stored, 16)
                sp.wait_ge(stored, 16)


def ssd_sample(nc, k):
    NSLOT = 3
    with ExitStack() as ctx:
        sem = signals(nc, ctx, "ss_")
        h, dtx, y, junk, skip = tensors(nc, ctx, ss_h=(P, NSLOT, KI, NST), ss_dtx=(P, KI, TS), ss_y=(P, KI, TS),
                                        ss_junk=(P, 4, NST), ss_skip=(P, KI, TS))
        pb = ctx.enter_context(nc.psum_tensor("ss_pb", [P, 2, GROUPS, NST], F32))
        pc = ctx.enter_context(nc.psum_tensor("ss_pc", [P, 2, GROUPS, NST], F32))
        loaded = [sem(f"ld{s}") for s in range(NSLOT)]
        stored = [sem(f"st{s}") for s in range(NSLOT)]
        scaled, broadcast, faded, updated, read, closing = (sem(n) for n in ("dtx", "bc", "fade", "upd", "read", "close"))
        block = ctx.enter_context(nc.Block())
        new = lambda t: t[:, :, SAMP0:CV:4]

        @block.sync
        def _(sp):
            for b in range(TS):
                s = b % NSLOT
                if b >= NSLOT:
                    sp.wait_ge(stored[s], 16 * (b // NSLOT))
                    sp.wait_ge(read, (b - NSLOT + 1) * KI)
                sp.dma_start(h[:, s], k.d_state[b]).then_inc(loaded[s], 16)
                if b >= 2:
                    sp.wait_ge(updated, KI * (b - 1))
                    sp.dma_start(k.o_ssm_s[b - 2], h[:, (b - 2) % NSLOT]).then_inc(stored[(b - 2) % NSLOT], 16)
            for b in range(TS - 2, TS):
                sp.wait_ge(updated, KI * (b + 1))
                sp.dma_start(k.o_ssm_s[b], h[:, b % NSLOT]).then_inc(stored[b % NSLOT], 16)
            for s in range(NSLOT):
                sp.wait_ge(stored[s], 16 * len(range(s, TS, NSLOT)))

        @block.tensor
        def _(pe):
            for b in range(TS):
                if b >= 2:
                    pe.wait_ge(read, (b - 1) * KI)
                for g in range(GROUPS):
                    for out, tile in ((pb, KI + g), (pc, KI + GROUPS + g)):
                        at = SAMP0 + 4 * b
                        mm = pe.matmul(out[:, b % 2, g, :], k.xbc[:, tile, at:at + 1].broadcast_to([P, P]), k.ident,
                                       start=True, stop=True)
                mm.then_inc(broadcast, 1)

        @block.scalar
        def _(act):
            for b in range(TS):
                s = b % NSLOT
                act.wait_ge(loaded[s], 16 * (b // NSLOT + 1))
                for c in range(KI):
                    act.activation(h[:, s, c, :], h[:, s, c, :], ACT.Copy, scale=k.ex[:, c, TS + b:TS + b + 1]
                                   ).then_inc(faded, 1)

        @block.vector
        def _(dve):
            dve.tensor_tensor(dtx[:], new(k.xbc[:, 0:KI]), k.ex[:, :, 0:TS], ALU.mult).then_inc(scaled, 1)
            dve.wait_ge(scaled, 1)
            for b in range(TS):
                s = b % NSLOT
                dve.wait_ge(broadcast, b + 1)
                for c in range(KI):
                    dve.wait_ge(faded, b * KI + c + 1)
                    dve.scalar_tensor_tensor(out=h[:, s, c, :], in0=pb[:, b % 2, c // 2, :],
                                             scalar=dtx[:, c, b:b + 1], in1=h[:, s, c, :],
                                             op0=ALU.mult, op1=ALU.add).then_inc(updated, 1)
                for c in range(KI):
                    dve.wait_ge(updated, b * KI + c + 1)
                    n = b * KI + c
                    if n >= 4:
                        dve.wait_ge(read, n - 3)
                    dve.tensor_tensor_reduce(junk[:, c % 4], h[:, s, c, :], pc[:, b % 2, c // 2, :], 1.0, 0.0,
                                             ALU.mult, ALU.add, y[:, c, b:b + 1]).then_inc(read, 1)
            dve.wait_ge(read, TS * KI)
            dve.tensor_tensor(skip[:], new(k.xbc[:, 0:KI]), k.dskip[:].unsqueeze(2).broadcast_to([P, KI, TS]),
                              ALU.mult).then_inc(closing, 1)
            dve.wait_ge(closing, 1)
            dve.tensor_tensor(skip[:], skip[:], y[:], ALU.add).then_inc(closing, 1)
            dve.wait_ge(closing, 2)
            dve.tensor_tensor(k.Y[:, :, TP:T], skip[:], k.zs[:, :, TP:T], ALU.mult).then_inc(closing, 1)
            dve.wait_ge(closing, 3)


def ssd_norm(nc, k):
    with ExitStack() as ctx:
        sem = signals(nc, ctx, "sn_")
        sq, rms, g = tensors(nc, ctx, sn_sq=(P, 2, 2, T), sn_rms=(P, 2, T), sn_g=(P, KI))
        ps = ctx.enter_context(nc.psum_tensor("sn_ps", [P, 2, 512], F32))
        loaded, squared, summed, rooted, inverted, done = (sem(n) for n in ("c", "sq", "sum", "root", "inv", "done"))
        block = ctx.enter_context(nc.Block())

        @block.sync
        def _(sp):
            sp.dma_start(g[:], k.d_gssd[:]).then_inc(loaded, 16)

        @block.scalar
        def _(act):
            for n in range(GROUPS + 1):
                if n < GROUPS:
                    if n >= 2:
                        act.wait_ge(summed, n - 1)
                    act.activation(sq[:, n % 2], k.Y[:, 2 * n:2 * n + 2, :], ACT.Square).then_inc(squared, 1)
                if n:
                    act.wait_ge(summed, n)
                    if n > 2:
                        act.wait_ge(done, n - 2)
                    act.activation(rms[:, (n - 1) % 2], ps[:, (n - 1) % 2, 0:T], ACT.Sqrt, scale=1.0 / (2 * P),
                                   bias=k.eps).then_inc(rooted, 1)

        @block.tensor
        def _(pe):
            for n in range(GROUPS):
                pe.wait_ge(squared, n + 1)
                if n >= 2:
                    pe.wait_ge(rooted, n - 1)
                for i in range(2):
                    mm = pe.matmul(ps[:, n % 2, 0:T], k.ones, sq[:, n % 2, i, :], start=i == 0, stop=i == 1)
                mm.then_inc(summed, 1)

        @block.vector
        def _(dve):
            dve.wait_ge(loaded, 16)
            for n in range(GROUPS):
                dve.wait_ge(rooted, n + 1)
                dve.reciprocal(rms[:, n % 2], rms[:, n % 2]).then_inc(inverted, 1)
                dve.wait_ge(inverted, n + 1)
                for c in (2 * n, 2 * n + 1):
                    o = dve.scalar_tensor_tensor(out=k.Y[:, c, :], in0=k.Y[:, c, :], scalar=g[:, c:c + 1],
                                                 in1=rms[:, n % 2], op0=ALU.mult, op1=ALU.mult)
                o.then_inc(done, 1)
            dve.wait_ge(done, GROUPS)


def choose_sample(nc, k):
    with ExitStack() as ctx:
        sem = signals(nc, ctx, "cs_")
        ik, ikt, iqd, r, score, wsel = tensors(
            nc, ctx, cs_ik=(P, TS * PAGES, HD), cs_ikt=(P, 2, 512), cs_iqd=(P, TS, TS * IH), cs_r=(TS * IH, NKS),
            cs_score=(TS, NKS), cs_wsel=(TS * IH, TS))
        top, = tensors(nc, ctx, cs_top=(TS, 8))
        tr = ctx.enter_context(nc.psum_tensor("cs_tr", [P, 2, 512], F32))
        small = ctx.enter_context(nc.psum_tensor("cs_small", [P, 512], F32))
        pw = ctx.enter_context(nc.psum_tensor("cs_pw", [P, 512], F32))
        ps = ctx.enter_context(nc.psum_tensor("cs_ps", [P, 3, 512], F32))
        (table, loaded, cleared, spread, diag, weighed, turned, copied, scored, rectified, summed, read, found,
         replaced, masked, wide) = (sem(n) for n in (
             "table", "ld", "clr", "spread", "diag", "w", "turn", "copy", "score", "relu", "sum", "read", "max", "rep",
             "mask", "wide"))
        block = ctx.enter_context(nc.Block())

        @block.sync
        def _(sp):
            sp.dma_start(k.pages[:], k.d_pages[:]).then_inc(table, 16)
            sp.wait_ge(table, 16)
            with sp.Fori(0, TS * PAGES) as i:
                page = sp.value_load(k.pages[0:1, bass.ds(i, 1)], min_val=0, max_val=k.n_pool - 1)
                sp.dma_start(ik[:, bass.ds(i, 1), :], k.d_cik[bass.ds(page, 1)].rearrange("a s d -> s a d")
                             ).then_inc(loaded, 16)
            sp.wait_ge(loaded, 16 * TS * PAGES)

        @block.tensor
        def _(pe):
            for h in range(IH):
                mm = pe.matmul(small[:, h * TS:(h + 1) * TS], k.selhi if h % 2 else k.sello,
                               k.att[:, IQ0 + h // 2, TP:T], start=True, stop=True)
            mm.then_inc(spread, 1)
            pe.matmul(pw[0:TS * IH, 0:TS], k.iwsel, k.misc[:, TP:T], start=True, stop=True).then_inc(wide, 1)
            pe.wait_ge(loaded, 16 * TS * PAGES)
            pe.wait_ge(diag, TS)

            def scores(b):
                pe.wait_ge(copied, b + 1)
                for half in range(2):
                    rows = slice(half * HD, half * HD + HD)
                    mm = pe.matmul(ps[0:TS * IH, half, :], iqd[rows, b, :], ikt[rows, b % 2, :],
                                   start=b == 0, stop=b == TS - 1)
                mm = pe.matmul(ps[0:TS * IH, 2, 0:1], iqd[0:HD, b, :], k.misc[0:HD, TP + b:TP + b + 1],
                               start=b == 0, stop=b == TS - 1)
                mm.then_inc(scored, 1)

            for b in range(TS + 1):
                if b < TS:
                    if b >= 2:
                        pe.wait_ge(copied, b - 1)
                    for j in range(PAGES // 2):
                        at = b * PAGES + 2 * j
                        mm = pe.transpose(tr[:, b % 2, j * P:(j + 1) * P],
                                          ik[:, at:at + 2, :].rearrange("p a d -> p (a d)"), k.ident)
                    mm.then_inc(turned, 1)
                if b:
                    scores(b - 1)
            pe.wait_ge(rectified, 1)
            pe.wait_ge(weighed, 2)
            for a, n in ((0, 512), (512, 512), (1024, 1)):
                mm = pe.matmul(ps[0:TS, a // 512, 0:n], wsel[:], r[:, a:a + n], start=True, stop=True)
            mm.then_inc(summed, 1)

        @block.scalar
        def _(act):
            for b in range(TS):
                act.wait_ge(turned, b + 1)
                if b >= 2:
                    act.wait_ge(scored, b - 1)
                act.activation(ikt[:, b % 2, :], tr[:, b % 2, :], ACT.Copy).then_inc(copied, 1)
            act.wait_ge(scored, TS)
            for half in range(2):
                act.activation(r[:, 0:PAST].rearrange("p (j a s) -> p j a s", a=2, s=PG)[:, :, half, :],
                               ps[0:TS * IH, half, :].rearrange("p (j s) -> p j s", s=PG), ACT.Relu, scale=HD ** -0.5)
            act.activation(r[:, PAST:NKS], ps[0:TS * IH, 2, 0:1], ACT.Relu, scale=HD ** -0.5).then_inc(rectified, 1)

        @block.vector
        def _(dve):
            dve.memset(iqd[:], 0.0).then_inc(cleared, 1)
            dve.wait_ge(cleared, 1)
            dve.wait_ge(spread, 1)
            for b in range(TS):
                dve.tensor_copy(iqd[:, b, b * IH:(b + 1) * IH],
                                small[:, 0:IH * TS].rearrange("p (h b) -> p h b", b=TS)[:, :, b]).then_inc(diag, 1)
            dve.wait_ge(wide, 1)
            dve.tensor_scalar(wsel[:], pw[0:TS * IH, 0:TS], IH ** -0.5, None, ALU.mult).then_inc(weighed, 1)
            dve.wait_ge(weighed, 1)
            dve.tensor_tensor(wsel[:], wsel[:], k.own_ih, ALU.mult).then_inc(weighed, 1)
            dve.wait_ge(summed, 1)
            for a, n in ((0, 512), (512, 512), (1024, 1)):
                o = dve.tensor_copy(score[:, a:a + n], ps[0:TS, a // 512, 0:n])
            o.then_inc(read, 1)
            dve.wait_ge(read, 1)
            for n in range(SEL_S // 8):
                if n:
                    dve.wait_ge(replaced, n)
                dve.max(top[:], score[:]).then_inc(found, 1)
                dve.wait_ge(found, n + 1)
                dve.match_replace(score[:], top[:], score[:], LOW).then_inc(replaced, 1)
            dve.wait_ge(replaced, SEL_S // 8)
            dve.tensor_scalar(k.negs[:], score[:], LOW, NEG, ALU.not_equal, ALU.mult).then_inc(masked, 1)
            dve.wait_ge(masked, 1)


def attend_sample(nc, k):
    NG = 4
    with ExitStack() as ctx:
        sem = signals(nc, ctx, "as_")
        kv, kt, qd, pr, prt = tensors(nc, ctx, as_kv=(P, NG, 8, KVH * HD), as_kt=(P, 2, 4 * P),
                                      as_qd=(P, TS, 2, P), as_p=(P, NKS), as_pt=(P, PAGES, P))
        pd, pdt, st, hot, rel = tensors(nc, ctx, as_pd=(P, TS), as_pdt=(TS, P), as_st=(P, 8), as_hot=(NB, NKS),
                                        as_rel=(NB, P))
        tr = ctx.enter_context(nc.psum_tensor("as_tr", [P, 2, 512], F32))
        pl = ctx.enter_context(nc.psum_tensor("as_pl", [P, 3, 512], F32))
        po = ctx.enter_context(nc.psum_tensor("as_po", [P, 512], F32))
        loaded = [sem(f"ld{s}") for s in range(NG)]
        (c_loaded, cleared, diag, turned, copied, logits, maxed, negated, expd, normed, newed, p_turned,
         p_copied, mixed, out) = (sem(n) for n in (
             "c", "clr", "diag", "turn", "copy", "logit", "max", "neg", "exp", "norm", "new", "pturn", "pcopy",
             "mix", "out"))
        block = ctx.enter_context(nc.Block())
        flat = qd[:].rearrange("p b j n -> p (b j n)")
        spans = ((0, 512), (512, 512), (PAST, 1))

        @block.sync
        def _(sp):
            sp.dma_start(hot[:], k.d_hots[:]).then_inc(c_loaded, 16)
            sp.dma_start(rel[:], k.d_relbh[:]).then_inc(c_loaded, 16)
            for visit in range(16):
                s = visit % NG
                if NG <= visit < 8 + NG:
                    sp.wait_ge(turned, 4 * (visit - NG + 1))
                if visit >= 8 + NG:
                    sp.wait_ge(mixed, visit - 8 - NG + 1)
                for i in range(8):
                    at = i * PAGES + visit if visit < 8 else (visit - 8) * PAGES + i
                    cache = k.d_ck if visit < 8 else k.d_cv
                    page = sp.value_load(k.pages[0:1, at:at + 1], min_val=0, max_val=k.n_pool - 1)
                    sp.dma_start(kv[:, s, i:i + 1, :], cache[bass.ds(page, 1)].rearrange("a s n -> s a n")
                                 ).then_inc(loaded[s], 16)

        @block.tensor
        def _(pe):
            pe.wait_ge(c_loaded, 32)
            pe.wait_ge(diag, 16)
            for n, (a, w) in enumerate(spans):
                pe.matmul(pl[:, n, 0:w], rel[:], hot[:, a:a + w], start=True, stop=False)

            def products(n):
                page, pair = n // 4, n % 4
                pe.wait_ge(copied, n + 1)
                for i in range(2):
                    for j in range(2):
                        mm = pe.matmul(pl[:, page // 4, page % 4 * P:(page % 4 + 1) * P], qd[:, 2 * pair + i, j, :],
                                       kt[:, n % 2, (2 * i + j) * P:(2 * i + j + 1) * P], start=False, stop=False)
                mm.then_inc(logits, 1)

            for n in range(4 * PAGES + 1):
                if n < 4 * PAGES:
                    page, pair = n // 4, n % 4
                    if pair == 0:
                        pe.wait_ge(loaded[page % NG], 16 * 8 * (page // NG + 1))
                    if n >= 2:
                        pe.wait_ge(copied, n - 1)
                    for i in range(2):
                        for j in range(2):
                            mm = pe.transpose(tr[:, n % 2, (2 * i + j) * P:(2 * i + j + 1) * P],
                                              kv[:, page % NG, 2 * pair + i, j * P:(j + 1) * P], k.ident)
                    mm.then_inc(turned, 1)
                if n:
                    products(n - 1)
            for b in range(TS):
                for j in range(2):
                    pe.matmul(pl[:, 2, 0:1], qd[:, b, j, :], k.att[:, K0 + j, TP + b:TP + b + 1], start=False, stop=False)
            for n, (a, w) in enumerate(spans):
                mm = pe.matmul(pl[:, n, 0:w], k.rep_h, k.negs[:, a:a + w], start=False, stop=True)
            mm.then_inc(logits, 1)
            pe.wait_ge(normed, 1)
            for n in range(2):
                for i in range(4):
                    mm = pe.transpose(tr[:, n, i * P:(i + 1) * P], pr[:, (4 * n + i) * P:(4 * n + i + 1) * P], k.ident)
                mm.then_inc(p_turned, 1)
            pe.wait_ge(newed, 1)
            pe.wait_ge(p_copied, 1)
            pe.transpose(tr[0:TS, 0, 0:P], pd[:], k.ident).then_inc(p_turned, 1)
            pe.wait_ge(p_copied, 4)
            for b in range(TS):
                visit = 8 + b
                pe.wait_ge(loaded[visit % NG], 16 * 8 * (visit // NG + 1))
                for j in range(2):
                    cols = slice(b * 2 * REP * 2 + j * 8, b * 2 * REP * 2 + j * 8 + 8)
                    for page in range(PAGES):
                        pe.matmul(po[:, cols], kv[:, visit % NG, page, j * P:(j + 1) * P], prt[:, page, cols],
                                  start=page == 0, stop=False)
                    mm = pe.matmul(po[:, cols], k.vnew[:, j * P:(j + 1) * P], pdt[:, cols], start=False, stop=True)
                mm.then_inc(mixed, 1)

        @block.scalar
        def _(act):
            for n in range(4 * PAGES):
                act.wait_ge(turned, n + 1)
                if n >= 2:
                    act.wait_ge(logits, n - 1)
                act.activation(kt[:, n % 2, :], tr[:, n % 2, :], ACT.Copy).then_inc(copied, 1)
            act.wait_ge(negated, 1)
            act.activation(pr[:, 0:PAST].rearrange("p (a n) -> p a n", n=512), pl[:, 0:2, :], ACT.Exp,
                           bias=st[:, 3:4], accum_out=st[:, 4:5])
            act.activation(pr[:, PAST:NKS], pl[:, 2, 0:1], ACT.Exp, bias=st[:, 3:4], accum_out=st[:, 5:6]
                           ).then_inc(expd, 1)
            for n in range(2):
                act.wait_ge(p_turned, n + 1)
                act.activation(prt[:, 4 * n:4 * n + 4, :], tr[:, n, :].rearrange("p (a n) -> p a n", n=P), ACT.Copy
                               ).then_inc(p_copied, 1)
            act.wait_ge(p_turned, 3)
            act.activation(pdt[:], tr[0:TS, 0, 0:P], ACT.Copy).then_inc(p_copied, 2)

        @block.vector
        def _(dve):
            dve.memset(qd[:], 0.0).then_inc(cleared, 1)
            dve.wait_ge(cleared, 1)
            for j in range(2):
                for half in range(2):
                    for r in range(REP):
                        rows = slice(half * HD, half * HD + HD)
                        at = j * P + 8 * j + 4 * half + r
                        dve.tensor_copy(flat[rows, at:at + (TS - 1) * (2 * P + HEADS) + 1:2 * P + HEADS],
                                        k.att[rows, 4 * j + r, TP:T]).then_inc(diag, 1)
            dve.wait_ge(logits, 4 * PAGES + 1)
            dve.tensor_reduce(st[:, 0:1], pl[:, 0:2, :], AX.XY, ALU.max)
            dve.tensor_copy(st[:, 1:2], pl[:, 2, 0:1]).then_inc(maxed, 1)
            dve.wait_ge(maxed, 1)
            dve.tensor_tensor(st[:, 2:3], st[:, 0:1], st[:, 1:2], ALU.max).then_inc(maxed, 1)
            dve.wait_ge(maxed, 2)
            dve.tensor_scalar(st[:, 3:4], st[:, 2:3], -1.0, None, ALU.mult).then_inc(negated, 1)
            dve.wait_ge(expd, 1)
            dve.tensor_tensor(st[:, 6:7], st[:, 4:5], st[:, 5:6], ALU.add).then_inc(maxed, 1)
            dve.wait_ge(maxed, 3)
            dve.reciprocal(st[:, 7:8], st[:, 6:7]).then_inc(maxed, 1)
            dve.wait_ge(maxed, 4)
            dve.tensor_scalar(pr[:], pr[:], st[:, 7:8], None, ALU.mult).then_inc(normed, 1)
            dve.wait_ge(normed, 1)
            dve.tensor_scalar(pd[:], k.own_h, pr[:, PAST:NKS], None, ALU.mult).then_inc(newed, 1)
            dve.wait_ge(mixed, TS)
            o4 = po[:, 0:P].rearrange("p (b j n) -> p b j n", j=2, n=8)
            for j in range(2):
                for half in range(2):
                    rows = slice(half * HD, half * HD + HD)
                    dve.tensor_copy(k.yatt[rows, 4 * j:4 * j + 4, TP:T],
                                    o4[rows, :, j, 4 * half:4 * half + 4].rearrange("p b r -> p r b")).then_inc(out, 1)
            dve.wait_ge(out, 4)


def merge(nc, k):
    KB, SLOTS = KI + KD, 3
    with ExitStack() as ctx:
        sem = signals(nc, ctx, "mg_")
        w, wo, merged, part = tensors(nc, ctx, mg_w=(P, SLOTS, KB * P), mg_wo=(P, 4, KD * P), mg_m=(P, KD, T),
                                      mg_part=(P, 2, 2, T))
        pa = ctx.enter_context(nc.psum_tensor("mg_pa", [P, 2, 512], F32))
        pb = ctx.enter_context(nc.psum_tensor("mg_pb", [P, 2, 512], F32))
        po = ctx.enter_context(nc.psum_tensor("mg_po", [P, 2, 512], F32))
        w_loaded = [sem(f"w{s}") for s in range(SLOTS)]
        wo_loaded = [sem(f"wo{s}") for s in range(4)]
        multiplied, gated, summed, out_done, added = (sem(n) for n in ("mm", "gate", "sum", "out", "add"))
        block = ctx.enter_context(nc.Block())

        @block.sync
        def _(sp):
            for n in range(KD):
                if n >= SLOTS:
                    sp.wait_ge(multiplied, n - SLOTS + 1)
                sp.dma_start(w[:, n % SLOTS, :], k.d_w_ab[n]).then_inc(w_loaded[n % SLOTS], 16)
            for n in range(KD):
                if n >= 4:
                    sp.wait_ge(out_done, n - 3)
                sp.dma_start(wo[:, n % 4, :], k.d_w_out[n]).then_inc(wo_loaded[n % 4], 16)

        @block.tensor
        def _(pe):
            for n in range(KD):
                pe.wait_ge(w_loaded[n % SLOTS], 16 * (n // SLOTS + 1))
                if n >= 2:
                    pe.wait_ge(gated, 2 * (n - 1))
                for c in range(KB):
                    o = pa if c < KI else pb
                    rhs = k.Y[:, c, :] if c < KI else k.yatt[:, c - KI, :]
                    mm = pe.matmul(o[:, n % 2, 0:T], w[:, n % SLOTS, c * P:(c + 1) * P], rhs,
                                   start=c in (0, KI), stop=c in (KI - 1, KB - 1))
                mm.then_inc(multiplied, 1)
            pe.wait_ge(summed, KD)
            for n in range(KD):
                pe.wait_ge(wo_loaded[n % 4], 16 * (n // 4 + 1))
                if n >= 2:
                    pe.wait_ge(added, n - 1)
                for c in range(KD):
                    mm = pe.matmul(po[:, n % 2, 0:T], wo[:, n % 4, c * P:(c + 1) * P], merged[:, c, :],
                                   start=c == 0, stop=c == KD - 1)
                mm.then_inc(out_done, 1)

        @block.vector
        def _(dve):
            for n in range(KD):
                dve.wait_ge(multiplied, n + 1)
                if n >= 2:
                    dve.wait_ge(summed, n - 1)
                dve.tensor_tensor(part[:, n % 2, 0], pa[:, n % 2, 0:T], k.gate[:, n, :], ALU.mult).then_inc(gated, 1)
                dve.tensor_tensor(part[:, n % 2, 1], pb[:, n % 2, 0:T], k.gate[:, KD + n, :], ALU.mult
                                  ).then_inc(gated, 1)
                dve.wait_ge(gated, 2 * n + 2)
                dve.tensor_tensor(merged[:, n, :], part[:, n % 2, 0], part[:, n % 2, 1], ALU.add).then_inc(summed, 1)
            for n in range(KD):
                dve.wait_ge(out_done, n + 1)
                dve.tensor_tensor(k.xT[:, n, :], k.xT[:, n, :], po[:, n % 2, 0:T], ALU.add).then_inc(added, 1)
            dve.wait_ge(added, KD)


def peer_queries(nc, k):
    NT = 2 * PH
    with ExitStack() as ctx:
        sem = signals(nc, ctx, "pq_")
        sq, rms, g2, w = tensors(nc, ctx, pq_sq=(P, KD, T), pq_rms=(P, T), pq_g=(P, KD), pq_w=(P, WSLOTS, KD * P))
        ps = ctx.enter_context(nc.psum_tensor("pq_ps", [P, WSLOTS, 512], F32))
        pn = ctx.enter_context(nc.psum_tensor("pq_pn", [P, 512], F32))
        w_loaded = [sem(f"w{s}") for s in range(WSLOTS)]
        loaded, squared, summed, rooted, inverted, normed, multiplied, evacuated = (sem(n) for n in (
            "c", "sq", "sum", "root", "inv", "norm", "mm", "evac"))
        block = ctx.enter_context(nc.Block())

        @block.sync
        def _(sp):
            sp.dma_start(g2[:], k.d_g2[:]).then_inc(loaded, 16)
            sp.dma_start(k.keys[:], k.d_keys[:]).then_inc(loaded, 16)
            for n in range(NT):
                if n >= WSLOTS:
                    sp.wait_ge(multiplied, n - WSLOTS + 1)
                sp.dma_start(w[:, n % WSLOTS, :], k.d_wq[n]).then_inc(w_loaded[n % WSLOTS], 16)
            sp.wait_ge(loaded, 32)

        @block.scalar
        def _(act):
            act.activation(sq[:], k.xT[:], ACT.Square).then_inc(squared, 1)
            act.wait_ge(summed, 1)
            act.activation(rms[:], pn[:, 0:T], ACT.Sqrt, scale=1.0 / D_MODEL, bias=k.eps).then_inc(rooted, 1)
            for n in range(NT):
                act.wait_ge(multiplied, n + 1)
                act.activation(k.pq[:, n, :], ps[:, n % WSLOTS, 0:T], ACT.Copy).then_inc(evacuated, 1)
            act.wait_ge(evacuated, NT)

        @block.tensor
        def _(pe):
            pe.wait_ge(squared, 1)
            for c in range(KD):
                mm = pe.matmul(pn[:, 0:T], k.ones, sq[:, c, :], start=c == 0, stop=c == KD - 1)
            mm.then_inc(summed, 1)
            for n in range(NT):
                pe.wait_ge(w_loaded[n % WSLOTS], 16 * (n // WSLOTS + 1))
                if n >= WSLOTS:
                    pe.wait_ge(evacuated, n - WSLOTS + 1)
                if n == 0:
                    pe.wait_ge(normed, KD)
                for c in range(KD):
                    mm = pe.matmul(ps[:, n % WSLOTS, 0:T], w[:, n % WSLOTS, c * P:(c + 1) * P], k.hN[:, c, :],
                                   start=c == 0, stop=c == KD - 1)
                mm.then_inc(multiplied, 1)

        @block.vector
        def _(dve):
            dve.wait_ge(loaded, 32)
            dve.wait_ge(rooted, 1)
            dve.reciprocal(rms[:], rms[:]).then_inc(inverted, 1)
            dve.wait_ge(inverted, 1)
            for c in range(KD):
                dve.scalar_tensor_tensor(out=k.hN[:, c, :], in0=k.xT[:, c, :], scalar=g2[:, c:c + 1],
                                         in1=rms[:], op0=ALU.mult, op1=ALU.mult).then_inc(normed, 1)


def peer(nc, k):
    RING = 8
    PER = PH * TOPK
    SPER = PER * TS // P
    TILES = ((0, P), (P, P), (TP, TS))
    with ExitStack() as ctx:
        sem = signals(nc, ctx, "pe_")
        s, v, cand, eq, tv, fa, fb, e1, e2, idf, gsm = tensors(
            nc, ctx, pe_s=(P, 2 * PH, PK), pe_v=(P, 2 * PH, TOPK), pe_cand=(P, PH, TOPK * TOPK),
            pe_eq=(P, PER, TOPK), pe_tv=(P, PH, TOPK), pe_fa=(P, PER), pe_fb=(P, PER), pe_e1=(P, PER),
            pe_e2=(P, PER), pe_idf=(P, 2 * PH, TOPK), pe_gs=(P, PH))
        uv, hnat, a, gl, wt, dg, y = tensors(
            nc, ctx, pe_uv=(P, RING, 2 * D_MODEL), pe_hnat=(P, 3, D_MODEL), pe_a=(P, RING), pe_gl=(P, RING),
            pe_w=(P, RING), pe_dg=(P, RING, P), pe_y=(P, D_MODEL))
        gw, gws, hrep = tensors(nc, ctx, pe_gw=(P, 3, PER), pe_gws=(P, SPER), pe_hrep=(P, KD, P))
        ints = lambda n, *shape, dt=U32: ctx.enter_context(nc.sbuf_tensor(n, list(shape), dt))
        iv, tp, pa, idx, idxs = (ints("pe_iv", P, 2 * PH, TOPK), ints("pe_tp", P, PH, TOPK),
                                      ints("pe_pa", P, 2, PER), ints("pe_idx", P, 3, PER, dt=I32),
                                 ints("pe_idxs", P, SPER, dt=I32))
        ps = ctx.enter_context(nc.psum_tensor("pe_ps", [P, 4, 4, P], F32))
        ph = ctx.enter_context(nc.psum_tensor("pe_ph", [P, KD, P], F32))
        acc = ctx.enter_context(nc.psum_tensor("pe_acc", [P, KD, P], F32))
        repeated = sem("rep")
        gathered = [sem(f"ga{i}") for i in range(RING)]
        (scored, s_read, h_turned, h_read, step, chosen, to_dram, moved, exped, indexed, dotted, gelued, weighed,
         diagonal, accumulated, y_read, y_out) = (sem(n) for n in (
             "score", "sread", "hturn", "hread", "step", "chosen", "todram", "moved", "exp", "index", "dot", "gelu",
             "w", "diag", "acc", "yread", "yout"))
        block = ctx.enter_context(nc.Block())
        BEFORE = (0, PER, 2 * PER)
        LOOPS = (PER // RING, PER // RING, SPER // RING)
        TOTAL = 2 * PER + SPER

        @block.tensor
        def _(pe):
            for n, (t0, m) in enumerate(TILES):
                if n:
                    pe.wait_ge(s_read, 4 * n)
                for i in range(2 * PH):
                    mm = pe.matmul(ps[0:m, i // 4, i % 4, :], k.pq[:, i, t0:t0 + m], k.keys[:, i, :],
                                   start=True, stop=True)
                mm.then_inc(scored, 1)
                if n:
                    pe.wait_ge(h_read, n)
                if n == 2:
                    pe.wait_ge(repeated, KD)
                for c in range(KD):
                    if n < 2:
                        h = k.hN[:, c, t0:t0 + P]
                    else:
                        h = hrep[:, c, :]
                    mm = pe.matmul(ph[:, c, :], h, k.ident, start=True, stop=True)
                mm.then_inc(h_turned, 1)
            for n, (t0, m) in enumerate(TILES):
                if n:
                    pe.wait_ge(y_read, n)
                for c in range(KD):
                    pe.matmul(acc[0:m, c, :], k.xT[:, c, t0:t0 + m], k.ident, start=c % 4 == 0, stop=False,
                              skip_group_check=True)

                def steps(i):
                    for r in range(RING):
                        pe.wait_ge(diagonal, BEFORE[n] + i * RING + r + 1)
                        lhsT = dg[:, r, :] if n < 2 else dg[:, r, 0:TS]
                        for half in range(2):
                            mm = pe.matmul(acc[0:m, 4 * half:4 * half + 4, :], lhsT,
                                           uv[:, r, D_MODEL + half * 512:D_MODEL + (half + 1) * 512],
                                           start=False, stop=False, skip_group_check=True)
                        mm.then_inc(accumulated, 1)
                if LOOPS[n] > 1:
                    with pe.Fori(0, LOOPS[n]) as i:
                        steps(i)
                else:
                    steps(0)

        @block.scalar
        def _(act):
            for n, (t0, m) in enumerate(TILES):
                act.wait_ge(scored, n + 1)
                if n:
                    act.wait_ge(chosen, n)
                for i in range(4):
                    act.activation(s[0:m, 4 * i:4 * i + 4, :], ps[0:m, i], ACT.Copy).then_inc(s_read, 1)
                act.wait_ge(h_turned, n + 1)
                act.activation(hnat[:, n, :], ph[:].rearrange("p c d -> p (c d)"), ACT.Copy).then_inc(h_read, 1)
                act.wait_ge(indexed, n + 1)
                act.activation(gw[0:m, n, :], gw[0:m, n, :], ACT.Exp).then_inc(exped, 1)
            for n, (t0, m) in enumerate(TILES):
                if n == 2:
                    act.wait_ge(moved, 32)

                def steps(i):
                    for r in range(RING):
                        at = BEFORE[n] + i * RING + r
                        act.wait_ge(dotted, at + 1)
                        act.activation(gl[:, r:r + 1], a[:, r:r + 1], ACT.Gelu_apprx_tanh).then_inc(gelued, 1)
                        act.wait_ge(gelued, at + 1)
                        g = gw[:, n, bass.ds(i * RING + r, 1)] if n < 2 else gws[:, bass.ds(i * RING + r, 1)]
                        act.activation(wt[:, r:r + 1], gl[:, r:r + 1], ACT.Copy, scale=g).then_inc(weighed, 1)
                        act.wait_ge(weighed, at + 1)
                        if n < 2:
                            act.activation(dg[:, r, :], k.ident, ACT.Copy, scale=wt[:, r:r + 1]).then_inc(diagonal, 1)
                        else:
                            act.activation(dg[:, r, 0:TS], k.own_h, ACT.Copy, scale=wt[:, r:r + 1]
                                           ).then_inc(diagonal, 1)
                if LOOPS[n] > 1:
                    with act.Fori(0, LOOPS[n]) as i:
                        steps(i)
                else:
                    steps(0)
                act.wait_ge(accumulated, BEFORE[n] + LOOPS[n] * RING)
                if n:
                    act.wait_ge(y_out, 16 * n)
                act.activation(y[0:m, :], acc[0:m].rearrange("p c d -> p (c d)"), ACT.Copy).then_inc(y_read, 1)
                act.wait_ge(y_read, n + 1)
                act.dma_start(k.o_y[t0:t0 + m, :], y[0:m, :]).then_inc(y_out, 16)
            act.wait_ge(y_out, 48)

        @block.gpsimd
        def _(pool):
            for c in range(KD):
                pool.tensor_copy(hrep[:, c, :].rearrange("p (b i) -> p b i", b=TS),
                                 k.hN[:, c, TP:T].unsqueeze(2).broadcast_to([P, TS, P // TS])).then_inc(repeated, 1)
            for n in range(3):
                if n < 2:
                    pool.wait_ge(chosen, n + 1)
                else:
                    pool.wait_ge(moved, 32)

                for i in range(LOOPS[n] * RING):
                    at = BEFORE[n] + i
                    r = at % RING
                    if at >= RING:
                        pool.wait_ge(accumulated, at - RING + 1)
                    src = idx[:, n, i:i + 1] if n < 2 else idxs[:, i:i + 1]
                    pool.indirect_dma_start(uv[:, r, :], None, k.d_uv[:], bass.IndirectOffsetOnAxis(
                        ap=src, axis=0)).then_inc(gathered[r], 16)

        @block.sync
        def _(sp):
            sp.wait_ge(chosen, 3)
            sp.dma_start(k.s_idx[:], idx[0:TS, 2, :]).then_inc(to_dram, 16)
            sp.dma_start(k.s_gw[:], gw[0:TS, 2, :]).then_inc(to_dram, 16)
            sp.wait_ge(to_dram, 32)
            sp.dma_start(idxs[:], k.s_idx.rearrange("b (p n) -> (b p) n", n=SPER)).then_inc(moved, 16)
            sp.dma_start(gws[:], k.s_gw.rearrange("b (p n) -> (b p) n", n=SPER)).then_inc(moved, 16)

        @block.vector
        def _(dve):
            steps_done = 0
            for n, (t0, m) in enumerate(TILES):
                dve.wait_ge(s_read, 4 * (n + 1))

                def largest(lists, values, places):
                    count = len(lists)
                    for half in range(2):
                        c8 = slice(8 * half, 8 * half + 8)
                        for x, o in zip(lists, values):
                            dve.max(o[:, c8], x).then_inc(step, 1)
                        yield count
                        for x, o, p in zip(lists, values, places):
                            dve.max_index(p[:, c8], o[:, c8], x).then_inc(step, 1)
                        yield count
                        if half == 0:
                            for x, o in zip(lists, values):
                                dve.match_replace(x, o[:, c8], x, LOW).then_inc(step, 1)
                            yield count

                def run(stages):
                    nonlocal steps_done
                    for count in stages:
                        steps_done += count
                        dve.wait_ge(step, steps_done)

                def one(instruction):
                    nonlocal steps_done
                    instruction.then_inc(step, 1)
                    steps_done += 1
                    dve.wait_ge(step, steps_done)

                lists = [s[0:m, i, :] for i in range(2 * PH)]
                run(largest(lists, [v[0:m, i, :] for i in range(2 * PH)], [iv[0:m, i, :] for i in range(2 * PH)]))
                v4 = v[0:m].rearrange("p (h c) i -> p h c i", c=2)
                one(dve.tensor_tensor(cand[0:m].rearrange("p h (i j) -> p h i j", j=TOPK),
                                      v4[:, :, 0, :].unsqueeze(3).broadcast_to([m, PH, TOPK, TOPK]),
                                      v4[:, :, 1, :].unsqueeze(2).broadcast_to([m, PH, TOPK, TOPK]), ALU.add))
                run(largest([cand[0:m, h, :] for h in range(PH)], [tv[0:m, h, :] for h in range(PH)],
                            [tp[0:m, h, :] for h in range(PH)]))
                dve.tensor_tensor(gw[0:m, n, :].rearrange("p (h i) -> p h i", h=PH), tv[0:m],
                                  tv[0:m, :, 0:1].broadcast_to([m, PH, TOPK]), ALU.subtract).then_inc(indexed, 1)
                flat = tp[0:m].rearrange("p h i -> p (h i)")
                one(dve.tensor_single_scalar(pa[0:m, 0, :], flat, 4, ALU.logical_shift_right))
                one(dve.tensor_single_scalar(pa[0:m, 1, :], flat, TOPK - 1, ALU.bitwise_and))
                one(dve.tensor_copy(fa[0:m], pa[0:m, 0, :]))
                one(dve.tensor_copy(fb[0:m], pa[0:m, 1, :]))
                one(dve.tensor_copy(idf[0:m], iv[0:m]))
                i4 = idf[0:m].rearrange("p (h c) i -> p h c i", c=2)
                for c, (f, e) in enumerate(((fa, e1), (fb, e2))):
                    one(dve.tensor_tensor(eq[0:m], f[0:m].unsqueeze(2).broadcast_to([m, PER, TOPK]),
                                          k.iota[0:m].unsqueeze(1).broadcast_to([m, PER, TOPK]), ALU.is_equal))
                    e4 = eq[0:m].rearrange("p (h i) j -> p h i j", h=PH)
                    one(dve.tensor_tensor(e4, e4, i4[:, :, c, :].unsqueeze(2).broadcast_to([m, PH, TOPK, TOPK]),
                                          ALU.mult))
                    one(dve.tensor_reduce(e[0:m], eq[0:m], AX.X, ALU.add))
                one(dve.scalar_tensor_tensor(out=idx[0:m, n, :], in0=e1[0:m], scalar=float(PK), in1=e2[0:m],
                                             op0=ALU.mult, op1=ALU.add))
                dve.wait_ge(exped, n + 1)
                g3 = gw[0:m, n, :].rearrange("p (h i) -> p h i", h=PH)
                one(dve.tensor_reduce(gsm[0:m], g3, AX.X, ALU.add))
                one(dve.reciprocal(gsm[0:m], gsm[0:m]))
                dve.tensor_tensor(g3, g3, gsm[0:m].unsqueeze(2).broadcast_to([m, PH, TOPK]), ALU.mult
                                  ).then_inc(chosen, 1)
                dve.wait_ge(chosen, n + 1)

            dve.wait_ge(h_read, 3)
            for n in range(3):
                def steps(i, fresh):
                    for r in range(RING):
                        at = BEFORE[n] + i * RING + r
                        visit = BEFORE[n] // RING + i + 1
                        dve.wait_ge(gathered[r], visit * 16)
                        if not fresh:
                            dve.wait_ge(gelued, at - RING + 1)
                        dve.tensor_tensor_reduce(uv[:, r, 0:D_MODEL], uv[:, r, 0:D_MODEL], hnat[:, n, :], 1.0, 0.0,
                                                 ALU.mult, ALU.add, a[:, r:r + 1]).then_inc(dotted, 1)
                first = 0
                if n == 0:
                    steps(0, True)
                    first = 1
                if LOOPS[n] > 1:
                    with dve.Fori(first, LOOPS[n]) as i:
                        steps(i, False)
                else:
                    steps(0, False)


def build(nc, ins, outs):
    k = Kept()
    (k.d_alog, k.d_cb, k.d_cik, k.d_ck, k.d_cst, k.d_cv, k.d_cw, k.d_cx, k.d_dskip, k.d_dtb, k.d_g1, k.d_g2,
     k.d_gqk, k.d_gssd, k.d_hot, k.d_hots, k.d_keys, k.d_old, k.d_pages, k.d_rel, k.d_relbh, k.d_spread,
     k.d_state, k.d_uv, k.d_w_ab, k.d_w_in, k.d_w_out, k.d_wq, k.d_xT)\
        = (ins[n] for n in IN_NAMES)
    (k.o_conv_p, k.o_conv_s, k.o_k, k.o_v, k.o_ik, k.o_y, k.o_ssm_p, k.o_ssm_s)\
        = (outs[n] for n in OUTS)
    k.n_pool = k.d_ck.shape[0]
    k.s_idx = nc.dram_tensor("s_idx", [TS, PH * TOPK], I32, kind="Internal").ap()
    k.s_gw = nc.dram_tensor("s_gw", [TS, PH * TOPK], F32, kind="Internal").ap()
    k.s_table = nc.dram_tensor("s_table", [HEADS, BIAS_N], F32, kind="Internal").ap()
    with ExitStack() as ctx:
        k.xT, k.cst, k.cx = tensors(nc, ctx, xT=(P, KD, T), cst=(P, C_END), cx=(P, CX_N))
        k.ident, k.ones, k.flip, k.tri, k.block, k.negt, k.sello, k.selhi = (
            k.cst[:, a:a + P] for a in range(0, C_END, P))
        k.eps, k.eps64 = k.cx[:, 0:1], k.cx[:, 1:2]
        k.iota, k.own_ih, k.own_h = k.cx[:, 16:32], k.cx[0:TS * IH, 32:40], k.cx[:, 40:48]
        k.iwsel, k.rep_h = k.cx[:, 64:128], k.cx[0:TS, 128:256]
        with ExitStack() as first:
            k.gate, k.Y, k.yatt = tensors(nc, first, gate=(P, 2 * KD, T), Y=(P, KI, T), yatt=(P, KD, T))
            with ExitStack() as mixers:
                k.att, k.misc, k.ikd, k.vnat, k.mnat, k.vnew = tensors(
                    nc, mixers, att=(P, N_ATT, T), misc=(P, T), ikd=(P, T), vnat=(P, 2, 2 * P), mnat=(P, 2, P),
                    vnew=(TS, 2 * P))
                with ExitStack() as ssd:
                    k.zs, k.xbc = tensors(nc, ssd, zs=(P, KI, T), xbc=(P, KC, CV))
                    with ExitStack() as inner:
                        k.xn, = tensors(nc, inner, xn=(P, KD, T))
                        norm_in(nc, k)
                        project_in(nc, k)
                    with ExitStack() as inner:
                        k.hankel, k.negp = tensors(nc, inner, hankel=(P, HEADS, TP), negp=(P, 2, TP))
                        prepare_attention(nc, k)
                        choose_prompt(nc, k)
                        attend_prompt(nc, k)
                    k.dt, k.dA, k.nac, k.dec, k.etot, k.ex, k.dskip, k.hT = tensors(
                        nc, ssd, dt=(P, 72), dA=(P, 72), nac=(P, 64), dec=(P, 64), etot=(P, 64), ex=(P, KI, 2 * TS),
                        dskip=(P, KI), hT=(P, D_INNER))
                    time_steps(nc, k)
                    ssd_chunk(nc, k, 0)
                    ssd_chunk(nc, k, 1)
                    ssd_sample(nc, k)
                ssd_norm(nc, k)
                k.pages = mixers.enter_context(nc.sbuf_tensor("pages", [1, TS * PAGES], I32))
                k.negs, = tensors(nc, mixers, negs=(TS, NKS))
                choose_sample(nc, k)
                attend_sample(nc, k)
            merge(nc, k)
        k.hN, k.pq, k.keys = tensors(nc, ctx, hN=(P, KD, T), pq=(P, 2 * PH, T), keys=(P, 2 * PH, PK))
        peer_queries(nc, k)
        peer(nc, k)


OUTS = dict(o_conv_p=(P, KC, 3), o_conv_s=(P, KC, TS, 3), o_k=(P, 2, T), o_v=(P, 2, T), o_ik=(HD, T),
            o_y=(T, D_MODEL), o_ssm_p=(P, SSDH * HD), o_ssm_s=(TS, P, KI, NST))


def constants():
    c = np.zeros((P, C_END), np.float32)
    i = np.arange(P)
    c[:, C_ID:C_ID + P] = np.eye(P)
    c[:, C_ONES:C_ONES + P] = 1
    c[:, C_J:C_J + P] = np.eye(P)[::-1]
    c[:, C_TRI:C_TRI + P] = i[:, None] <= i[None]
    c[:, C_BLK:C_BLK + P] = i[:, None] // HD == i[None] // HD
    c[:, C_NEGT:C_NEGT + P] = np.where(i[:, None] <= i[None], 0, NEG)
    c[:, C_SELLO:C_SELLO + P] = i[:, None] == i[None] % HD
    c[:, C_SELHI:C_SELHI + P] = i[:, None] == HD + i[None] % HD
    x = np.zeros((P, CX_N), np.float32)
    x[:, 0], x[:, 1] = EPS, EPS * HD
    b = np.arange(TS)
    x[:, 16:32] = np.arange(TOPK)
    x[:, 32:40] = i[:, None] // IH == b
    x[:, 40:48] = i[:, None] // HEADS == b
    x[IW_P:IW_P + IH, 64:128] = np.arange(IH)[:, None] == np.arange(TS * IH)[None] % IH
    x[0:TS, 128:256] = b[:, None] == i[None] // HEADS
    return c, x


def bucket(dist):
    import math
    n = np.maximum(dist, 0)
    nf = np.maximum(n, 1).astype(np.float32)
    large = 16 + (np.log(nf / np.float32(16)) / np.float32(math.log(128 / 16)) * np.float32(16)).astype(np.int32)
    return np.where(n < 16, n, np.minimum(large, 31))


def kernel(x_prompt, x_sample, cache_k, cache_v, cache_idx_k, state_ssm, state_conv, page_table, rel_bias,
           norm1_g, w_in, conv_w, conv_b, dt_bias, a_log, d_skip, ssd_norm_g, q_norm_g, k_norm_g,
           w_branch_a, w_branch_b, w_out, norm2_g, peer_wq, peer_keys, peer_u, peer_v):
    import concourse.bacc as bacc
    from concourse.bass_utils import run_bass_kernel_spmd

    A = np.ascontiguousarray
    npa = np.asarray

    def chan(v):
        v = npa(v)
        v = v.reshape(*v.shape[:-1], v.shape[-1] // P, P)
        return A(np.moveaxis(v, (-1, -2), (0, 1)))

    def tiles(w):
        w = npa(w)
        return A(w.reshape(w.shape[0] // P, P, w.shape[1] // P, P).transpose(2, 1, 0, 3).reshape(
            w.shape[1] // P, P, w.shape[0]))

    def per_head(v):
        v = npa(v)[0]
        o = np.zeros((P, 2 * SSDH + TS), np.float32)
        o[:, :2 * SSDH] = np.tile(v, 2)[None]
        o[DT_P:, 2 * SSDH:] = v[:, None]
        return o

    spread = np.zeros((P, D_INNER), np.float32)
    spread[DT_P:] = np.arange(SSDH)[:, None] == np.arange(D_INNER)[None] // HD
    w = npa(w_in)[0]
    edges = np.cumsum((0, D_INNER, CONV_DIM, SSDH, HEADS * HD, KVH * HD, KVH * HD, IH * HD, HD, IH,
                       D_MODEL, D_MODEL))
    z, xbc, dt, q, kk, v, iq, ik, iw, ga, gb = (w[:, a:b] for a, b in zip(edges, edges[1:]))
    q = q.reshape(D_MODEL, 2, 2, REP, HD).transpose(0, 1, 3, 2, 4).reshape(D_MODEL, HEADS * HD)
    gap = np.zeros((D_MODEL, DT_P - IW_P - IH), np.float32)
    d_w_in = tiles(np.concatenate([z, xbc, q, kk, v, iq, ga, gb, ik, iw, gap, dt], axis=1))
    w_b = npa(w_branch_b)[0].reshape(2, 2, REP, HD, D_MODEL).transpose(0, 2, 1, 3, 4).reshape(HEADS * HD, D_MODEL)
    x = np.concatenate([npa(x_prompt)[0], npa(x_sample)[:, 0]], axis=0)
    d_cst, d_cx = constants()
    hot = (bucket(TP - 1 - np.arange(BIAS_N))[None] == np.arange(NB)[:, None]).astype(np.float32)
    arrays = dict(
        d_xT=chan(x), d_cst=d_cst, d_cx=d_cx, d_g1=chan(npa(norm1_g)[0]), d_w_in=d_w_in,
        d_cw=chan(npa(conv_w)[0]), d_cb=chan(npa(conv_b)[0]), d_old=chan(npa(state_conv)[0]),
        d_gqk=A(np.tile(np.stack([npa(q_norm_g)[0], npa(k_norm_g)[0]], axis=1), (2, 1))),
        d_rel=A(npa(rel_bias)), d_hot=hot,
        d_dtb=per_head(dt_bias), d_alog=per_head(a_log), d_spread=spread,
        d_dskip=chan(np.repeat(npa(d_skip)[0], HD)), d_gssd=chan(npa(ssd_norm_g)[0]),
        d_pages=A(npa(page_table).reshape(1, -1)), d_cik=A(npa(cache_idx_k)[0]),
        d_ck=A(npa(cache_k)[0].reshape(-1, PG, KVH * HD)), d_cv=A(npa(cache_v)[0].reshape(-1, PG, KVH * HD)),
        d_hots=(bucket(PAST - np.arange(NKS))[None] == np.arange(NB)[:, None]).astype(np.float32),
        d_relbh=A(np.tile(npa(rel_bias), (1, TS))),
        d_w_ab=tiles(np.concatenate([npa(w_branch_a)[0], w_b], axis=0)), d_w_out=tiles(npa(w_out)[0]),
        d_g2=chan(npa(norm2_g)[0]), d_wq=tiles(npa(peer_wq)[0]),
        d_keys=A(npa(peer_keys)[0].transpose(3, 1, 0, 2).reshape(PK, 2 * PH, PK)),
        d_uv=A(np.concatenate([npa(peer_u)[0], npa(peer_v)[0]], axis=1)),
        d_state=A(npa(state_ssm)[0].reshape(TS, KI, P, NST).transpose(0, 2, 1, 3)),
    )
    nc = bacc.Bacc("TRN2", target_bir_lowering=False, num_devices=1)
    ins = {n: nc.dram_tensor(n, list(a.shape), mybir.dt.from_np(a.dtype), kind="ExternalInput").ap()
           for n, a in arrays.items()}
    outs = {n: nc.dram_tensor(n, list(s), F32, kind="ExternalOutput").ap() for n, s in OUTS.items()}
    build(nc, ins, outs)
    r = run_bass_kernel_spmd(nc, [arrays], core_ids=[0]).results[0]

    def rows(o, n):
        return o.reshape(P, n, -1).transpose(2, 1, 0).reshape(-1, n * P)

    kn, vn, ikn = rows(r["o_k"], 2), rows(r["o_v"], 2), r["o_ik"].T
    heads = lambda a: A(a.reshape(-1, KVH, HD))
    conv_p = r["o_conv_p"].transpose(2, 1, 0).reshape(3, CONV_DIM)
    conv_s = r["o_conv_s"].transpose(2, 3, 1, 0).reshape(TS, 3, CONV_DIM)
    y = r["o_y"]
    ssm_p = r["o_ssm_p"].T.reshape(SSDH, HD, NST)
    ssm_s = r["o_ssm_s"].transpose(0, 2, 1, 3).reshape(TS, SSDH, HD, NST)
    return (A(y[None, :TP]), A(y[TP:, None]),
            heads(kn[:TP])[None, None], heads(vn[:TP])[None, None], A(ikn[:TP])[None, None],
            A(ssm_p)[None, None], A(conv_p)[None, None],
            A(heads(kn[TP:])[None, :, None]), A(heads(vn[TP:])[None, :, None]), A(ikn[TP:][None, :, None]),
            A(ssm_s)[None], A(conv_s)[None])
```

```python
from contextlib import ExitStack

import concourse.bass as bass
from concourse import mybir
import numpy as np

ALU = mybir.AluOpType
ACT = mybir.ActivationFunctionType
AX = mybir.AxisListType
F32 = mybir.dt.float32
I32 = mybir.dt.int32
U32 = mybir.dt.uint32

P = 128
D_MODEL, D_INNER, CONV_DIM = 1024, 2048, 4096
KD = D_MODEL // P
KI = D_INNER // P
KC = CONV_DIM // P
TP, TS = 256, 8
T = TP + TS
CW = 4
RAW = 3 + TP + 4 * TS
CV = RAW - 3
SAMP0 = 3 + TP
HEADS, KVH, REP, HD = 16, 4, 4, 64
IH = 8
SSDH, GROUPS, NST = 32, 8, 128
PAGES, PG = 8, 128
PAST = PAGES * PG
NKS = PAST + 1
SEL_P, SEL_S = 64, 256
NB = 32
PH, PK, TOPK = 8, 128, 16
NEXP = PK * PK
EPS = 1e-6
NEG = -1.0e30
LOW = -3.0e38

N_Z, N_XBC, N_ATT, N_GATE = KI, KC, 16, 16
N_TILES = N_Z + N_XBC + N_ATT + N_GATE + 1
Z0 = N_ATT + 1
XBC0 = Z0 + N_Z
GATE0 = XBC0 + N_XBC
Q0, K0, V0, IQ0 = 0, 8, 10, 12
IW_P, DT_P = 64, 96
WSLOTS, BANKS = 4, 2
IK_FIRST = 44

C_ID, C_ONES, C_J, C_TRI, C_BLK, C_NEGT, C_SELLO, C_SELHI, C_END = (P * i for i in range(9))
CX_N = 256
BIAS_N = 384


def tensors(nc, ctx, **shapes):
    return [ctx.enter_context(nc.sbuf_tensor(n, [s[0], *s[1:]], F32)) for n, s in shapes.items()]


class Kept:
    pass


IN_NAMES = ("d_alog", "d_cb", "d_cik", "d_ck", "d_cst", "d_cv", "d_cw", "d_cx", "d_dskip", "d_dtb", "d_g1",
            "d_g2", "d_gqk", "d_gssd", "d_hot", "d_hots", "d_keys", "d_old", "d_pages", "d_rel",
            "d_relbh", "d_spread", "d_state", "d_uv", "d_w_ab", "d_w_in", "d_w_out", "d_wq", "d_xT")


def signals(nc, ctx, prefix=""):
    made = []

    def close():
        nc.clear_and_free_semaphores(made)
        nc.all_engine_barrier()
    ctx.callback(close)

    def sem(name):
        made.append(nc.alloc_semaphore(prefix + name))
        return made[-1]
    return sem


def norm_in(nc, k):
    with ExitStack() as ctx:
        sem = signals(nc, ctx)
        xsq, g1, rms = tensors(nc, ctx, n1_xsq=(P, KD, T), n1_g=(P, KD), n1_rms=(P, T))
        ps = ctx.enter_context(nc.psum_tensor("n1_ps", [P, 512], F32))
        x_loaded, c_loaded, squared, summed, rooted, inverted, done = (sem(n) for n in (
            "n1_x", "n1_c", "n1_sq", "n1_sum", "n1_root", "n1_inv", "n1_done"))
        block = ctx.enter_context(nc.Block())

        @block.sync
        def _(sp):
            sp.dma_start(k.xT[:], k.d_xT[:]).then_inc(x_loaded, 16)
            sp.dma_start(k.cst[:], k.d_cst[:]).then_inc(c_loaded, 16)
            sp.dma_start(k.cx[:], k.d_cx[:]).then_inc(c_loaded, 16)
            sp.dma_start(g1[:], k.d_g1[:]).then_inc(c_loaded, 16)
            for n in range(WSLOTS):
                k.proj.load(sp, n)
            sp.wait_ge(c_loaded, 48)

        @block.scalar
        def _(act):
            act.wait_ge(x_loaded, 16)
            act.activation(xsq[:], k.xT[:], ACT.Square).then_inc(squared, 1)
            act.wait_ge(c_loaded, 48)
            act.wait_ge(summed, 1)
            act.activation(rms[:], ps[:, 0:T], ACT.Sqrt, scale=1.0 / D_MODEL, bias=k.eps).then_inc(rooted, 1)

        @block.tensor
        def _(pe):
            pe.wait_ge(c_loaded, 48)
            pe.wait_ge(squared, 1)
            for c in range(KD):
                mm = pe.matmul(ps[:, 0:T], k.ones, xsq[:, c, :], start=c == 0, stop=c == KD - 1)
            mm.then_inc(summed, 1)

        @block.vector
        def _(dve):
            dve.wait_ge(rooted, 1)
            dve.reciprocal(rms[:], rms[:]).then_inc(inverted, 1)
            dve.wait_ge(inverted, 1)
            dve.wait_ge(c_loaded, 48)
            for c in range(KD):
                dve.scalar_tensor_tensor(out=k.xn[:, c, :], in0=k.xT[:, c, :], scalar=g1[:, c:c + 1],
                                         in1=rms[:], op0=ALU.mult, op1=ALU.mult).then_inc(done, 1)
            dve.wait_ge(done, KD)


class Projection:

    def __init__(self, nc, ctx, k):
        self.k = k
        (k.xn, self.w, self.raw, self.cv, self.cw, self.cb, self.old, self.tail_p, self.tail_s) = tensors(
            nc, ctx, xn=(P, KD, T), pi_w=(P, WSLOTS, KD * P), pi_raw=(P, WSLOTS, RAW), pi_cv=(P, WSLOTS, CV),
            pi_cw=(P, KC, CW), pi_cb=(P, KC), pi_old=(P, KC, TS, 3), pi_tail_p=(P, KC, 3),
            pi_tail_s=(P, KC, TS, 3))
        self.ps = ctx.enter_context(nc.psum_tensor("pi_ps", [P, BANKS, 512], F32))
        sem = signals(nc, ctx, "pi_")
        self.w_loaded = [sem(f"w{s}") for s in range(WSLOTS)]
        (self.c_loaded, self.zeroed, self.multiplied, self.evacuated, self.filled, self.saved, self.tap,
         self.convolved, self.rectified, self.stored) = (sem(n) for n in (
             "c", "zero", "mm", "evac", "fill", "saved", "tap", "conv", "silu", "store"))

    def blocks(self, s):
        return self.raw[:, s, SAMP0:SAMP0 + 4 * TS].rearrange("p (b j) -> p b j", j=4)

    def load(self, sp, n):
        if n < N_TILES:
            if n >= WSLOTS:
                sp.wait_ge(self.multiplied, n - WSLOTS + 1)
            sp.dma_start(self.w[:, n % WSLOTS, :], self.k.d_w_in[n]).then_inc(self.w_loaded[n % WSLOTS], 16)

    def multiply(self, pe, n):
        pe.wait_ge(self.w_loaded[n % WSLOTS], 16 * (n // WSLOTS + 1))
        if n >= BANKS:
            pe.wait_ge(self.evacuated, n - BANKS + 1)
        for c in range(KD):
            mm = pe.matmul(self.ps[:, n % BANKS, 0:T], self.w[:, n % WSLOTS, c * P:(c + 1) * P],
                           self.k.xn[:, c, :], start=c == 0, stop=c == KD - 1)
        mm.then_inc(self.multiplied, 1)

    def evacuate(self, act, n):
        k, ps = self.k, self.ps[:, n % BANKS, 0:T]
        act.wait_ge(self.multiplied, n + 1)
        if n < XBC0:
            act.activation(k.zs[:, n - Z0, :], ps, ACT.Silu).then_inc(self.evacuated, 1)
        elif n < GATE0:
            s = (n - XBC0) % WSLOTS
            if n - XBC0 >= WSLOTS:
                act.wait_ge(self.convolved, n - XBC0 - WSLOTS + 1)
                act.wait_ge(self.saved, n - XBC0 - WSLOTS + 1)
            act.activation(self.raw[:, s, 3:3 + TP], self.ps[:, n % BANKS, 0:TP], ACT.Copy)
            act.activation(self.blocks(s)[:, :, 3], self.ps[:, n % BANKS, TP:T], ACT.Copy
                           ).then_inc(self.evacuated, 1)
        else:
            act.activation(k.gate[:, n - GATE0, :], ps, ACT.Sigmoid).then_inc(self.evacuated, 1)
        i = n - WSLOTS - XBC0
        if 0 <= i < KC:
            act.wait_ge(self.convolved, i + 1)
            act.activation(k.xbc[:, i, :], self.cv[:, i % WSLOTS, :], ACT.Silu).then_inc(self.rectified, 1)

    def convolve(self, dve, n):
        i = n - 2 - XBC0
        if not 0 <= i < KC:
            return
        s, cv = i % WSLOTS, self.cv[:, i % WSLOTS, :]
        dve.wait_ge(self.evacuated, i + XBC0 + 1)
        dve.wait_ge(self.filled, i + 1)
        if i >= WSLOTS:
            dve.wait_ge(self.rectified, i - WSLOTS + 1)
        else:
            dve.wait_ge(self.c_loaded, 48)
            dve.wait_ge(self.zeroed, WSLOTS)
        dve.tensor_scalar(cv, self.raw[:, s, 0:CV], self.cw[:, i, 0:1], self.cb[:, i:i + 1], ALU.mult, ALU.add
                          ).then_inc(self.tap, 1)
        for j in range(1, CW):
            dve.wait_ge(self.tap, i * (CW - 1) + j)
            dve.scalar_tensor_tensor(out=cv, in0=self.raw[:, s, j:j + CV], scalar=self.cw[:, i, j:j + 1], in1=cv,
                                     op0=ALU.mult, op1=ALU.add
                                     ).then_inc(self.tap if j < CW - 1 else self.convolved, 1)

    def tails(self, pool, n):
        i = n - XBC0
        if not 0 <= i < KC:
            return
        s = i % WSLOTS
        if i >= WSLOTS:
            pool.wait_ge(self.convolved, i - WSLOTS + 1)
            pool.wait_ge(self.saved, i - WSLOTS + 1)
        else:
            pool.wait_ge(self.c_loaded, 48)
        pool.tensor_copy(self.blocks(s)[:, :, 0:3], self.old[:, i]).then_inc(self.filled, 1)
        pool.wait_ge(self.evacuated, n + 1)
        pool.wait_ge(self.filled, i + 1)
        pool.tensor_copy(self.tail_p[:, i, :], self.raw[:, s, TP:TP + 3])
        pool.tensor_copy(self.tail_s[:, i], self.blocks(s)[:, :, 1:4]).then_inc(self.saved, 1)


def shares(tiles, slots):
    return [[t for i, t in enumerate(tiles) if i * slots // len(tiles) == m] for m in range(slots)]


def load_indexer_pages(pool, k, first, end):
    ik = k.paged[:].rearrange("p (a d) -> p a d", d=HD)
    with pool.Fori(first, end) as i:
        page = pool.value_load(k.pages[0:1, bass.ds(i, 1)], min_val=0, max_val=k.n_pool - 1)
        pool.dma_start(ik[:, bass.ds(i, 1), :], k.d_cik[bass.ds(page, 1)].rearrange("a s d -> s a d")
                       ).then_inc(k.ik_loaded, 16)


def project_attention(nc, k):
    with ExitStack() as ctx:
        sem = signals(nc, ctx, "pr_")
        table, = (sem("table"),)
        block = ctx.enter_context(nc.Block())
        pj = k.proj

        @block.sync
        def _(sp):
            with sp.Fori(1, N_ATT // WSLOTS) as i:
                for s in range(WSLOTS):
                    sp.wait_ge(pj.multiplied, (i - 1) * WSLOTS + s + 1)
                    sp.dma_start(pj.w[:, s, :], k.d_w_in[bass.ds(i * WSLOTS + s, 1)].rearrange("a p n -> p (a n)")
                                 ).then_inc(pj.w_loaded[s], 16)
            for n in range(N_ATT, Z0 + WSLOTS):
                pj.load(sp, n)

        @block.tensor
        def _(pe):
            for n in range(WSLOTS):
                pj.multiply(pe, n)
            with pe.Fori(1, N_ATT // WSLOTS) as i:
                for s in range(WSLOTS):
                    pe.wait_ge(pj.w_loaded[s], (i + 1) * 16)
                    pe.wait_ge(pj.evacuated, i * WSLOTS + s - BANKS + 1)
                    for c in range(KD):
                        mm = pe.matmul(pj.ps[:, s % BANKS, 0:T], pj.w[:, s, c * P:(c + 1) * P], k.xn[:, c, :],
                                       start=c == 0, stop=c == KD - 1)
                    mm.then_inc(pj.multiplied, 1)
            pj.multiply(pe, N_ATT)

        @block.scalar
        def _(act):
            act.dma_start(pj.cw[:], k.d_cw[:]).then_inc(pj.c_loaded, 16)
            act.dma_start(pj.cb[:], k.d_cb[:]).then_inc(pj.c_loaded, 16)
            act.dma_start(pj.old[:], k.d_old[:]).then_inc(pj.c_loaded, 16)
            with act.Fori(0, N_ATT // WSLOTS) as i:
                for s in range(WSLOTS):
                    act.wait_ge(pj.multiplied, i * WSLOTS + s + 1)
                    act.activation(k.att[:, bass.ds(i * WSLOTS + s, 1), :], pj.ps[:, s % BANKS:s % BANKS + 1, 0:T],
                                   ACT.Copy).then_inc(pj.evacuated, 1)
            act.wait_ge(pj.multiplied, N_ATT + 1)
            act.activation(k.misc[:], pj.ps[:, N_ATT % BANKS, 0:T], ACT.Copy).then_inc(pj.evacuated, 1)
            act.wait_ge(pj.evacuated, N_ATT + 1)

        @block.gpsimd
        def _(pool):
            pool.dma_start(k.pages[:], k.d_pages[:]).then_inc(table, 16)
            for s in range(WSLOTS):
                pool.memset(pj.raw[:, s, 0:3], 0.0).then_inc(pj.zeroed, 1)
            pool.wait_ge(table, 16)
            load_indexer_pages(pool, k, 0, IK_FIRST)


def prepare_attention(nc, k, tiles):
    with ExitStack() as ctx:
        sem = signals(nc, ctx)
        sq, rms, gqk, table, rel = tensors(nc, ctx, pa_sq=(P, 2, T), pa_rms=(P, 2, T), pa_g=(P, 2),
                                           pa_table=(HEADS, BIAS_N), pa_rel=(NB, HEADS))
        hot, = tensors(nc, ctx, pa_hot=(NB, BIAS_N))
        ps = ctx.enter_context(nc.psum_tensor("pa_ps", [P, 2, 512], F32))
        tr = ctx.enter_context(nc.psum_tensor("pa_tr", [P, 3, 512], F32))
        pt = ctx.enter_context(nc.psum_tensor("pa_pt", [P, 512], F32))
        (c_loaded, squared, summed, rooted, inverted, normed, turned, copied, tabled, table_out, spread,
         stored, doubled, copied_table) = (sem("pa_" + n) for n in (
             "c", "sq", "sum", "root", "inv", "normed", "turned", "copied", "tab", "tabout", "spread",
             "stored", "dup", "tabcp"))
        block = ctx.enter_context(nc.Block())
        NQ, NK = 8, 2
        share = shares(tiles, NQ + NK)

        @block.sync
        def _(sp):
            sp.dma_start(gqk[:], k.d_gqk[:]).then_inc(c_loaded, 16)
            sp.dma_start(rel[:], k.d_rel[:]).then_inc(c_loaded, 16)
            sp.dma_start(hot[:], k.d_hot[:]).then_inc(c_loaded, 16)
            sp.dma_start(k.ikd[0:HD, :], k.misc[0:HD, :]).then_inc(doubled, 16)
            sp.dma_start(k.ikd[HD:P, :], k.misc[0:HD, :]).then_inc(doubled, 16)
            sp.dma_start(k.o_ik[:], k.misc[0:HD, :]).then_inc(stored, 16)
            sp.dma_start(k.o_v[:], k.att[:, V0:V0 + 2, :]).then_inc(stored, 16)
            sp.wait_ge(copied_table, 1)
            sp.dma_start(k.s_table[:], table[:]).then_inc(table_out, 16)
            sp.wait_ge(table_out, 16)
            hankel = bass.AP(tensor=k.s_table.tensor, offset=0, ap=[[1, P], [BIAS_N, HEADS], [1, TP]])
            sp.dma_start(k.hankel[:], hankel).then_inc(spread, 16)
            for n in tiles:
                k.proj.load(sp, n + WSLOTS)
            sp.wait_ge(normed, NQ + NK)
            sp.dma_start(k.o_k[:], k.att[:, K0:K0 + 2, :]).then_inc(stored, 16)
            sp.wait_ge(spread, 16)
            sp.wait_ge(doubled, 32)
            sp.wait_ge(stored, 48)

        @block.scalar
        def _(act):
            def square(n):
                if n >= 2:
                    act.wait_ge(summed, n - 1)
                act.activation(sq[:, n % 2], k.att[:, n, :], ACT.Square).then_inc(squared, 1)

            square(0)
            square(1)
            for n in range(NQ + NK):
                act.wait_ge(summed, n + 1)
                if n >= 2:
                    act.wait_ge(normed, n - 1)
                if n < NQ:
                    act.activation(rms[:, n % 2], ps[:, n % 2, 0:T], ACT.Sqrt, bias=k.eps64).then_inc(rooted, 1)
                else:
                    act.activation(rms[:, n % 2], ps[:, n % 2, 0:T], ACT.Sqrt, scale=1.0 / HD,
                                   bias=k.eps).then_inc(rooted, 1)
                if n + 2 < NQ + NK:
                    square(n + 2)
                for tile in share[n]:
                    k.proj.evacuate(act, tile)

        @block.tensor
        def _(pe):
            pe.wait_ge(c_loaded, 48)
            pe.matmul(pt[0:HEADS, 0:BIAS_N], rel[:], hot[:], start=True, stop=True).then_inc(tabled, 1)
            for c, at in enumerate((0, P, TP)):
                n = P if at < TP else TS
                for i, src in enumerate((k.att[:, V0, at:at + n], k.att[:, V0 + 1, at:at + n],
                                         k.misc[:, at:at + n])):
                    mm = pe.transpose(tr[0:n, c, i * P:(i + 1) * P], src, k.ident)
                mm.then_inc(turned, 1)
            for n in range(NQ + NK):
                pe.wait_ge(squared, n + 1)
                if n >= 2:
                    pe.wait_ge(rooted, n - 1)
                pe.matmul(ps[:, n % 2, 0:T], k.block, sq[:, n % 2], start=True, stop=True).then_inc(summed, 1)
                for tile in share[n]:
                    k.proj.multiply(pe, tile)

        @block.vector
        def _(dve):
            dve.wait_ge(tabled, 1)
            dve.tensor_copy(table[:], pt[0:HEADS, 0:BIAS_N]).then_inc(copied_table, 1)
            for c in range(2):
                dve.wait_ge(turned, c + 1)
                dve.tensor_copy(k.vnat[:, c, :], tr[:, c, 0:2 * P]).then_inc(copied, 1)
                dve.tensor_copy(k.mnat[:, c, :], tr[:, c, 2 * P:3 * P]).then_inc(copied, 1)
            dve.wait_ge(turned, 3)
            dve.tensor_copy(k.vnew[:], tr[0:TS, 2, 0:2 * P]).then_inc(copied, 1)
            dve.wait_ge(copied, 5)
            for n in range(NQ + NK):
                dve.wait_ge(rooted, n + 1)
                dve.reciprocal(rms[:, n % 2], rms[:, n % 2]).then_inc(inverted, 1)
                dve.wait_ge(inverted, n + 1)
                g = gqk[:, 0:1] if n < NQ else gqk[:, 1:2]
                dve.scalar_tensor_tensor(out=k.att[:, n, :], in0=k.att[:, n, :], scalar=g, in1=rms[:, n % 2],
                                         op0=ALU.mult, op1=ALU.mult).then_inc(normed, 1)
                for tile in share[n]:
                    k.proj.convolve(dve, tile)
            dve.wait_ge(normed, NQ + NK)

        @block.gpsimd
        def _(pool):
            load_indexer_pages(pool, k, IK_FIRST, TS * PAGES)
            for tile in tiles:
                k.proj.tails(pool, tile)


def choose_prompt(nc, k, tiles):
    with ExitStack() as ctx:
        sem = signals(nc, ctx)
        r, iw = tensors(nc, ctx, cp_r=(P, 4, TP), cp_iw=(P, 2, IH))
        score, = tensors(nc, ctx, cp_score=(P, 2, TP))
        top, = tensors(nc, ctx, cp_top=(P, 2, 8))
        ps = ctx.enter_context(nc.psum_tensor("cp_ps", [P, 4, 512], F32))
        weighed, multiplied, rectified, added, cut, found, replaced, masked, final = (sem("cp_" + n) for n in (
            "w", "mm", "relu", "add", "cut", "max", "rep", "mask", "final"))
        block = ctx.enter_context(nc.Block())
        steps = [(i, h) for i in range(2) for h in range(IH)]
        width = lambda i: P * (i + 1)
        share = shares(tiles, len(steps))

        @block.sync
        def _(sp):
            for n in tiles:
                k.proj.load(sp, n + WSLOTS)

        @block.tensor
        def _(pe):
            for n, (i, h) in enumerate(steps):
                if n >= 4:
                    pe.wait_ge(rectified, n - 3)
                half = slice(h % 2 * HD, h % 2 * HD + HD)
                pe.matmul(ps[:, n % 4, 0:width(i)], k.att[half, IQ0 + h // 2, i * P:(i + 1) * P],
                          k.ikd[half, 0:width(i)], start=True, stop=True).then_inc(multiplied, 1)
                for tile in share[n]:
                    k.proj.multiply(pe, tile)

        @block.scalar
        def _(act):
            for n, (i, h) in enumerate(steps):
                act.wait_ge(multiplied, n + 1)
                if n >= 4:
                    act.wait_ge(added, n - 3)
                act.activation(r[:, n % 4, 0:width(i)], ps[:, n % 4, 0:width(i)], ACT.Relu,
                               scale=HD ** -0.5).then_inc(rectified, 1)
                for tile in share[n]:
                    k.proj.evacuate(act, tile)

        @block.vector
        def _(dve):
            dve.tensor_scalar(iw[:], k.mnat[:, :, IW_P:IW_P + IH], IH ** -0.5, None, ALU.mult).then_inc(weighed, 1)
            dve.wait_ge(weighed, 1)
            for n, (i, h) in enumerate(steps):
                dve.wait_ge(rectified, n + 1)
                s = score[:, i, 0:width(i)]
                if h == 0:
                    dve.tensor_scalar(s, r[:, n % 4, 0:width(i)], iw[:, i, h:h + 1], None, ALU.mult
                                      ).then_inc(added, 1)
                else:
                    dve.wait_ge(added, n)
                    dve.scalar_tensor_tensor(out=s, in0=r[:, n % 4, 0:width(i)], scalar=iw[:, i, h:h + 1], in1=s,
                                             op0=ALU.mult, op1=ALU.add).then_inc(added, 1)
                for tile in share[n]:
                    k.proj.convolve(dve, tile)
            for step in range(SEL_P // 8):
                for i in range(2):
                    s = score[:, i, 0:width(i)]
                    n = 2 * step + i
                    if step == 0:
                        dve.wait_ge(cut, i + 1)
                    else:
                        dve.wait_ge(replaced, n - 1)
                    dve.max(top[:, i, :], s).then_inc(found, 1)
                    dve.wait_ge(found, n + 1)
                    dve.match_replace(s, top[:, i, :], s, LOW).then_inc(replaced, 1)
            for i in range(2):
                dve.wait_ge(replaced, SEL_P // 4 - 1 + i)
                dve.tensor_scalar(k.negp[:, i, 0:width(i)], score[:, i, 0:width(i)], LOW, NEG,
                                  ALU.not_equal, ALU.mult).then_inc(masked, 1)

        @block.gpsimd
        def _(pool):
            for tile in tiles:
                k.proj.tails(pool, tile)
            for i in range(2):
                pool.wait_ge(added, IH * (i + 1))
                s = score[:, i, i * P:(i + 1) * P]
                pool.affine_select(out=s, in_=s, compare_op=ALU.is_ge, fill=-1.0e38, base=0,
                                   pattern=[[-1, P]], channel_multiplier=1).then_inc(cut, 1)
            for i in range(2):
                pool.wait_ge(masked, i + 1)
                s = k.negp[:, i, i * P:(i + 1) * P]
                pool.affine_select(out=s, in_=s, compare_op=ALU.is_ge, fill=NEG, base=0,
                                   pattern=[[-1, P]], channel_multiplier=1).then_inc(final, 1)
            pool.wait_ge(final, 2)


def attend_prompt(nc, k, tiles):
    NL, NPR, LAG_T, LAG_O = 3, 4, 2, 3
    with ExitStack() as ctx:
        sem = signals(nc, ctx)
        lg, pr, prt, st = tensors(nc, ctx, ap_l=(P, NL, TP), ap_p=(P, NPR, TP), ap_pt=(P, 2, TP), ap_st=(P, NPR, 4))
        psl = ctx.enter_context(nc.psum_tensor("ap_psl", [P, 2, 512], F32))
        pst = ctx.enter_context(nc.psum_tensor("ap_pst", [P, 2, 512], F32))
        pso = ctx.enter_context(nc.psum_tensor("ap_pso", [P, 2, 512], F32))
        logits, maxed, negated, expd, inverted, normed, turned, copied, mixed, out = (sem("ap_" + n) for n in (
            "logit", "max", "neg", "exp", "inv", "norm", "turn", "copy", "mix", "out"))
        block = ctx.enter_context(nc.Block())
        steps = [(i, j, half, r) for i in range(2) for j in range(2) for half in range(2) for r in range(REP)]
        N = len(steps)
        share = shares(tiles, N) + [[]] * LAG_O
        width = lambda i: P * (i + 1)

        @block.sync
        def _(sp):
            for n in tiles:
                k.proj.load(sp, n + WSLOTS)

        @block.gpsimd
        def _(pool):
            for n in tiles:
                k.proj.tails(pool, n)

        @block.tensor
        def _(pe):
            for m in range(N + LAG_O):
                if m < N:
                    i, j, half, r = steps[m]
                    if m >= 2:
                        pe.wait_ge(maxed, m - 1)
                    rows = slice(half * HD, half * HD + HD)
                    o = psl[:, m % 2, 0:width(i)]
                    pe.matmul(o, k.att[rows, 4 * j + r, i * P:(i + 1) * P], k.att[rows, K0 + j, 0:width(i)],
                              start=True, stop=False)
                    pe.matmul(o, k.flip, k.hankel[:, 8 * j + 4 * half + r, TP - width(i):TP],
                              start=False, stop=True).then_inc(logits, 1)
                n = m - LAG_T
                if 0 <= n < N:
                    i = steps[n][0]
                    pe.wait_ge(normed, n + 1)
                    if n >= 2:
                        pe.wait_ge(copied, n - 1)
                    for c in range(i + 1):
                        mm = pe.transpose(pst[:, n % 2, c * P:(c + 1) * P], pr[:, n % NPR, c * P:(c + 1) * P], k.ident)
                    mm.then_inc(turned, 1)
                n = m - LAG_O
                if n >= 0:
                    i, j = steps[n][0:2]
                    pe.wait_ge(copied, n + 1)
                    if n >= 2:
                        pe.wait_ge(out, n - 1)
                    for c in range(i + 1):
                        mm = pe.matmul(pso[:, n % 2, 0:P], k.vnat[:, c, j * P:(j + 1) * P],
                                       prt[:, n % 2, c * P:(c + 1) * P], start=c == 0, stop=c == i)
                    mm.then_inc(mixed, 1)
                for tile in share[m]:
                    k.proj.multiply(pe, tile)

        @block.vector
        def _(dve):
            for m in range(N + 1):
                if m < N:
                    i = steps[m][0]
                    w = width(i)
                    dve.wait_ge(logits, m + 1)
                    if m >= NL:
                        dve.wait_ge(expd, m - NL + 1)
                    if m >= NPR:
                        dve.wait_ge(normed, m - NPR + 1)
                    s = st[:, m % NPR]
                    dve.tensor_tensor_reduce(lg[:, m % NL, 0:w], psl[:, m % 2, 0:w], k.negp[:, i, 0:w], 1.0, LOW,
                                             ALU.add, ALU.max, s[:, 0:1]).then_inc(maxed, 1)
                    dve.wait_ge(maxed, m + 1)
                    dve.tensor_scalar(s[:, 1:2], s[:, 0:1], -1.0, None, ALU.mult).then_inc(negated, 1)
                if m >= 1:
                    n = m - 1
                    w = width(steps[n][0])
                    s = st[:, n % NPR]
                    dve.wait_ge(expd, n + 1)
                    dve.reciprocal(s[:, 3:4], s[:, 2:3]).then_inc(inverted, 1)
                    dve.wait_ge(inverted, n + 1)
                    dve.tensor_scalar(pr[:, n % NPR, 0:w], pr[:, n % NPR, 0:w], s[:, 3:4], None, ALU.mult
                                      ).then_inc(normed, 1)
                for tile in share[m]:
                    k.proj.convolve(dve, tile)

        @block.scalar
        def _(act):
            for m in range(N + LAG_O):
                if m < N:
                    w = width(steps[m][0])
                    act.wait_ge(negated, m + 1)
                    if m >= NPR:
                        act.wait_ge(turned, m - NPR + 1)
                    act.activation(pr[:, m % NPR, 0:w], lg[:, m % NL, 0:w], ACT.Exp, bias=st[:, m % NPR, 1:2],
                                   accum_out=st[:, m % NPR, 2:3]).then_inc(expd, 1)
                n = m - LAG_T
                if 0 <= n < N:
                    w = width(steps[n][0])
                    act.wait_ge(turned, n + 1)
                    if n >= 2:
                        act.wait_ge(mixed, n - 1)
                    act.activation(prt[:, n % 2, 0:w], pst[:, n % 2, 0:w], ACT.Copy).then_inc(copied, 1)
                n = m - LAG_O
                if n >= 0:
                    i, j, half, r = steps[n]
                    rows = slice(half * HD, half * HD + HD)
                    act.wait_ge(mixed, n + 1)
                    act.activation(k.yatt[rows, 4 * j + r, i * P:(i + 1) * P], pso[rows, n % 2, 0:P], ACT.Copy
                                   ).then_inc(out, 1)
                for tile in share[m]:
                    k.proj.evacuate(act, tile)
            act.wait_ge(out, N)


def time_steps(nc, k):
    NP_, ALL = 2 * SSDH, 2 * SSDH + TS
    with ExitStack() as ctx:
        sem = signals(nc, ctx)
        bias, alog, x, a, e, u, l, seg, both = tensors(nc, ctx, **{"ts_" + n: (P, ALL) for n in "bias alog x a e u l".split()},
                                                       ts_seg=(P, NP_), ts_both=(P, 2 * TS))
        spread, = tensors(nc, ctx, ts_spread=(P, D_INNER))
        ps = ctx.enter_context(nc.psum_tensor("ts_ps", [P, 512], F32))
        px = ctx.enter_context(nc.psum_tensor("ts_px", [P, 512], F32))
        c_loaded, cleared, step_v, step_a, cumulated, widened, last = (sem("ts_" + n) for n in (
            "c", "clear", "v", "a", "cum", "wide", "last"))
        block = ctx.enter_context(nc.Block())
        rows = slice(DT_P, P)

        @block.sync
        def _(sp):
            sp.dma_start(bias[:], k.d_dtb[:]).then_inc(c_loaded, 16)
            sp.dma_start(alog[:], k.d_alog[:]).then_inc(c_loaded, 16)
            sp.dma_start(spread[:], k.d_spread[:]).then_inc(c_loaded, 16)
            sp.dma_start(k.dskip[:], k.d_dskip[:]).then_inc(c_loaded, 16)

        @block.vector
        def _(dve):
            dve.memset(x[:], 0.0).then_inc(cleared, 1)
            dve.wait_ge(cleared, 1)
            dve.wait_ge(c_loaded, 64)
            dve.tensor_tensor(x[:, 0:NP_].rearrange("p (c h) -> p c h", c=2), k.mnat[:, :, DT_P:P],
                              bias[:, 0:NP_].rearrange("p (c h) -> p c h", c=2), ALU.add)
            dve.tensor_tensor(x[rows, NP_:ALL], k.misc[rows, TP:T], bias[rows, NP_:ALL], ALU.add).then_inc(step_v, 1)
            dve.wait_ge(step_a, 2)
            dve.tensor_scalar(u[:], e[:], 1.0, None, ALU.add).then_inc(step_v, 1)
            dve.wait_ge(step_v, 2)
            dve.scalar_tensor_tensor(out=a[:], in0=u[:], scalar=-1.0, in1=e[:], op0=ALU.add, op1=ALU.subtract
                                     ).then_inc(step_v, 1)
            dve.wait_ge(step_v, 3)
            dve.reciprocal(e[:], u[:]).then_inc(step_v, 1)
            dve.wait_ge(step_v, 4)
            dve.tensor_tensor(e[:], a[:], e[:], ALU.mult).then_inc(step_v, 1)
            dve.wait_ge(step_a, 3)
            dve.wait_ge(step_v, 5)
            dve.tensor_tensor(l[:], l[:], e[:], ALU.subtract).then_inc(step_v, 1)
            dve.wait_ge(step_v, 6)
            dve.scalar_tensor_tensor(out=k.dt[:], in0=x[:], scalar=0.0, in1=l[:], op0=ALU.max, op1=ALU.add
                                     ).then_inc(step_v, 1)
            dve.wait_ge(step_a, 4)
            dve.wait_ge(step_v, 7)
            dve.scalar_tensor_tensor(out=k.dA[:], in0=k.dt[:], scalar=-1.0, in1=alog[:], op0=ALU.mult, op1=ALU.mult
                                     ).then_inc(step_v, 1)
            dve.tensor_copy(both[rows, 0:TS], k.dt[rows, NP_:ALL]).then_inc(step_v, 1)
            dve.wait_ge(cumulated, 1)
            dve.tensor_scalar(k.nac[:], ps[:, 0:NP_], -1.0, None, ALU.mult).then_inc(step_v, 1)
            dve.wait_ge(step_v, 10)
            dve.tensor_tensor(seg[:], k.nac[:], ps[:, NP_:2 * NP_], ALU.add).then_inc(step_v, 1)
            dve.wait_ge(step_a, 6)
            dve.tensor_tensor(k.dec[:], seg[:], k.dt[:, 0:NP_], ALU.mult).then_inc(last, 1)
            dve.wait_ge(widened, 1)
            dve.tensor_copy(k.ex[:], px[:, 0:KI * 2 * TS].rearrange("p (c n) -> p c n", c=KI)).then_inc(last, 1)
            dve.wait_ge(last, 2)

        @block.scalar
        def _(act):
            act.wait_ge(step_v, 1)
            act.activation(a[:], x[:], ACT.Abs).then_inc(step_a, 1)
            act.wait_ge(step_a, 1)
            act.activation(e[:], a[:], ACT.Exp, scale=-1.0).then_inc(step_a, 1)
            act.wait_ge(step_v, 2)
            act.activation(l[:], u[:], ACT.Ln).then_inc(step_a, 1)
            act.wait_ge(c_loaded, 64)
            act.activation(alog[:], alog[:], ACT.Exp).then_inc(step_a, 1)
            act.wait_ge(step_v, 9)
            act.activation(both[rows, TS:2 * TS], k.dA[rows, NP_:ALL], ACT.Exp).then_inc(step_a, 1)
            act.wait_ge(step_v, 11)
            act.activation(seg[:], seg[:], ACT.Exp).then_inc(step_a, 1)
            act.activation(k.etot[:], ps[:, NP_:2 * NP_], ACT.Exp).then_inc(step_a, 1)
            act.wait_ge(step_a, 7)

        @block.tensor
        def _(pe):
            pe.wait_ge(step_v, 8)
            pe.matmul(ps[:, 0:NP_], k.tri, k.dA[:, 0:NP_], start=True, stop=True)
            pe.matmul(ps[:, NP_:2 * NP_], k.ones, k.dA[:, 0:NP_], start=True, stop=True).then_inc(cumulated, 1)
            pe.wait_ge(step_v, 9)
            pe.wait_ge(step_a, 5)
            for c in range(KI):
                mm = pe.matmul(px[:, c * 2 * TS:(c + 1) * 2 * TS], spread[rows, c * P:(c + 1) * P], both[rows, :],
                               start=True, stop=True, tile_position=(DT_P, 0))
            mm.then_inc(widened, 1)


def ssd_chunk(nc, k, c):
    t0 = c * P
    with ExitStack() as ctx:
        sem = signals(nc, ctx, f"sc{c}_")
        xdt, xdec, bnat, cb, lm, em, mx, ea, ce = tensors(
            nc, ctx, **{f"sc{c}_{n}": s for n, s in dict(
                xdt=(P, D_INNER), xdec=(P, D_INNER), bnat=(P, GROUPS, P), cb=(P, GROUPS, P), lm=(P, 2, 4, P),
                em=(P, 2, 4, P), mx=(P, 2, 4, P), ea=(P, 2, 4, P), ce=(P, 2, 4, P)).items()})
        tr = ctx.enter_context(nc.psum_tensor(f"sc{c}_tr", [P, 2, 512], F32))
        pl = ctx.enter_context(nc.psum_tensor(f"sc{c}_pl", [P, 2, 4, P], F32))
        py = ctx.enter_context(nc.psum_tensor(f"sc{c}_py", [P, 2, 512], F32))
        ph = ctx.enter_context(nc.psum_tensor(f"sc{c}_ph", [P, 512], F32))
        (turned, drained_v, drained_a, crossed, crossed_out, cumulated, lm_ready, ea_ready, em_ready, mixed,
         carried, y_done, y_skip, y_out, h_done, h_scaled, h_out) = (sem(n) for n in (
             "turn", "drv", "dra", "cross", "crossout", "cum", "lm", "ea", "em", "mix", "ce", "y", "yskip", "yout", "h",
             "hsc", "hout"))
        block = ctx.enter_context(nc.Block())
        heads = lambda a, h0, n: a[:, c * SSDH + h0:c * SSDH + h0 + n]

        @block.tensor
        def _(pe):
            for n in range(6):
                if 2 <= n < 6:
                    pe.wait_ge(drained_v, n - 1) if n < 6 else None
                for i in range(4):
                    mm = pe.transpose(tr[:, n % 2, i * P:(i + 1) * P], k.xbc[:, 4 * n + i, t0:t0 + P], k.ident)
                mm.then_inc(turned, 1)
            for n in range(2):
                pe.wait_ge(drained_a, n + 1)
                for i in range(4):
                    g = 4 * n + i
                    mm = pe.matmul(tr[:, n, i * P:(i + 1) * P], k.xbc[:, KI + g, t0:t0 + P],
                                   k.xbc[:, KI + GROUPS + g, t0:t0 + P], start=True, stop=True)
                mm.then_inc(crossed, 1)

            def outputs(g):
                pe.wait_ge(mixed, g + 1)
                if c:
                    pe.wait_ge(carried, g + 1)
                if g >= 2:
                    pe.wait_ge(y_skip, g - 1)
                for r in range(4):
                    h = 4 * g + r
                    o = py[r % 2 * HD:r % 2 * HD + HD, g % 2, r // 2 * P:(r // 2 + 1) * P]
                    mm = pe.matmul(o, xdt[:, h * HD:(h + 1) * HD], mx[:, g % 2, r, :], start=True, stop=c == 0)
                    if c:
                        mm = pe.matmul(o, k.hT[:, h * HD:(h + 1) * HD], ce[:, g % 2, r, :], start=False, stop=True)
                mm.then_inc(y_done, 1)

            for g in range(GROUPS):
                if g >= 2:
                    pe.wait_ge(lm_ready, g - 1)
                    if c:
                        pe.wait_ge(ea_ready, g - 1)
                for r in range(4):
                    dah = heads(k.dA, 4 * g + r, 1).broadcast_to([P, P])
                    mm = pe.matmul(pl[:, g % 2, r, :], dah, k.tri, start=True, stop=True)
                mm.then_inc(cumulated, 1)
                if g:
                    outputs(g - 1)
                    pe.wait_ge(h_out, g)
                else:
                    pe.wait_ge(drained_v, 4)
                pe.matmul(ph[:, 0:4 * HD], bnat[:, g, :], xdec[:, g * 4 * HD:(g + 1) * 4 * HD],
                          start=True, stop=True).then_inc(h_done, 1)
            outputs(GROUPS - 1)

        @block.scalar
        def _(act):
            for n in range(2):
                act.wait_ge(turned, 5 + n)
                act.activation(bnat[:, 4 * n:4 * n + 4, :].rearrange("p g n -> p (g n)"), tr[:, n, :], ACT.Copy
                               ).then_inc(drained_a, 1)
            for n in range(2):
                act.wait_ge(crossed, n + 1)
                act.activation(cb[:, 4 * n:4 * n + 4, :].rearrange("p g n -> p (g n)"), tr[:, n, :], ACT.Copy
                               ).then_inc(crossed_out, 1)
            for g in range(GROUPS):
                act.wait_ge(lm_ready, g + 1)
                if c:
                    if g >= 2:
                        act.wait_ge(carried, g - 1)
                    act.activation(ea[:, g % 2], pl[:, g % 2], ACT.Exp).then_inc(ea_ready, 1)
                if g >= 2:
                    act.wait_ge(mixed, g - 1)
                for r in range(4):
                    e = act.activation(em[:, g % 2, r, :], lm[:, g % 2, r, :], ACT.Exp, bias=heads(k.nac, 4 * g + r, 1))
                e.then_inc(em_ready, 1)
                if c == 0:
                    act.wait_ge(h_done, g + 1)
                    act.activation(k.hT[:, g * 4 * HD:(g + 1) * 4 * HD], ph[:, 0:4 * HD], ACT.Copy).then_inc(h_out, 1)

        @block.vector
        def _(dve):
            if c == 0:
                dve.tensor_copy(k.Y[:, :, TP:T], k.ys[:])
            for n in range(4):
                dve.wait_ge(turned, n + 1)
                for out, f in ((xdt, k.dt), (xdec, k.dec)):
                    o = dve.tensor_tensor(out[:, n * 512:(n + 1) * 512].rearrange("p (h d) -> p h d", d=HD),
                                          tr[:, n % 2, :].rearrange("p (h d) -> p h d", d=HD),
                                          heads(f, 8 * n, 8).unsqueeze(2).broadcast_to([P, 8, HD]), ALU.mult)
                o.then_inc(drained_v, 1)

            def finish(g):
                dve.wait_ge(y_done, g + 1)
                if g:
                    dve.wait_ge(y_out, g)
                for i in range(2):
                    o = dve.scalar_tensor_tensor(out=k.Y[:, 2 * g + i, t0:t0 + P], in0=k.xbc[:, 2 * g + i, t0:t0 + P],
                                                 scalar=k.dskip[:, 2 * g + i:2 * g + i + 1],
                                                 in1=py[:, g % 2, i * P:(i + 1) * P], op0=ALU.mult, op1=ALU.add)
                o.then_inc(y_skip, 1)
                if c:
                    hg = k.hT[:, g * 4 * HD:(g + 1) * 4 * HD]
                    dve.wait_ge(h_done, g + 1)
                    dve.tensor_tensor(hg.rearrange("p (h d) -> p h d", d=HD), hg.rearrange("p (h d) -> p h d", d=HD),
                                      heads(k.etot, 4 * g, 4).unsqueeze(2).broadcast_to([P, 4, HD]), ALU.mult
                                      ).then_inc(h_scaled, 1)
                    dve.wait_ge(h_scaled, g + 1)
                    dve.tensor_tensor(hg, hg, ph[:, 0:4 * HD], ALU.add).then_inc(h_out, 1)
                dve.wait_ge(y_skip, g + 1)
                yg = k.Y[:, 2 * g:2 * g + 2, t0:t0 + P]
                dve.tensor_tensor(yg, yg, k.zs[:, 2 * g:2 * g + 2, t0:t0 + P], ALU.mult).then_inc(y_out, 1)

            for g in range(GROUPS):
                dve.wait_ge(cumulated, g + 1)
                if g >= 2:
                    dve.wait_ge(em_ready, g - 1)
                dve.tensor_tensor(lm[:, g % 2], pl[:, g % 2], k.negt.unsqueeze(1).broadcast_to([P, 4, P]), ALU.add
                                  ).then_inc(lm_ready, 1)
                if g == 0:
                    dve.wait_ge(crossed_out, 2)
                if g:
                    finish(g - 1)
                if c:
                    dve.wait_ge(ea_ready, g + 1)
                    ct = k.xbc[:, KI + GROUPS + g, t0:t0 + P].unsqueeze(1).broadcast_to([P, 4, P])
                    dve.tensor_tensor(ce[:, g % 2], ea[:, g % 2], ct, ALU.mult).then_inc(carried, 1)
                dve.wait_ge(em_ready, g + 1)
                dve.tensor_tensor(mx[:, g % 2], em[:, g % 2], cb[:, g, :].unsqueeze(1).broadcast_to([P, 4, P]),
                                  ALU.mult).then_inc(mixed, 1)
            finish(GROUPS - 1)
            dve.wait_ge(y_out, GROUPS)

        stored = sem("store")
        if c:
            @block.sync
            def _(sp):
                sp.wait_ge(h_out, GROUPS)
                sp.dma_start(k.o_ssm_p[:], k.hT[:]).then_inc(stored, 16)
                sp.wait_ge(stored, 16)


def ssd_norm(nc, k):
    with ExitStack() as ctx:
        sem = signals(nc, ctx, "sn_")
        sq, rms, g = tensors(nc, ctx, sn_sq=(P, 2, 2, T), sn_rms=(P, 2, T), sn_g=(P, KI))
        ps = ctx.enter_context(nc.psum_tensor("sn_ps", [P, 2, 512], F32))
        loaded, squared, summed, rooted, inverted, done = (sem(n) for n in ("c", "sq", "sum", "root", "inv", "done"))
        block = ctx.enter_context(nc.Block())

        @block.sync
        def _(sp):
            sp.dma_start(g[:], k.d_gssd[:]).then_inc(loaded, 16)

        @block.scalar
        def _(act):
            for n in range(GROUPS + 1):
                if n < GROUPS:
                    if n >= 2:
                        act.wait_ge(summed, n - 1)
                    act.activation(sq[:, n % 2], k.Y[:, 2 * n:2 * n + 2, :], ACT.Square).then_inc(squared, 1)
                if n:
                    act.wait_ge(summed, n)
                    if n > 2:
                        act.wait_ge(done, n - 2)
                    act.activation(rms[:, (n - 1) % 2], ps[:, (n - 1) % 2, 0:T], ACT.Sqrt, scale=1.0 / (2 * P),
                                   bias=k.eps).then_inc(rooted, 1)

        @block.tensor
        def _(pe):
            for n in range(GROUPS):
                pe.wait_ge(squared, n + 1)
                if n >= 2:
                    pe.wait_ge(rooted, n - 1)
                for i in range(2):
                    mm = pe.matmul(ps[:, n % 2, 0:T], k.ones, sq[:, n % 2, i, :], start=i == 0, stop=i == 1)
                mm.then_inc(summed, 1)

        @block.vector
        def _(dve):
            dve.wait_ge(loaded, 16)
            for n in range(GROUPS):
                dve.wait_ge(rooted, n + 1)
                dve.reciprocal(rms[:, n % 2], rms[:, n % 2]).then_inc(inverted, 1)
                dve.wait_ge(inverted, n + 1)
                for c in (2 * n, 2 * n + 1):
                    o = dve.scalar_tensor_tensor(out=k.Y[:, c, :], in0=k.Y[:, c, :], scalar=g[:, c:c + 1],
                                                 in1=rms[:, n % 2], op0=ALU.mult, op1=ALU.mult)
                o.then_inc(done, 1)
            dve.wait_ge(done, GROUPS)


def choose_sample(nc, k, tiles):
    with ExitStack() as ctx:
        sem = signals(nc, ctx, "cs_")
        ikt, iqd, r, score, wsel = tensors(
            nc, ctx, cs_ikt=(P, 2, 512), cs_iqd=(P, TS, TS * IH), cs_r=(TS * IH, NKS),
            cs_score=(TS, NKS), cs_wsel=(TS * IH, TS))
        top, = tensors(nc, ctx, cs_top=(TS, 8))
        tr = ctx.enter_context(nc.psum_tensor("cs_tr", [P, 2, 512], F32))
        small = ctx.enter_context(nc.psum_tensor("cs_small", [P, 512], F32))
        ps = ctx.enter_context(nc.psum_tensor("cs_ps", [P, 3, 512], F32))
        (cleared, spread, diag, weighed, turned, copied, scored, rectified, summed, read, found,
         replaced, masked) = (sem(n) for n in (
             "clr", "spread", "diag", "w", "turn", "copy", "score", "relu", "sum", "read", "max", "rep",
             "mask"))
        block = ctx.enter_context(nc.Block())

        ik = k.paged[:].rearrange("p (a d) -> p a d", d=HD)
        ROUNDS = SEL_S // 8
        early = [[t] for t in tiles[:TS]]
        late = shares(tiles[TS:], ROUNDS)

        @block.sync
        def _(sp):
            for n in tiles:
                k.proj.load(sp, n + WSLOTS)
            sp.wait_ge(k.proj.saved, KC)
            sp.dma_start(k.o_conv_p[:], k.proj.tail_p[:]).then_inc(k.proj.stored, 16)
            sp.dma_start(k.o_conv_s[:], k.proj.tail_s[:]).then_inc(k.proj.stored, 16)
            sp.wait_ge(k.proj.stored, 32)

        @block.gpsimd
        def _(pool):
            for n in tiles:
                k.proj.tails(pool, n)

        @block.tensor
        def _(pe):
            for h in range(IH):
                pe.matmul(small[:, h * TS:(h + 1) * TS], k.selhi if h % 2 else k.sello,
                               k.att[:, IQ0 + h // 2, TP:T], start=True, stop=True)
            pe.matmul(small[0:TS * IH, 128:128 + TS], k.iwsel, k.misc[:, TP:T], start=True, stop=True).then_inc(spread, 1)
            pe.wait_ge(k.ik_loaded, 16 * TS * PAGES)
            pe.wait_ge(diag, TS)

            def scores(b):
                pe.wait_ge(copied, b + 1)
                for half in range(2):
                    rows = slice(half * HD, half * HD + HD)
                    mm = pe.matmul(ps[0:TS * IH, half, :], iqd[rows, b, :], ikt[rows, b % 2, :],
                                   start=b == 0, stop=b == TS - 1)
                mm = pe.matmul(ps[0:TS * IH, 2, 0:1], iqd[0:HD, b, :], k.misc[0:HD, TP + b:TP + b + 1],
                               start=b == 0, stop=b == TS - 1)
                mm.then_inc(scored, 1)

            for b in range(TS + 1):
                if b < TS:
                    if b >= 2:
                        pe.wait_ge(copied, b - 1)
                    for j in range(PAGES // 2):
                        at = b * PAGES + 2 * j
                        mm = pe.transpose(tr[:, b % 2, j * P:(j + 1) * P],
                                          ik[:, at:at + 2, :].rearrange("p a d -> p (a d)"), k.ident)
                    mm.then_inc(turned, 1)
                if b:
                    scores(b - 1)
                if b < TS:
                    for tile in early[b]:
                        k.proj.multiply(pe, tile)
            pe.wait_ge(rectified, 1)
            pe.wait_ge(weighed, 2)
            for a, n in ((0, 512), (512, 512), (1024, 1)):
                mm = pe.matmul(ps[0:TS, a // 512, 0:n], wsel[:], r[:, a:a + n], start=True, stop=True)
            mm.then_inc(summed, 1)
            for tile in tiles[TS:]:
                k.proj.multiply(pe, tile)

        @block.scalar
        def _(act):
            for b in range(TS):
                act.wait_ge(turned, b + 1)
                if b >= 2:
                    act.wait_ge(scored, b - 1)
                act.activation(ikt[:, b % 2, :], tr[:, b % 2, :], ACT.Copy).then_inc(copied, 1)
                for tile in early[b]:
                    k.proj.evacuate(act, tile)
            act.wait_ge(scored, TS)
            for half in range(2):
                act.activation(r[:, 0:PAST].rearrange("p (j a s) -> p j a s", a=2, s=PG)[:, :, half, :],
                               ps[0:TS * IH, half, :].rearrange("p (j s) -> p j s", s=PG), ACT.Relu, scale=HD ** -0.5)
            act.activation(r[:, PAST:NKS], ps[0:TS * IH, 2, 0:1], ACT.Relu, scale=HD ** -0.5).then_inc(rectified, 1)
            for tile in tiles[TS:]:
                k.proj.evacuate(act, tile)

        @block.vector
        def _(dve):
            dve.memset(iqd[:], 0.0).then_inc(cleared, 1)
            dve.wait_ge(cleared, 1)
            dve.wait_ge(spread, 1)
            for b in range(TS):
                dve.tensor_copy(iqd[:, b, b * IH:(b + 1) * IH],
                                small[:, 0:IH * TS].rearrange("p (h b) -> p h b", b=TS)[:, :, b]).then_inc(diag, 1)
            dve.tensor_scalar(wsel[:], small[0:TS * IH, 128:128 + TS], IH ** -0.5, None, ALU.mult).then_inc(weighed, 1)
            dve.wait_ge(weighed, 1)
            dve.tensor_tensor(wsel[:], wsel[:], k.own_ih, ALU.mult).then_inc(weighed, 1)
            for tile in tiles[:TS]:
                k.proj.convolve(dve, tile)
            dve.wait_ge(summed, 1)
            for a, n in ((0, 512), (512, 512), (1024, 1)):
                o = dve.tensor_copy(score[:, a:a + n], ps[0:TS, a // 512, 0:n])
            o.then_inc(read, 1)
            dve.wait_ge(read, 1)
            for n in range(SEL_S // 8):
                if n:
                    dve.wait_ge(replaced, n)
                dve.max(top[:], score[:]).then_inc(found, 1)
                dve.wait_ge(found, n + 1)
                dve.match_replace(score[:], top[:], score[:], LOW).then_inc(replaced, 1)
                for tile in late[n]:
                    k.proj.convolve(dve, tile)
            dve.wait_ge(replaced, SEL_S // 8)
            dve.tensor_scalar(k.negs[:], score[:], LOW, NEG, ALU.not_equal, ALU.mult).then_inc(masked, 1)
            dve.wait_ge(masked, 1)


class SampleState:
    SLOTS, UNITS, CT, GT = 3, 2 * TS, KI // 2, GROUPS // 2

    def __init__(self, nc, ctx, k):
        self.k = k
        self.h, self.dtx, self.y, self.junk, self.skip = tensors(
            nc, ctx, ss_h=(P, self.SLOTS, KI, NST), ss_dtx=(P, KI, TS), ss_y=(P, KI, TS), ss_junk=(P, 4, NST),
            ss_skip=(P, KI, TS))
        self.pb = ctx.enter_context(nc.psum_tensor("ss_pb", [P, self.GT, NST], F32))
        self.pc = ctx.enter_context(nc.psum_tensor("ss_pc", [P, self.GT, NST], F32))
        sem = signals(nc, ctx, "ss_")
        self.loaded = [sem(f"ld{s}") for s in range(self.SLOTS)]
        self.stored = [sem(f"st{s}") for s in range(self.SLOTS)]
        self.scaled, self.b_ready, self.c_ready, self.faded, self.updated, self.read, self.closing = (
            sem(n) for n in ("dtx", "b", "c", "fade", "upd", "read", "close"))
        self.new = k.xbc[:, 0:KI, SAMP0:CV:4]

    def load(self, sp, b):
        s = b % self.SLOTS
        if b >= self.SLOTS:
            sp.wait_ge(self.stored[s], 16 * (b // self.SLOTS))
            sp.wait_ge(self.read, (b - self.SLOTS + 1) * KI)
        sp.dma_start(self.h[:, s], self.k.d_state[b]).then_inc(self.loaded[s], 16)

    def store(self, sp, b):
        sp.wait_ge(self.updated, KI * (b + 1))
        sp.dma_start(self.k.o_ssm_s[b], self.h[:, b % self.SLOTS]).then_inc(self.stored[b % self.SLOTS], 16)

    def all_stored(self, sp):
        for s in range(self.SLOTS):
            sp.wait_ge(self.stored[s], 16 * len(range(s, TS, self.SLOTS)))

    def spread(self, pe, u):
        k, at = self.k, SAMP0 + 4 * (u // 2)
        for out, first, ready, free in ((self.pb, KI, self.b_ready, self.updated),
                                        (self.pc, KI + GROUPS, self.c_ready, self.read)):
            if u:
                pe.wait_ge(free, u * self.CT)
            for i in range(self.GT):
                g = first + u % 2 * self.GT + i
                mm = pe.matmul(out[:, i, :], k.xbc[:, g, at:at + 1].broadcast_to([P, P]), k.ident,
                               start=True, stop=True)
            mm.then_inc(ready, 1)

    def fade(self, act, u):
        b, k = u // 2, self.k
        act.wait_ge(self.loaded[b % self.SLOTS], 16 * (b // self.SLOTS + 1))
        for i in range(self.CT):
            c = u % 2 * self.CT + i
            h = self.h[:, b % self.SLOTS, c, :]
            act.activation(h, h, ACT.Copy, scale=k.ex[:, c, TS + b:TS + b + 1]).then_inc(self.faded, 1)

    def update(self, dve, u):
        b, k = u // 2, self.k
        if u == 0:
            dve.tensor_tensor(self.dtx[:], self.new, k.ex[:, :, 0:TS], ALU.mult).then_inc(self.scaled, 1)
            dve.wait_ge(self.scaled, 1)
        dve.wait_ge(self.b_ready, u + 1)
        for i in range(self.CT):
            c = u % 2 * self.CT + i
            h = self.h[:, b % self.SLOTS, c, :]
            dve.wait_ge(self.faded, u * self.CT + i + 1)
            dve.scalar_tensor_tensor(out=h, in0=self.pb[:, i // 2, :], scalar=self.dtx[:, c, b:b + 1], in1=h,
                                     op0=ALU.mult, op1=ALU.add).then_inc(self.updated, 1)
        dve.wait_ge(self.c_ready, u + 1)
        for i in range(self.CT):
            c, n = u % 2 * self.CT + i, u * self.CT + i
            dve.wait_ge(self.updated, n + 1)
            if n >= 4:
                dve.wait_ge(self.read, n - 3)
            dve.tensor_tensor_reduce(self.junk[:, n % 4], self.h[:, b % self.SLOTS, c, :], self.pc[:, i // 2, :],
                                     1.0, 0.0, ALU.mult, ALU.add, self.y[:, c, b:b + 1]).then_inc(self.read, 1)

    def finish(self, dve):
        k = self.k
        dve.tensor_tensor(self.skip[:], self.new, k.dskip[:].unsqueeze(2).broadcast_to([P, KI, TS]), ALU.mult
                          ).then_inc(self.closing, 1)
        dve.wait_ge(self.closing, 1)
        dve.wait_ge(self.read, TS * KI)
        dve.tensor_tensor(self.skip[:], self.skip[:], self.y[:], ALU.add).then_inc(self.closing, 1)
        dve.wait_ge(self.closing, 2)
        dve.tensor_tensor(k.ys[:], self.skip[:], k.zs[:, :, TP:T], ALU.mult).then_inc(self.closing, 1)
        dve.wait_ge(self.closing, 3)


def attend_sample(nc, k):
    NG, GP = 4, 4
    with ExitStack() as ctx:
        sem = signals(nc, ctx, "as_")
        kt, qd, pr, prt = tensors(nc, ctx, as_kt=(P, 2, 4 * P),
                                      as_qd=(P, TS, 2, P), as_p=(P, NKS), as_pt=(P, PAGES, P))
        pd, pdt, st, hot, rel = tensors(nc, ctx, as_pd=(P, TS), as_pdt=(TS, P), as_st=(P, 8), as_hot=(NB, NKS),
                                        as_rel=(NB, P))
        tr = ctx.enter_context(nc.psum_tensor("as_tr", [P, 2, 512], F32))
        pl = ctx.enter_context(nc.psum_tensor("as_pl", [P, 3, 512], F32))
        po = ctx.enter_context(nc.psum_tensor("as_po", [P, 512], F32))
        by_sp = [sem(f"lsp{s}") for s in range(NG)]
        by_pool = [sem(f"lpool{s}") for s in range(NG)]
        (c_loaded, cleared, diag, turned, copied, logits, maxed, negated, expd, normed, newed, p_turned,
         p_copied, mixed, out) = (sem(n) for n in (
             "c", "clr", "diag", "turn", "copy", "logit", "max", "neg", "exp", "norm", "new", "pturn", "pcopy",
             "mix", "out"))
        ssd = SampleState(nc, ctx, k)
        EARLY = 12
        block = ctx.enter_context(nc.Block())
        flat = qd[:].rearrange("p b j n -> p (b j n)")
        kv = k.paged[:].rearrange("p (g i n) -> p g i n", g=NG, i=GP)
        assert PAGES * TS // GP % NG == 0
        VK = PAGES * TS // GP
        spans = ((0, 512), (512, 512), (PAST, 1))

        def load(eng, loaded, half, visit):
            if NG <= visit < VK + NG:
                eng.wait_ge(turned, 2 * (visit - NG + 1))
            elif visit >= VK + NG:
                eng.wait_ge(mixed, visit - VK - NG + 1)
            for i in (2 * half, 2 * half + 1):
                if visit < VK:
                    cache, at = k.d_ck, (visit % 2 * GP + i) * PAGES + visit // 2
                else:
                    cache, at = k.d_cv, (visit - VK) * GP + i
                page = eng.value_load(k.pages[0:1, at:at + 1], min_val=0, max_val=k.n_pool - 1)
                eng.dma_start(kv[:, visit % NG, i:i + 1, :], cache[bass.ds(page, 1)].rearrange("a s n -> s a n")
                              ).then_inc(loaded[visit % NG], 16)

        def arrived(pe, visit):
            pe.wait_ge(by_sp[visit % NG], 32 * (visit // NG + 1))
            pe.wait_ge(by_pool[visit % NG], 32 * (visit // NG + 1))

        @block.sync
        def _(sp):
            sp.dma_start(hot[:], k.d_hots[:]).then_inc(c_loaded, 16)
            sp.dma_start(rel[:], k.d_relbh[:]).then_inc(c_loaded, 16)
            for b in range(ssd.SLOTS):
                load(sp, by_sp, 0, b)
                ssd.load(sp, b)
            store_at = {6 + 2 * b: b for b in range(6)} | {24: 6, 28: 7}
            load_at = {7 + 2 * i: ssd.SLOTS + i for i in range(TS - ssd.SLOTS)}
            for visit in range(ssd.SLOTS, 2 * VK):
                load(sp, by_sp, 0, visit)
                if visit in store_at:
                    ssd.store(sp, store_at[visit])
                if visit in load_at:
                    ssd.load(sp, load_at[visit])
            ssd.all_stored(sp)

        @block.gpsimd
        def _(pool):
            for visit in range(2 * VK):
                load(pool, by_pool, 1, visit)

        @block.tensor
        def _(pe):
            pe.wait_ge(c_loaded, 32)
            pe.wait_ge(diag, 16)
            for n, (a, w) in enumerate(spans):
                pe.matmul(pl[:, n, 0:w], rel[:], hot[:, a:a + w], start=True, stop=False)

            def products(n):
                page, pair = n // 4, n % 4
                pe.wait_ge(copied, n + 1)
                for i in range(2):
                    for j in range(2):
                        mm = pe.matmul(pl[:, page // 4, page % 4 * P:(page % 4 + 1) * P], qd[:, 2 * pair + i, j, :],
                                       kt[:, n % 2, (2 * i + j) * P:(2 * i + j + 1) * P], start=False, stop=False)
                mm.then_inc(logits, 1)

            for n in range(4 * PAGES + 1):
                if n < 4 * PAGES:
                    page, pair = n // 4, n % 4
                    visit = n // 2
                    if n % 2 == 0:
                        arrived(pe, visit)
                    if n >= 2:
                        pe.wait_ge(copied, n - 1)
                    for i in range(2):
                        for j in range(2):
                            mm = pe.transpose(tr[:, n % 2, (2 * i + j) * P:(2 * i + j + 1) * P],
                                              kv[:, visit % NG, 2 * (n % 2) + i, j * P:(j + 1) * P], k.ident)
                    mm.then_inc(turned, 1)
                if n:
                    products(n - 1)
                if n % 2 == 1 and n // 2 < EARLY:
                    ssd.spread(pe, n // 2)
            for b in range(TS):
                for j in range(2):
                    pe.matmul(pl[:, 2, 0:1], qd[:, b, j, :], k.att[:, K0 + j, TP + b:TP + b + 1], start=False, stop=False)
            for n, (a, w) in enumerate(spans):
                mm = pe.matmul(pl[:, n, 0:w], k.rep_h, k.negs[:, a:a + w], start=False, stop=True)
            mm.then_inc(logits, 1)
            pe.wait_ge(normed, 1)
            for n in range(2):
                for i in range(4):
                    mm = pe.transpose(tr[:, n, i * P:(i + 1) * P], pr[:, (4 * n + i) * P:(4 * n + i + 1) * P], k.ident)
                mm.then_inc(p_turned, 1)
            pe.wait_ge(newed, 1)
            pe.wait_ge(p_copied, 1)
            pe.transpose(tr[0:TS, 0, 0:P], pd[:], k.ident).then_inc(p_turned, 1)
            pe.wait_ge(p_copied, 4)
            for b in range(TS):
                for part in range(2):
                    visit = VK + 2 * b + part
                    arrived(pe, visit)
                    for j in range(2):
                        cols = slice(b * 4 * REP + j * 8, b * 4 * REP + j * 8 + 8)
                        for i in range(GP):
                            mm = pe.matmul(po[:, cols], kv[:, visit % NG, i, j * P:(j + 1) * P],
                                           prt[:, GP * part + i, cols], start=b + part + j + i == 0, stop=False,
                                           skip_group_check=True)
                    if part == 0:
                        mm.then_inc(mixed, 1)
                for j in range(2):
                    cols = slice(b * 4 * REP + j * 8, b * 4 * REP + j * 8 + 8)
                    mm = pe.matmul(po[:, cols], k.vnew[:, j * P:(j + 1) * P], pdt[:, cols], start=False,
                                   stop=b == TS - 1 and j == 1, skip_group_check=True)
                mm.then_inc(mixed, 1)
                if EARLY + b < ssd.UNITS:
                    ssd.spread(pe, EARLY + b)

        @block.scalar
        def _(act):
            for n in range(4 * PAGES):
                act.wait_ge(turned, n + 1)
                if n >= 2:
                    act.wait_ge(logits, n - 1)
                act.activation(kt[:, n % 2, :], tr[:, n % 2, :], ACT.Copy).then_inc(copied, 1)
                if n % 2 == 1 and n // 2 < EARLY:
                    ssd.fade(act, n // 2)
            act.wait_ge(negated, 1)
            act.activation(pr[:, 0:PAST].rearrange("p (a n) -> p a n", n=512), pl[:, 0:2, :], ACT.Exp,
                           bias=st[:, 3:4], accum_out=st[:, 4:5])
            act.activation(pr[:, PAST:NKS], pl[:, 2, 0:1], ACT.Exp, bias=st[:, 3:4], accum_out=st[:, 5:6]
                           ).then_inc(expd, 1)
            for n in range(2):
                act.wait_ge(p_turned, n + 1)
                act.activation(prt[:, 4 * n:4 * n + 4, :], tr[:, n, :].rearrange("p (a n) -> p a n", n=P), ACT.Copy
                               ).then_inc(p_copied, 1)
            act.wait_ge(p_turned, 3)
            act.activation(pdt[:], tr[0:TS, 0, 0:P], ACT.Copy).then_inc(p_copied, 2)
            for u in range(EARLY, ssd.UNITS):
                ssd.fade(act, u)

        @block.vector
        def _(dve):
            dve.memset(qd[:], 0.0).then_inc(cleared, 1)
            dve.wait_ge(cleared, 1)
            for j in range(2):
                for half in range(2):
                    for r in range(REP):
                        rows = slice(half * HD, half * HD + HD)
                        at = j * P + 8 * j + 4 * half + r
                        dve.tensor_copy(flat[rows, at:at + (TS - 1) * (2 * P + HEADS) + 1:2 * P + HEADS],
                                        k.att[rows, 4 * j + r, TP:T]).then_inc(diag, 1)
            for u in range(EARLY):
                ssd.update(dve, u)
            dve.wait_ge(logits, 4 * PAGES + 1)
            dve.tensor_reduce(st[:, 0:1], pl[:, 0:2, :], AX.XY, ALU.max)
            dve.tensor_copy(st[:, 1:2], pl[:, 2, 0:1]).then_inc(maxed, 1)
            dve.wait_ge(maxed, 1)
            dve.tensor_tensor(st[:, 2:3], st[:, 0:1], st[:, 1:2], ALU.max).then_inc(maxed, 1)
            dve.wait_ge(maxed, 2)
            dve.tensor_scalar(st[:, 3:4], st[:, 2:3], -1.0, None, ALU.mult).then_inc(negated, 1)
            dve.wait_ge(expd, 1)
            dve.tensor_tensor(st[:, 6:7], st[:, 4:5], st[:, 5:6], ALU.add).then_inc(maxed, 1)
            dve.wait_ge(maxed, 3)
            dve.reciprocal(st[:, 7:8], st[:, 6:7]).then_inc(maxed, 1)
            dve.wait_ge(maxed, 4)
            dve.tensor_scalar(pr[:], pr[:], st[:, 7:8], None, ALU.mult).then_inc(normed, 1)
            dve.wait_ge(normed, 1)
            dve.tensor_scalar(pd[:], k.own_h, pr[:, PAST:NKS], None, ALU.mult).then_inc(newed, 1)
            for u in range(EARLY, ssd.UNITS):
                ssd.update(dve, u)
            ssd.finish(dve)
            dve.wait_ge(mixed, 2 * TS)
            o4 = po[:, 0:P].rearrange("p (b j n) -> p b j n", j=2, n=8)
            for j in range(2):
                for half in range(2):
                    rows = slice(half * HD, half * HD + HD)
                    dve.tensor_copy(k.yatt[rows, 4 * j:4 * j + 4, TP:T],
                                    o4[rows, :, j, 4 * half:4 * half + 4].rearrange("p b r -> p r b")).then_inc(out, 1)
            dve.wait_ge(out, 4)


def merge(nc, k):
    KB, SLOTS = KI + KD, 3
    with ExitStack() as ctx:
        sem = signals(nc, ctx, "mg_")
        w, wo, merged, part = tensors(nc, ctx, mg_w=(P, SLOTS, KB * P), mg_wo=(P, 4, KD * P), mg_m=(P, KD, T),
                                      mg_part=(P, 2, 2, T))
        pa = ctx.enter_context(nc.psum_tensor("mg_pa", [P, 2, 512], F32))
        pb = ctx.enter_context(nc.psum_tensor("mg_pb", [P, 2, 512], F32))
        po = ctx.enter_context(nc.psum_tensor("mg_po", [P, 2, 512], F32))
        w_loaded = [sem(f"w{s}") for s in range(SLOTS)]
        wo_loaded = [sem(f"wo{s}") for s in range(4)]
        multiplied, gated, summed, out_done, added = (sem(n) for n in ("mm", "gate", "sum", "out", "add"))
        block = ctx.enter_context(nc.Block())

        @block.sync
        def _(sp):
            for n in range(KD):
                if n >= SLOTS:
                    sp.wait_ge(multiplied, n - SLOTS + 1)
                sp.dma_start(w[:, n % SLOTS, :], k.d_w_ab[n]).then_inc(w_loaded[n % SLOTS], 16)
            for n in range(KD):
                if n >= 4:
                    sp.wait_ge(out_done, n - 3)
                sp.dma_start(wo[:, n % 4, :], k.d_w_out[n]).then_inc(wo_loaded[n % 4], 16)

        @block.tensor
        def _(pe):
            for n in range(KD):
                pe.wait_ge(w_loaded[n % SLOTS], 16 * (n // SLOTS + 1))
                if n >= 2:
                    pe.wait_ge(gated, 2 * (n - 1))
                for c in range(KB):
                    o = pa if c < KI else pb
                    rhs = k.Y[:, c, :] if c < KI else k.yatt[:, c - KI, :]
                    mm = pe.matmul(o[:, n % 2, 0:T], w[:, n % SLOTS, c * P:(c + 1) * P], rhs,
                                   start=c in (0, KI), stop=c in (KI - 1, KB - 1))
                mm.then_inc(multiplied, 1)
            pe.wait_ge(summed, KD)
            for n in range(KD):
                pe.wait_ge(wo_loaded[n % 4], 16 * (n // 4 + 1))
                if n >= 2:
                    pe.wait_ge(added, n - 1)
                for c in range(KD):
                    mm = pe.matmul(po[:, n % 2, 0:T], wo[:, n % 4, c * P:(c + 1) * P], merged[:, c, :],
                                   start=c == 0, stop=c == KD - 1)
                mm.then_inc(out_done, 1)

        @block.vector
        def _(dve):
            for n in range(KD):
                dve.wait_ge(multiplied, n + 1)
                if n >= 2:
                    dve.wait_ge(summed, n - 1)
                dve.tensor_tensor(part[:, n % 2, 0], pa[:, n % 2, 0:T], k.gate[:, n, :], ALU.mult).then_inc(gated, 1)
                dve.tensor_tensor(part[:, n % 2, 1], pb[:, n % 2, 0:T], k.gate[:, KD + n, :], ALU.mult
                                  ).then_inc(gated, 1)
                dve.wait_ge(gated, 2 * n + 2)
                dve.tensor_tensor(merged[:, n, :], part[:, n % 2, 0], part[:, n % 2, 1], ALU.add).then_inc(summed, 1)
            for n in range(KD):
                dve.wait_ge(out_done, n + 1)
                dve.tensor_tensor(k.xT[:, n, :], k.xT[:, n, :], po[:, n % 2, 0:T], ALU.add).then_inc(added, 1)
            dve.wait_ge(added, KD)


def peer_queries(nc, k):
    NT = 2 * PH
    with ExitStack() as ctx:
        sem = signals(nc, ctx, "pq_")
        sq, rms, g2, w = tensors(nc, ctx, pq_sq=(P, KD, T), pq_rms=(P, T), pq_g=(P, KD), pq_w=(P, WSLOTS, KD * P))
        ps = ctx.enter_context(nc.psum_tensor("pq_ps", [P, WSLOTS, 512], F32))
        pn = ctx.enter_context(nc.psum_tensor("pq_pn", [P, 512], F32))
        w_loaded = [sem(f"w{s}") for s in range(WSLOTS)]
        loaded, squared, summed, rooted, inverted, normed, multiplied, evacuated = (sem(n) for n in (
            "c", "sq", "sum", "root", "inv", "norm", "mm", "evac"))
        block = ctx.enter_context(nc.Block())

        @block.sync
        def _(sp):
            sp.dma_start(g2[:], k.d_g2[:]).then_inc(loaded, 16)
            sp.dma_start(k.keys[:], k.d_keys[:]).then_inc(loaded, 16)
            for n in range(NT):
                if n >= WSLOTS:
                    sp.wait_ge(multiplied, n - WSLOTS + 1)
                sp.dma_start(w[:, n % WSLOTS, :], k.d_wq[n]).then_inc(w_loaded[n % WSLOTS], 16)
            sp.wait_ge(loaded, 32)

        @block.scalar
        def _(act):
            act.activation(sq[:], k.xT[:], ACT.Square).then_inc(squared, 1)
            act.wait_ge(summed, 1)
            act.activation(rms[:], pn[:, 0:T], ACT.Sqrt, scale=1.0 / D_MODEL, bias=k.eps).then_inc(rooted, 1)
            for n in range(NT):
                act.wait_ge(multiplied, n + 1)
                act.activation(k.pq[:, n, :], ps[:, n % WSLOTS, 0:T], ACT.Copy).then_inc(evacuated, 1)
            act.wait_ge(evacuated, NT)

        @block.tensor
        def _(pe):
            pe.wait_ge(squared, 1)
            for c in range(KD):
                mm = pe.matmul(pn[:, 0:T], k.ones, sq[:, c, :], start=c == 0, stop=c == KD - 1)
            mm.then_inc(summed, 1)
            for n in range(NT):
                pe.wait_ge(w_loaded[n % WSLOTS], 16 * (n // WSLOTS + 1))
                if n >= WSLOTS:
                    pe.wait_ge(evacuated, n - WSLOTS + 1)
                if n == 0:
                    pe.wait_ge(normed, KD)
                for c in range(KD):
                    mm = pe.matmul(ps[:, n % WSLOTS, 0:T], w[:, n % WSLOTS, c * P:(c + 1) * P], k.hN[:, c, :],
                                   start=c == 0, stop=c == KD - 1)
                mm.then_inc(multiplied, 1)

        @block.vector
        def _(dve):
            dve.wait_ge(loaded, 32)
            dve.wait_ge(rooted, 1)
            dve.reciprocal(rms[:], rms[:]).then_inc(inverted, 1)
            dve.wait_ge(inverted, 1)
            for c in range(KD):
                dve.scalar_tensor_tensor(out=k.hN[:, c, :], in0=k.xT[:, c, :], scalar=g2[:, c:c + 1],
                                         in1=rms[:], op0=ALU.mult, op1=ALU.mult).then_inc(normed, 1)


def peer(nc, k):
    RING = 8
    PER = PH * TOPK
    SPER = PER * TS // P
    TILES = ((0, P), (P, P), (TP, TS))
    with ExitStack() as ctx:
        sem = signals(nc, ctx, "pe_")
        s, v, cand, eq, tv, fa, fb, e1, e2, idf, gsm = tensors(
            nc, ctx, pe_s=(P, 2 * PH, PK), pe_v=(P, 2 * PH, TOPK), pe_cand=(P, PH, TOPK * TOPK),
            pe_eq=(P, PER, TOPK), pe_tv=(P, PH, TOPK), pe_fa=(P, PER), pe_fb=(P, PER), pe_e1=(P, PER),
            pe_e2=(P, PER), pe_idf=(P, 2 * PH, TOPK), pe_gs=(P, PH))
        uv, hnat, a, gl, wt, dg, y = tensors(
            nc, ctx, pe_uv=(P, RING, 2 * D_MODEL), pe_hnat=(P, 3, D_MODEL), pe_a=(P, RING), pe_gl=(P, RING),
            pe_w=(P, RING), pe_dg=(P, RING, P), pe_y=(P, D_MODEL))
        gw, gws, hrep = tensors(nc, ctx, pe_gw=(P, 3, PER), pe_gws=(P, SPER), pe_hrep=(P, KD, P))
        ints = lambda n, *shape, dt=U32: ctx.enter_context(nc.sbuf_tensor(n, list(shape), dt))
        iv, tp, pa, idx, idxs = (ints("pe_iv", P, 2 * PH, TOPK), ints("pe_tp", P, PH, TOPK),
                                      ints("pe_pa", P, 2, PER), ints("pe_idx", P, 3, PER, dt=I32),
                                 ints("pe_idxs", P, SPER, dt=I32))
        ps = ctx.enter_context(nc.psum_tensor("pe_ps", [P, 4, 4, P], F32))
        ph = ctx.enter_context(nc.psum_tensor("pe_ph", [P, KD, P], F32))
        acc = ctx.enter_context(nc.psum_tensor("pe_acc", [P, KD, P], F32))
        repeated = sem("rep")
        gathered = [sem(f"ga{i}") for i in range(RING)]
        (scored, s_read, h_turned, h_read, step, subtracted, chosen, to_dram, moved, exped, indexed, dotted, gelued, weighed,
         diagonal, accumulated, y_read, y_out) = (sem(n) for n in (
             "score", "sread", "hturn", "hread", "step", "sub", "chosen", "todram", "moved", "exp", "index", "dot", "gelu",
             "w", "diag", "acc", "yread", "yout"))
        block = ctx.enter_context(nc.Block())
        BEFORE = (0, PER, 2 * PER)
        LOOPS = (PER // RING, PER // RING, SPER // RING)
        HALFWAY = LOOPS[0] // 2

        @block.tensor
        def _(pe):
            def scores(n):
                t0, m = TILES[n]
                if n:
                    pe.wait_ge(s_read, n)
                for i in range(2 * PH):
                    mm = pe.matmul(ps[0:m, i // 4, i % 4, :], k.pq[:, i, t0:t0 + m], k.keys[:, i, :],
                                   start=True, stop=True)
                mm.then_inc(scored, 1)

            scores(0)
            for n in range(3):
                if n:
                    pe.wait_ge(h_read, n)
                if n == 2:
                    pe.wait_ge(repeated, KD)
                for c in range(KD):
                    h = k.hN[:, c, n * P:(n + 1) * P] if n < 2 else hrep[:, c, :]
                    mm = pe.matmul(ph[:, c, :], h, k.ident, start=True, stop=True)
                mm.then_inc(h_turned, 1)
            scores(1)
            for n, (t0, m) in enumerate(TILES):
                if n:
                    pe.wait_ge(y_read, n)
                for c in range(KD):
                    pe.matmul(acc[0:m, c, :], k.xT[:, c, t0:t0 + m], k.ident, start=c % 4 == 0, stop=False,
                              skip_group_check=True)

                def steps(i):
                    for r in range(RING):
                        pe.wait_ge(diagonal, BEFORE[n] + i * RING + r + 1)
                        lhsT = dg[:, r, :] if n < 2 else dg[:, r, 0:TS]
                        for half in range(2):
                            mm = pe.matmul(acc[0:m, 4 * half:4 * half + 4, :], lhsT,
                                           uv[:, r, D_MODEL + half * 512:D_MODEL + (half + 1) * 512],
                                           start=False, stop=False, skip_group_check=True)
                        mm.then_inc(accumulated, 1)
                if n == 0:
                    with pe.Fori(0, HALFWAY) as i:
                        steps(i)
                    scores(2)
                    with pe.Fori(HALFWAY, LOOPS[n]) as i:
                        steps(i)
                elif n == 1:
                    with pe.Fori(0, LOOPS[n]) as i:
                        steps(i)
                else:
                    steps(0)

        @block.scalar
        def _(act):
            def exponents(n):
                m = TILES[n][1]
                act.wait_ge(subtracted, n + 1)
                act.activation(gw[0:m, n, :], gw[0:m, n, :], ACT.Exp).then_inc(exped, 1)

            for n in range(3):
                act.wait_ge(h_turned, n + 1)
                act.activation(hnat[:, n, :], ph[:].rearrange("p c d -> p (c d)"), ACT.Copy).then_inc(h_read, 1)
            exponents(0)
            for n, (t0, m) in enumerate(TILES):
                if n < 2:
                    act.wait_ge(chosen, n + 1)
                else:
                    act.wait_ge(moved, 32)

                def steps(i):
                    for r in range(RING):
                        at = BEFORE[n] + i * RING + r
                        act.wait_ge(dotted, at + 1)
                        act.activation(gl[:, r:r + 1], a[:, r:r + 1], ACT.Gelu_apprx_tanh).then_inc(gelued, 1)
                        act.wait_ge(gelued, at + 1)
                        g = gw[:, n, bass.ds(i * RING + r, 1)] if n < 2 else gws[:, bass.ds(i * RING + r, 1)]
                        act.activation(wt[:, r:r + 1], gl[:, r:r + 1], ACT.Copy, scale=g).then_inc(weighed, 1)
                        act.wait_ge(weighed, at + 1)
                        if n < 2:
                            act.activation(dg[:, r, :], k.ident, ACT.Copy, scale=wt[:, r:r + 1]).then_inc(diagonal, 1)
                        else:
                            act.activation(dg[:, r, 0:TS], k.own_h, ACT.Copy, scale=wt[:, r:r + 1]
                                           ).then_inc(diagonal, 1)
                if n == 0:
                    with act.Fori(0, HALFWAY) as i:
                        steps(i)
                    exponents(1)
                    with act.Fori(HALFWAY, LOOPS[n]) as i:
                        steps(i)
                    exponents(2)
                elif n == 1:
                    with act.Fori(0, LOOPS[n]) as i:
                        steps(i)
                else:
                    steps(0)
                act.wait_ge(accumulated, BEFORE[n] + LOOPS[n] * RING)
                if n:
                    act.wait_ge(y_out, 16 * n)
                act.activation(y[0:m, :], acc[0:m].rearrange("p c d -> p (c d)"), ACT.Copy).then_inc(y_read, 1)
                act.wait_ge(y_read, n + 1)
                act.dma_start(k.o_y[t0:t0 + m, :], y[0:m, :]).then_inc(y_out, 16)
            act.wait_ge(y_out, 48)

        @block.gpsimd
        def _(pool):
            for c in range(KD):
                pool.tensor_copy(hrep[:, c, :].rearrange("p (b i) -> p b i", b=TS),
                                 k.hN[:, c, TP:T].unsqueeze(2).broadcast_to([P, TS, P // TS])).then_inc(repeated, 1)
            for n in range(3):
                if n < 2:
                    pool.wait_ge(indexed, n + 1)
                else:
                    pool.wait_ge(moved, 32)

                for i in range(LOOPS[n] * RING):
                    at = BEFORE[n] + i
                    r = at % RING
                    if at >= RING:
                        pool.wait_ge(accumulated, at - RING + 1)
                    src = idx[:, n, i:i + 1] if n < 2 else idxs[:, i:i + 1]
                    pool.indirect_dma_start(uv[:, r, :], None, k.d_uv[:], bass.IndirectOffsetOnAxis(
                        ap=src, axis=0)).then_inc(gathered[r], 16)

        @block.sync
        def _(sp):
            sp.wait_ge(chosen, 3)
            sp.dma_start(k.s_idx[:], idx[0:TS, 2, :]).then_inc(to_dram, 16)
            sp.dma_start(k.s_gw[:], gw[0:TS, 2, :]).then_inc(to_dram, 16)
            sp.wait_ge(to_dram, 32)
            sp.dma_start(idxs[:], k.s_idx.rearrange("b (p n) -> (b p) n", n=SPER)).then_inc(moved, 16)
            sp.dma_start(gws[:], k.s_gw.rearrange("b (p n) -> (b p) n", n=SPER)).then_inc(moved, 16)

        @block.vector
        def _(dve):
            done = 0

            def one(instruction):
                nonlocal done
                instruction.then_inc(step, 1)
                done += 1

            def settled():
                dve.wait_ge(step, done)

            def largest(lists, rest, values, places, read=None):
                for half in range(2):
                    c8 = slice(8 * half, 8 * half + 8)
                    for n, (x, o) in enumerate(zip(lists, values)):
                        one(dve.max(o[:, c8], x))
                        if n % 4 == 3:
                            yield
                    settled()
                    for n, (x, o, p) in enumerate(zip(lists, values, places)):
                        one(dve.max_index(p[:, c8], o[:, c8], x))
                        if n % 4 == 3:
                            yield
                    if half == 0:
                        settled()
                        for n, (x, y, o) in enumerate(zip(lists, rest, values)):
                            ins = dve.match_replace(y, o[:, c8], x, LOW)
                            if read is not None and n == len(lists) - 1:
                                ins.then_inc(read, 1)
                                dve.wait_ge(read, reads + 1)
                            else:
                                one(ins)
                            if n % 4 == 3:
                                yield
                        settled()
                        lists = rest

            reads = 0

            def choose(n):
                nonlocal reads
                m = TILES[n][1]
                dve.wait_ge(scored, n + 1)
                yield from largest([ps[0:m, i // 4, i % 4, :] for i in range(2 * PH)],
                                   [s[0:m, i, :] for i in range(2 * PH)], [v[0:m, i, :] for i in range(2 * PH)],
                                   [iv[0:m, i, :] for i in range(2 * PH)], s_read)
                reads += 1
                settled()
                v4 = v[0:m].rearrange("p (h c) i -> p h c i", c=2)
                one(dve.tensor_tensor(cand[0:m].rearrange("p h (i j) -> p h i j", j=TOPK),
                                      v4[:, :, 0, :].unsqueeze(3).broadcast_to([m, PH, TOPK, TOPK]),
                                      v4[:, :, 1, :].unsqueeze(2).broadcast_to([m, PH, TOPK, TOPK]), ALU.add))
                yield
                settled()
                sums = [cand[0:m, h, :] for h in range(PH)]
                yield from largest(sums, sums, [tv[0:m, h, :] for h in range(PH)], [tp[0:m, h, :] for h in range(PH)])
                settled()
                dve.tensor_tensor(gw[0:m, n, :].rearrange("p (h i) -> p h i", h=PH), tv[0:m],
                                  tv[0:m, :, 0:1].broadcast_to([m, PH, TOPK]), ALU.subtract).then_inc(subtracted, 1)
                flat = tp[0:m].rearrange("p h i -> p (h i)")
                one(dve.tensor_single_scalar(pa[0:m, 0, :], flat, 4, ALU.logical_shift_right))
                one(dve.tensor_single_scalar(pa[0:m, 1, :], flat, TOPK - 1, ALU.bitwise_and))
                one(dve.tensor_copy(idf[0:m], iv[0:m]))
                settled()
                one(dve.tensor_copy(fa[0:m], pa[0:m, 0, :]))
                one(dve.tensor_copy(fb[0:m], pa[0:m, 1, :]))
                yield
                i4 = idf[0:m].rearrange("p (h c) i -> p h c i", c=2)
                for c, (f, e) in enumerate(((fa, e1), (fb, e2))):
                    settled()
                    one(dve.tensor_tensor(eq[0:m], f[0:m].unsqueeze(2).broadcast_to([m, PER, TOPK]),
                                          k.iota[0:m].unsqueeze(1).broadcast_to([m, PER, TOPK]), ALU.is_equal))
                    yield
                    settled()
                    e4 = eq[0:m].rearrange("p (h i) j -> p h i j", h=PH)
                    one(dve.tensor_tensor(e4, e4, i4[:, :, c, :].unsqueeze(2).broadcast_to([m, PH, TOPK, TOPK]),
                                          ALU.mult))
                    yield
                    settled()
                    one(dve.tensor_reduce(e[0:m], eq[0:m], AX.X, ALU.add))
                    yield
                settled()
                dve.scalar_tensor_tensor(out=idx[0:m, n, :], in0=e1[0:m], scalar=float(PK), in1=e2[0:m],
                                         op0=ALU.mult, op1=ALU.add).then_inc(indexed, 1)
                dve.wait_ge(indexed, n + 1)
                dve.wait_ge(subtracted, n + 1)

            def weights(n):
                m = TILES[n][1]
                if n:
                    dve.wait_ge(chosen, n)
                dve.wait_ge(exped, n + 1)
                g3 = gw[0:m, n, :].rearrange("p (h i) -> p h i", h=PH)
                one(dve.tensor_reduce(gsm[0:m], g3, AX.X, ALU.add))
                settled()
                one(dve.reciprocal(gsm[0:m], gsm[0:m]))
                settled()
                dve.tensor_tensor(g3, g3, gsm[0:m].unsqueeze(2).broadcast_to([m, PH, TOPK]), ALU.mult
                                  ).then_inc(chosen, 1)

            def dot(n, i, r, fresh=False):
                at = BEFORE[n] + i * RING + r
                dve.wait_ge(gathered[r], (BEFORE[n] // RING + i + 1) * 16)
                if not fresh:
                    dve.wait_ge(gelued, at - RING + 1)
                dve.tensor_tensor_reduce(uv[:, r, 0:D_MODEL], uv[:, r, 0:D_MODEL], hnat[:, n, :], 1.0, 0.0,
                                         ALU.mult, ALU.add, a[:, r:r + 1]).then_inc(dotted, 1)

            for _ in choose(0):
                pass
            weights(0)
            dve.wait_ge(h_read, 3)
            for half in range(2):
                rest = choose(half + 1)
                for i in range(HALFWAY * half, HALFWAY * (half + 1)):
                    for r in range(RING):
                        dot(0, i, r, i == 0)
                        next(rest, None)
                for _ in rest:
                    pass
            weights(1)
            weights(2)
            with dve.Fori(0, LOOPS[1]) as i:
                for r in range(RING):
                    dot(1, i, r)
            for r in range(RING):
                dot(2, 0, r)


def attend(nc, k, ctx):
    k.att, k.ikd, k.vnat, k.vnew, k.paged = tensors(
        nc, ctx, att=(P, N_ATT, T), ikd=(P, T), vnat=(P, 2, 2 * P), vnew=(TS, 2 * P), paged=(P, TS * PAGES * HD))
    k.pages = ctx.enter_context(nc.sbuf_tensor("pages", [1, TS * PAGES], I32))
    k.negs, = tensors(nc, ctx, negs=(TS, NKS))
    k.ik_loaded = signals(nc, ctx)("ik_loaded")
    with ExitStack() as projection:
        k.proj = Projection(nc, projection, k)
        ends = [Z0, Z0 + 5, Z0 + 9, Z0 + 32, N_TILES]
        part = [list(range(a, b)) for a, b in zip(ends, ends[1:])]
        norm_in(nc, k)
        project_attention(nc, k)
        with ExitStack() as inner:
            k.hankel, k.negp = tensors(nc, inner, hankel=(P, HEADS, TP), negp=(P, 2, TP))
            prepare_attention(nc, k, part[0])
            choose_prompt(nc, k, part[1])
            attend_prompt(nc, k, part[2])
        choose_sample(nc, k, part[3])
    time_steps(nc, k)
    attend_sample(nc, k)


def build(nc, ins, outs):
    k = Kept()
    (k.d_alog, k.d_cb, k.d_cik, k.d_ck, k.d_cst, k.d_cv, k.d_cw, k.d_cx, k.d_dskip, k.d_dtb, k.d_g1, k.d_g2,
     k.d_gqk, k.d_gssd, k.d_hot, k.d_hots, k.d_keys, k.d_old, k.d_pages, k.d_rel, k.d_relbh, k.d_spread,
     k.d_state, k.d_uv, k.d_w_ab, k.d_w_in, k.d_w_out, k.d_wq, k.d_xT)\
        = (ins[n] for n in IN_NAMES)
    (k.o_conv_p, k.o_conv_s, k.o_k, k.o_v, k.o_ik, k.o_y, k.o_ssm_p, k.o_ssm_s)\
        = (outs[n] for n in OUTS)
    k.n_pool = k.d_ck.shape[0]
    k.s_idx = nc.dram_tensor("s_idx", [TS, PH * TOPK], I32, kind="Internal").ap()
    k.s_gw = nc.dram_tensor("s_gw", [TS, PH * TOPK], F32, kind="Internal").ap()
    k.s_table = nc.dram_tensor("s_table", [HEADS, BIAS_N], F32, kind="Internal").ap()
    with ExitStack() as ctx:
        k.xT, k.cst, k.cx = tensors(nc, ctx, xT=(P, KD, T), cst=(P, C_END), cx=(P, CX_N))
        k.ident, k.ones, k.flip, k.tri, k.block, k.negt, k.sello, k.selhi = (
            k.cst[:, a:a + P] for a in range(0, C_END, P))
        k.eps, k.eps64 = k.cx[:, 0:1], k.cx[:, 1:2]
        k.iota, k.own_ih, k.own_h = k.cx[:, 16:32], k.cx[0:TS * IH, 32:40], k.cx[:, 40:48]
        k.iwsel, k.rep_h = k.cx[:, 64:128], k.cx[0:TS, 128:256]
        with ExitStack() as first:
            k.gate, k.yatt, k.misc, k.mnat, k.zs, k.xbc = tensors(
                nc, first, gate=(P, 2 * KD, T), yatt=(P, KD, T), misc=(P, T), mnat=(P, 2, P), zs=(P, KI, T),
                xbc=(P, KC, CV))
            k.dt, k.dA, k.nac, k.dec, k.etot, k.ex, k.dskip, k.ys = tensors(
                nc, first, dt=(P, 72), dA=(P, 72), nac=(P, 64), dec=(P, 64), etot=(P, 64), ex=(P, KI, 2 * TS),
                dskip=(P, KI), ys=(P, KI, TS))
            with ExitStack() as attention:
                attend(nc, k, attention)
            k.Y, = tensors(nc, first, Y=(P, KI, T))
            with ExitStack() as ssd:
                k.hT, = tensors(nc, ssd, hT=(P, D_INNER))
                ssd_chunk(nc, k, 0)
                ssd_chunk(nc, k, 1)
            ssd_norm(nc, k)
            merge(nc, k)
        k.hN, k.pq, k.keys = tensors(nc, ctx, hN=(P, KD, T), pq=(P, 2 * PH, T), keys=(P, 2 * PH, PK))
        peer_queries(nc, k)
        peer(nc, k)


OUTS = dict(o_conv_p=(P, KC, 3), o_conv_s=(P, KC, TS, 3), o_k=(P, 2, T), o_v=(P, 2, T), o_ik=(HD, T),
            o_y=(T, D_MODEL), o_ssm_p=(P, SSDH * HD), o_ssm_s=(TS, P, KI, NST))


def constants():
    c = np.zeros((P, C_END), np.float32)
    i = np.arange(P)
    c[:, C_ID:C_ID + P] = np.eye(P)
    c[:, C_ONES:C_ONES + P] = 1
    c[:, C_J:C_J + P] = np.eye(P)[::-1]
    c[:, C_TRI:C_TRI + P] = i[:, None] <= i[None]
    c[:, C_BLK:C_BLK + P] = i[:, None] // HD == i[None] // HD
    c[:, C_NEGT:C_NEGT + P] = np.where(i[:, None] <= i[None], 0, NEG)
    c[:, C_SELLO:C_SELLO + P] = i[:, None] == i[None] % HD
    c[:, C_SELHI:C_SELHI + P] = i[:, None] == HD + i[None] % HD
    x = np.zeros((P, CX_N), np.float32)
    x[:, 0], x[:, 1] = EPS, EPS * HD
    b = np.arange(TS)
    x[:, 16:32] = np.arange(TOPK)
    x[:, 32:40] = i[:, None] // IH == b
    x[:, 40:48] = i[:, None] // HEADS == b
    x[IW_P:IW_P + IH, 64:128] = np.arange(IH)[:, None] == np.arange(TS * IH)[None] % IH
    x[0:TS, 128:256] = b[:, None] == i[None] // HEADS
    return c, x


def bucket(dist):
    import math
    n = np.maximum(dist, 0)
    nf = np.maximum(n, 1).astype(np.float32)
    large = 16 + (np.log(nf / np.float32(16)) / np.float32(math.log(128 / 16)) * np.float32(16)).astype(np.int32)
    return np.where(n < 16, n, np.minimum(large, 31))


def kernel(x_prompt, x_sample, cache_k, cache_v, cache_idx_k, state_ssm, state_conv, page_table, rel_bias,
           norm1_g, w_in, conv_w, conv_b, dt_bias, a_log, d_skip, ssd_norm_g, q_norm_g, k_norm_g,
           w_branch_a, w_branch_b, w_out, norm2_g, peer_wq, peer_keys, peer_u, peer_v):
    import concourse.bacc as bacc
    from concourse.bass_utils import run_bass_kernel_spmd

    A = np.ascontiguousarray
    npa = np.asarray

    def chan(v):
        v = npa(v)
        v = v.reshape(*v.shape[:-1], v.shape[-1] // P, P)
        return A(np.moveaxis(v, (-1, -2), (0, 1)))

    def tiles(w):
        w = npa(w)
        return A(w.reshape(w.shape[0] // P, P, w.shape[1] // P, P).transpose(2, 1, 0, 3).reshape(
            w.shape[1] // P, P, w.shape[0]))

    def per_head(v):
        v = npa(v)[0]
        o = np.zeros((P, 2 * SSDH + TS), np.float32)
        o[:, :2 * SSDH] = np.tile(v, 2)[None]
        o[DT_P:, 2 * SSDH:] = v[:, None]
        return o

    spread = np.zeros((P, D_INNER), np.float32)
    spread[DT_P:] = np.arange(SSDH)[:, None] == np.arange(D_INNER)[None] // HD
    w = npa(w_in)[0]
    edges = np.cumsum((0, D_INNER, CONV_DIM, SSDH, HEADS * HD, KVH * HD, KVH * HD, IH * HD, HD, IH,
                       D_MODEL, D_MODEL))
    z, xbc, dt, q, kk, v, iq, ik, iw, ga, gb = (w[:, a:b] for a, b in zip(edges, edges[1:]))
    q = q.reshape(D_MODEL, 2, 2, REP, HD).transpose(0, 1, 3, 2, 4).reshape(D_MODEL, HEADS * HD)
    gap = np.zeros((D_MODEL, DT_P - IW_P - IH), np.float32)
    d_w_in = tiles(np.concatenate([q, kk, v, iq, ik, iw, gap, dt, z, xbc, ga, gb], axis=1))
    w_b = npa(w_branch_b)[0].reshape(2, 2, REP, HD, D_MODEL).transpose(0, 2, 1, 3, 4).reshape(HEADS * HD, D_MODEL)
    x = np.concatenate([npa(x_prompt)[0], npa(x_sample)[:, 0]], axis=0)
    d_cst, d_cx = constants()
    hot = (bucket(TP - 1 - np.arange(BIAS_N))[None] == np.arange(NB)[:, None]).astype(np.float32)
    arrays = dict(
        d_xT=chan(x), d_cst=d_cst, d_cx=d_cx, d_g1=chan(npa(norm1_g)[0]), d_w_in=d_w_in,
        d_cw=chan(npa(conv_w)[0]), d_cb=chan(npa(conv_b)[0]), d_old=chan(npa(state_conv)[0]),
        d_gqk=A(np.tile(np.stack([npa(q_norm_g)[0], npa(k_norm_g)[0]], axis=1), (2, 1))),
        d_rel=A(npa(rel_bias)), d_hot=hot,
        d_dtb=per_head(dt_bias), d_alog=per_head(a_log), d_spread=spread,
        d_dskip=chan(np.repeat(npa(d_skip)[0], HD)), d_gssd=chan(npa(ssd_norm_g)[0]),
        d_pages=A(npa(page_table).reshape(1, -1)), d_cik=A(npa(cache_idx_k)[0]),
        d_ck=A(npa(cache_k)[0].reshape(-1, PG, KVH * HD)), d_cv=A(npa(cache_v)[0].reshape(-1, PG, KVH * HD)),
        d_hots=(bucket(PAST - np.arange(NKS))[None] == np.arange(NB)[:, None]).astype(np.float32),
        d_relbh=A(np.tile(npa(rel_bias), (1, TS))),
        d_w_ab=tiles(np.concatenate([npa(w_branch_a)[0], w_b], axis=0)), d_w_out=tiles(npa(w_out)[0]),
        d_g2=chan(npa(norm2_g)[0]), d_wq=tiles(npa(peer_wq)[0]),
        d_keys=A(npa(peer_keys)[0].transpose(3, 1, 0, 2).reshape(PK, 2 * PH, PK)),
        d_uv=A(np.concatenate([npa(peer_u)[0], npa(peer_v)[0]], axis=1)),
        d_state=A(npa(state_ssm)[0].reshape(TS, KI, P, NST).transpose(0, 2, 1, 3)),
    )
    nc = bacc.Bacc("TRN2", target_bir_lowering=False, num_devices=1)
    ins = {n: nc.dram_tensor(n, list(a.shape), mybir.dt.from_np(a.dtype), kind="ExternalInput").ap()
           for n, a in arrays.items()}
    outs = {n: nc.dram_tensor(n, list(s), F32, kind="ExternalOutput").ap() for n, s in OUTS.items()}
    build(nc, ins, outs)
    r = run_bass_kernel_spmd(nc, [arrays], core_ids=[0]).results[0]

    def rows(o, n):
        return o.reshape(P, n, -1).transpose(2, 1, 0).reshape(-1, n * P)

    kn, vn, ikn = rows(r["o_k"], 2), rows(r["o_v"], 2), r["o_ik"].T
    heads = lambda a: A(a.reshape(-1, KVH, HD))
    conv_p = r["o_conv_p"].transpose(2, 1, 0).reshape(3, CONV_DIM)
    conv_s = r["o_conv_s"].transpose(2, 3, 1, 0).reshape(TS, 3, CONV_DIM)
    y = r["o_y"]
    ssm_p = r["o_ssm_p"].T.reshape(SSDH, HD, NST)
    ssm_s = r["o_ssm_s"].transpose(0, 2, 1, 3).reshape(TS, SSDH, HD, NST)
    return (A(y[None, :TP]), A(y[TP:, None]),
            heads(kn[:TP])[None, None], heads(vn[:TP])[None, None], A(ikn[:TP])[None, None],
            A(ssm_p)[None, None], A(conv_p)[None, None],
            A(heads(kn[TP:])[None, :, None]), A(heads(vn[TP:])[None, :, None]), A(ikn[TP:][None, :, None]),
            A(ssm_s)[None], A(conv_s)[None])
```

```python
from contextlib import ExitStack

import concourse.bass as bass
from concourse import mybir
import numpy as np

ALU = mybir.AluOpType
ACT = mybir.ActivationFunctionType
AX = mybir.AxisListType
F32 = mybir.dt.float32
I32 = mybir.dt.int32
U32 = mybir.dt.uint32

P = 128
D_MODEL, D_INNER, CONV_DIM = 1024, 2048, 4096
KD = D_MODEL // P
KI = D_INNER // P
KC = CONV_DIM // P
TP, TS = 256, 8
T = TP + TS
CW = 4
RAW = 3 + TP + 4 * TS
CV = RAW - 3
SAMP0 = 3 + TP
HEADS, KVH, REP, HD = 16, 4, 4, 64
IH = 8
SSDH, GROUPS, NST = 32, 8, 128
PAGES, PG = 8, 128
PAST = PAGES * PG
NKS = PAST + 1
SEL_P, SEL_S = 64, 256
NB = 32
PH, PK, TOPK = 8, 128, 16
NEXP = PK * PK
EPS = 1e-6
NEG = -1.0e30
LOW = -3.0e38

N_Z, N_XBC, N_ATT, N_GATE = KI, KC, 16, 16
N_TILES = N_Z + N_XBC + N_ATT + N_GATE + 1
Z0 = N_ATT + 1
XBC0 = Z0 + N_Z
GATE0 = XBC0 + N_XBC
N_LAST = 10
END = N_TILES - N_LAST
Q0, K0, V0, IQ0 = 0, 8, 10, 12
IW_P, DT_P = 64, 96
WSLOTS, BANKS = 4, 2
IK_FIRST = 44

C_ID, C_ONES, C_J, C_TRI, C_BLK, C_NEGT, C_SELLO, C_SELHI, C_END = (P * i for i in range(9))
CX_N = 256
BIAS_N = 384


def tensors(nc, ctx, **shapes):
    return [ctx.enter_context(nc.sbuf_tensor(n, [s[0], *s[1:]], F32)) for n, s in shapes.items()]


class Kept:
    pass


IN_NAMES = ("d_alog", "d_cb", "d_cik", "d_ck", "d_cst", "d_cv", "d_cw", "d_cx", "d_dskip", "d_dtb", "d_g1",
            "d_g2", "d_gqk", "d_gssd", "d_hot", "d_hots", "d_keys", "d_old", "d_pages", "d_rel",
            "d_relbh", "d_spread", "d_state", "d_uv", "d_w_ab", "d_w_in", "d_w_out", "d_wq", "d_xT")


def signals(nc, ctx, prefix=""):
    made = []

    def close():
        nc.clear_and_free_semaphores(made)
        nc.all_engine_barrier()
    ctx.callback(close)

    def sem(name):
        made.append(nc.alloc_semaphore(prefix + name))
        return made[-1]
    return sem


def norm_in(nc, k):
    with ExitStack() as ctx:
        sem = signals(nc, ctx)
        xsq, g1, rms = tensors(nc, ctx, n1_xsq=(P, KD, T), n1_g=(P, KD), n1_rms=(P, T))
        ps = ctx.enter_context(nc.psum_tensor("n1_ps", [P, 512], F32))
        x_loaded, c_loaded, squared, summed, rooted, inverted, done = (sem(n) for n in (
            "n1_x", "n1_c", "n1_sq", "n1_sum", "n1_root", "n1_inv", "n1_done"))
        block = ctx.enter_context(nc.Block())

        @block.sync
        def _(sp):
            sp.dma_start(k.xT[:], k.d_xT[:]).then_inc(x_loaded, 16)
            sp.dma_start(k.cst[:], k.d_cst[:]).then_inc(c_loaded, 16)
            sp.dma_start(k.cx[:], k.d_cx[:]).then_inc(c_loaded, 16)
            sp.dma_start(g1[:], k.d_g1[:]).then_inc(c_loaded, 16)
            for n in range(WSLOTS):
                k.proj.load(sp, n)
            sp.wait_ge(c_loaded, 48)

        @block.scalar
        def _(act):
            act.wait_ge(x_loaded, 16)
            act.activation(xsq[:], k.xT[:], ACT.Square).then_inc(squared, 1)
            act.wait_ge(c_loaded, 48)
            act.wait_ge(summed, 1)
            act.activation(rms[:], ps[:, 0:T], ACT.Sqrt, scale=1.0 / D_MODEL, bias=k.eps).then_inc(rooted, 1)

        @block.tensor
        def _(pe):
            pe.wait_ge(c_loaded, 48)
            pe.wait_ge(squared, 1)
            for c in range(KD):
                mm = pe.matmul(ps[:, 0:T], k.ones, xsq[:, c, :], start=c == 0, stop=c == KD - 1)
            mm.then_inc(summed, 1)

        @block.vector
        def _(dve):
            dve.wait_ge(rooted, 1)
            dve.reciprocal(rms[:], rms[:]).then_inc(inverted, 1)
            dve.wait_ge(inverted, 1)
            dve.wait_ge(c_loaded, 48)
            for c in range(KD):
                dve.scalar_tensor_tensor(out=k.xn[:, c, :], in0=k.xT[:, c, :], scalar=g1[:, c:c + 1],
                                         in1=rms[:], op0=ALU.mult, op1=ALU.mult).then_inc(done, 1)
            dve.wait_ge(done, KD)


class Projection:

    def __init__(self, nc, ctx, k):
        self.k = k
        (self.w, self.raw, self.cv, self.cw, self.cb, self.old, self.tail_p, self.tail_s) = tensors(
            nc, ctx, pi_w=(P, WSLOTS, KD * P), pi_raw=(P, WSLOTS, RAW), pi_cv=(P, WSLOTS, CV),
            pi_cw=(P, KC, CW), pi_cb=(P, KC), pi_old=(P, KC, TS, 3), pi_tail_p=(P, KC, 3),
            pi_tail_s=(P, KC, TS, 3))
        self.ps = ctx.enter_context(nc.psum_tensor("pi_ps", [P, BANKS, 512], F32))
        sem = signals(nc, ctx, "pi_")
        self.w_loaded = [sem(f"w{s}") for s in range(WSLOTS)]
        (self.c_loaded, self.zeroed, self.multiplied, self.evacuated, self.filled, self.saved, self.tap,
         self.convolved, self.rectified, self.stored) = (sem(n) for n in (
             "c", "zero", "mm", "evac", "fill", "saved", "tap", "conv", "silu", "store"))

    def blocks(self, s):
        return self.raw[:, s, SAMP0:SAMP0 + 4 * TS].rearrange("p (b j) -> p b j", j=4)

    def load(self, sp, n):
        if n < END:
            if n >= WSLOTS:
                sp.wait_ge(self.multiplied, n - WSLOTS + 1)
            sp.dma_start(self.w[:, n % WSLOTS, :], self.k.d_w_in[n]).then_inc(self.w_loaded[n % WSLOTS], 16)

    def multiply(self, pe, n):
        pe.wait_ge(self.w_loaded[n % WSLOTS], 16 * (n // WSLOTS + 1))
        if n >= BANKS:
            pe.wait_ge(self.evacuated, n - BANKS + 1)
        for c in range(KD):
            mm = pe.matmul(self.ps[:, n % BANKS, 0:T], self.w[:, n % WSLOTS, c * P:(c + 1) * P],
                           self.k.xn[:, c, :], start=c == 0, stop=c == KD - 1)
        mm.then_inc(self.multiplied, 1)

    def evacuate(self, act, n):
        k, ps = self.k, self.ps[:, n % BANKS, 0:T]
        act.wait_ge(self.multiplied, n + 1)
        if n < XBC0:
            act.activation(k.zs[:, n - Z0, :], ps, ACT.Silu).then_inc(self.evacuated, 1)
        elif n < GATE0:
            s = (n - XBC0) % WSLOTS
            if n - XBC0 >= WSLOTS:
                act.wait_ge(self.convolved, n - XBC0 - WSLOTS + 1)
                act.wait_ge(self.saved, n - XBC0 - WSLOTS + 1)
            act.activation(self.raw[:, s, 3:3 + TP], self.ps[:, n % BANKS, 0:TP], ACT.Copy)
            act.activation(self.blocks(s)[:, :, 3], self.ps[:, n % BANKS, TP:T], ACT.Copy
                           ).then_inc(self.evacuated, 1)
        else:
            act.activation(k.gate[:, n - GATE0, :], ps, ACT.Sigmoid).then_inc(self.evacuated, 1)
        i = n - WSLOTS - XBC0
        if 0 <= i < KC:
            act.wait_ge(self.convolved, i + 1)
            act.activation(k.xbc[:, i, :], self.cv[:, i % WSLOTS, :], ACT.Silu).then_inc(self.rectified, 1)

    def convolve(self, dve, n):
        i = n - 2 - XBC0
        if not 0 <= i < KC:
            return
        s, cv = i % WSLOTS, self.cv[:, i % WSLOTS, :]
        dve.wait_ge(self.evacuated, i + XBC0 + 1)
        dve.wait_ge(self.filled, i + 1)
        if i >= WSLOTS:
            dve.wait_ge(self.rectified, i - WSLOTS + 1)
        else:
            dve.wait_ge(self.c_loaded, 48)
            dve.wait_ge(self.zeroed, WSLOTS)
        dve.tensor_scalar(cv, self.raw[:, s, 0:CV], self.cw[:, i, 0:1], self.cb[:, i:i + 1], ALU.mult, ALU.add
                          ).then_inc(self.tap, 1)
        for j in range(1, CW):
            dve.wait_ge(self.tap, i * (CW - 1) + j)
            dve.scalar_tensor_tensor(out=cv, in0=self.raw[:, s, j:j + CV], scalar=self.cw[:, i, j:j + 1], in1=cv,
                                     op0=ALU.mult, op1=ALU.add
                                     ).then_inc(self.tap if j < CW - 1 else self.convolved, 1)

    def tails(self, pool, n):
        i = n - XBC0
        if not 0 <= i < KC:
            return
        s = i % WSLOTS
        if i >= WSLOTS:
            pool.wait_ge(self.convolved, i - WSLOTS + 1)
            pool.wait_ge(self.saved, i - WSLOTS + 1)
        else:
            pool.wait_ge(self.c_loaded, 48)
        pool.tensor_copy(self.blocks(s)[:, :, 0:3], self.old[:, i]).then_inc(self.filled, 1)
        pool.wait_ge(self.evacuated, n + 1)
        pool.wait_ge(self.filled, i + 1)
        pool.tensor_copy(self.tail_p[:, i, :], self.raw[:, s, TP:TP + 3])
        pool.tensor_copy(self.tail_s[:, i], self.blocks(s)[:, :, 1:4]).then_inc(self.saved, 1)


class LastGates:
    SLOTS = 3

    def __init__(self, nc, ctx, k):
        self.k = k
        self.w, = tensors(nc, ctx, lg_w=(P, self.SLOTS, KD * P))
        self.ps = ctx.enter_context(nc.psum_tensor("lg_ps", [P, 512], F32))
        sem = signals(nc, ctx, "lg_")
        self.w_loaded = [sem(f"w{s}") for s in range(self.SLOTS)]
        self.multiplied, self.evacuated = sem("mm"), sem("evac")

    def load(self, sp, g):
        if g >= N_LAST:
            return
        s = g % self.SLOTS
        if g >= self.SLOTS:
            sp.wait_ge(self.multiplied, g - self.SLOTS + 1)
        sp.dma_start(self.w[:, s, :], self.k.d_w_in[END + g]).then_inc(self.w_loaded[s], 16)

    def multiply(self, pe, g):
        s = g % self.SLOTS
        pe.wait_ge(self.w_loaded[s], 16 * (g // self.SLOTS + 1))
        if g:
            pe.wait_ge(self.evacuated, g)
        for c in range(KD):
            mm = pe.matmul(self.ps[:, 0:T], self.w[:, s, c * P:(c + 1) * P], self.k.xn[:, c, :],
                           start=c == 0, stop=c == KD - 1)
        mm.then_inc(self.multiplied, 1)

    def evacuate(self, act, g):
        act.wait_ge(self.multiplied, g + 1)
        act.activation(self.k.gate[:, END - GATE0 + g, :], self.ps[:, 0:T], ACT.Sigmoid).then_inc(self.evacuated, 1)


def shares(tiles, slots):
    return [[t for i, t in enumerate(tiles) if i * slots // len(tiles) == m] for m in range(slots)]


def load_indexer_pages(pool, k, first, end):
    ik = k.paged[:].rearrange("p (a d) -> p a d", d=HD)
    with pool.Fori(first, end) as i:
        page = pool.value_load(k.pages[0:1, bass.ds(i, 1)], min_val=0, max_val=k.n_pool - 1)
        pool.dma_start(ik[:, bass.ds(i, 1), :], k.d_cik[bass.ds(page, 1)].rearrange("a s d -> s a d")
                       ).then_inc(k.ik_loaded, 16)


def project_attention(nc, k):
    with ExitStack() as ctx:
        sem = signals(nc, ctx, "pr_")
        table, = (sem("table"),)
        block = ctx.enter_context(nc.Block())
        pj = k.proj

        @block.sync
        def _(sp):
            with sp.Fori(1, N_ATT // WSLOTS) as i:
                for s in range(WSLOTS):
                    sp.wait_ge(pj.multiplied, (i - 1) * WSLOTS + s + 1)
                    sp.dma_start(pj.w[:, s, :], k.d_w_in[bass.ds(i * WSLOTS + s, 1)].rearrange("a p n -> p (a n)")
                                 ).then_inc(pj.w_loaded[s], 16)
            for n in range(N_ATT, Z0 + WSLOTS):
                pj.load(sp, n)

        @block.tensor
        def _(pe):
            for n in range(WSLOTS):
                pj.multiply(pe, n)
            with pe.Fori(1, N_ATT // WSLOTS) as i:
                for s in range(WSLOTS):
                    pe.wait_ge(pj.w_loaded[s], (i + 1) * 16)
                    pe.wait_ge(pj.evacuated, i * WSLOTS + s - BANKS + 1)
                    for c in range(KD):
                        mm = pe.matmul(pj.ps[:, s % BANKS, 0:T], pj.w[:, s, c * P:(c + 1) * P], k.xn[:, c, :],
                                       start=c == 0, stop=c == KD - 1)
                    mm.then_inc(pj.multiplied, 1)
            pj.multiply(pe, N_ATT)

        @block.scalar
        def _(act):
            act.dma_start(pj.cw[:], k.d_cw[:]).then_inc(pj.c_loaded, 16)
            act.dma_start(pj.cb[:], k.d_cb[:]).then_inc(pj.c_loaded, 16)
            act.dma_start(pj.old[:], k.d_old[:]).then_inc(pj.c_loaded, 16)
            with act.Fori(0, N_ATT // WSLOTS) as i:
                for s in range(WSLOTS):
                    act.wait_ge(pj.multiplied, i * WSLOTS + s + 1)
                    act.activation(k.att[:, bass.ds(i * WSLOTS + s, 1), :], pj.ps[:, s % BANKS:s % BANKS + 1, 0:T],
                                   ACT.Copy).then_inc(pj.evacuated, 1)
            act.wait_ge(pj.multiplied, N_ATT + 1)
            act.activation(k.misc[:], pj.ps[:, N_ATT % BANKS, 0:T], ACT.Copy).then_inc(pj.evacuated, 1)
            act.wait_ge(pj.evacuated, N_ATT + 1)

        @block.gpsimd
        def _(pool):
            pool.dma_start(k.pages[:], k.d_pages[:]).then_inc(table, 16)
            for s in range(WSLOTS):
                pool.memset(pj.raw[:, s, 0:3], 0.0).then_inc(pj.zeroed, 1)
            pool.wait_ge(table, 16)
            load_indexer_pages(pool, k, 0, IK_FIRST)


def prepare_attention(nc, k, tiles):
    with ExitStack() as ctx:
        sem = signals(nc, ctx)
        sq, rms, gqk, table, rel = tensors(nc, ctx, pa_sq=(P, 2, T), pa_rms=(P, 2, T), pa_g=(P, 2),
                                           pa_table=(HEADS, BIAS_N), pa_rel=(NB, HEADS))
        hot, = tensors(nc, ctx, pa_hot=(NB, BIAS_N))
        ps = ctx.enter_context(nc.psum_tensor("pa_ps", [P, 2, 512], F32))
        tr = ctx.enter_context(nc.psum_tensor("pa_tr", [P, 3, 512], F32))
        pt = ctx.enter_context(nc.psum_tensor("pa_pt", [P, 512], F32))
        (c_loaded, squared, summed, rooted, inverted, normed, turned, copied, tabled, table_out, spread,
         stored, doubled, copied_table) = (sem("pa_" + n) for n in (
             "c", "sq", "sum", "root", "inv", "normed", "turned", "copied", "tab", "tabout", "spread",
             "stored", "dup", "tabcp"))
        block = ctx.enter_context(nc.Block())
        NQ, NK = 8, 2
        share = shares(tiles, NQ + NK)

        @block.sync
        def _(sp):
            sp.dma_start(gqk[:], k.d_gqk[:]).then_inc(c_loaded, 16)
            sp.dma_start(rel[:], k.d_rel[:]).then_inc(c_loaded, 16)
            sp.dma_start(hot[:], k.d_hot[:]).then_inc(c_loaded, 16)
            sp.dma_start(k.ikd[0:HD, :], k.misc[0:HD, :]).then_inc(doubled, 16)
            sp.dma_start(k.ikd[HD:P, :], k.misc[0:HD, :]).then_inc(doubled, 16)
            sp.dma_start(k.o_ik[:], k.misc[0:HD, :]).then_inc(stored, 16)
            sp.dma_start(k.o_v[:], k.att[:, V0:V0 + 2, :]).then_inc(stored, 16)
            sp.wait_ge(copied_table, 1)
            sp.dma_start(k.s_table[:], table[:]).then_inc(table_out, 16)
            sp.wait_ge(table_out, 16)
            hankel = bass.AP(tensor=k.s_table.tensor, offset=0, ap=[[1, P], [BIAS_N, HEADS], [1, TP]])
            sp.dma_start(k.hankel[:], hankel).then_inc(spread, 16)
            for n in tiles:
                k.proj.load(sp, n + WSLOTS)
            sp.wait_ge(normed, NQ + NK)
            sp.dma_start(k.o_k[:], k.att[:, K0:K0 + 2, :]).then_inc(stored, 16)
            sp.wait_ge(spread, 16)
            sp.wait_ge(doubled, 32)
            sp.wait_ge(stored, 48)

        @block.scalar
        def _(act):
            def square(n):
                if n >= 2:
                    act.wait_ge(summed, n - 1)
                act.activation(sq[:, n % 2], k.att[:, n, :], ACT.Square).then_inc(squared, 1)

            square(0)
            square(1)
            for n in range(NQ + NK):
                act.wait_ge(summed, n + 1)
                if n >= 2:
                    act.wait_ge(normed, n - 1)
                if n < NQ:
                    act.activation(rms[:, n % 2], ps[:, n % 2, 0:T], ACT.Sqrt, bias=k.eps64).then_inc(rooted, 1)
                else:
                    act.activation(rms[:, n % 2], ps[:, n % 2, 0:T], ACT.Sqrt, scale=1.0 / HD,
                                   bias=k.eps).then_inc(rooted, 1)
                if n + 2 < NQ + NK:
                    square(n + 2)
                for tile in share[n]:
                    k.proj.evacuate(act, tile)

        @block.tensor
        def _(pe):
            pe.wait_ge(c_loaded, 48)
            pe.matmul(pt[0:HEADS, 0:BIAS_N], rel[:], hot[:], start=True, stop=True).then_inc(tabled, 1)
            for c, at in enumerate((0, P, TP)):
                n = P if at < TP else TS
                for i, src in enumerate((k.att[:, V0, at:at + n], k.att[:, V0 + 1, at:at + n],
                                         k.misc[:, at:at + n])):
                    mm = pe.transpose(tr[0:n, c, i * P:(i + 1) * P], src, k.ident)
                mm.then_inc(turned, 1)
            for n in range(NQ + NK):
                pe.wait_ge(squared, n + 1)
                if n >= 2:
                    pe.wait_ge(rooted, n - 1)
                pe.matmul(ps[:, n % 2, 0:T], k.block, sq[:, n % 2], start=True, stop=True).then_inc(summed, 1)
                for tile in share[n]:
                    k.proj.multiply(pe, tile)

        @block.vector
        def _(dve):
            dve.wait_ge(tabled, 1)
            dve.tensor_copy(table[:], pt[0:HEADS, 0:BIAS_N]).then_inc(copied_table, 1)
            for c in range(2):
                dve.wait_ge(turned, c + 1)
                dve.tensor_copy(k.vnat[:, c, :], tr[:, c, 0:2 * P]).then_inc(copied, 1)
                dve.tensor_copy(k.mnat[:, c, :], tr[:, c, 2 * P:3 * P]).then_inc(copied, 1)
            dve.wait_ge(turned, 3)
            dve.tensor_copy(k.vnew[:], tr[0:TS, 2, 0:2 * P]).then_inc(copied, 1)
            dve.wait_ge(copied, 5)
            for n in range(NQ + NK):
                dve.wait_ge(rooted, n + 1)
                dve.reciprocal(rms[:, n % 2], rms[:, n % 2]).then_inc(inverted, 1)
                dve.wait_ge(inverted, n + 1)
                g = gqk[:, 0:1] if n < NQ else gqk[:, 1:2]
                dve.scalar_tensor_tensor(out=k.att[:, n, :], in0=k.att[:, n, :], scalar=g, in1=rms[:, n % 2],
                                         op0=ALU.mult, op1=ALU.mult).then_inc(normed, 1)
                for tile in share[n]:
                    k.proj.convolve(dve, tile)
            dve.wait_ge(normed, NQ + NK)

        @block.gpsimd
        def _(pool):
            load_indexer_pages(pool, k, IK_FIRST, TS * PAGES)
            for tile in tiles:
                k.proj.tails(pool, tile)


def choose_prompt(nc, k, tiles):
    TAIL = 4
    with ExitStack() as ctx:
        sem = signals(nc, ctx)
        r, iw = tensors(nc, ctx, cp_r=(P, 4, TP), cp_iw=(P, 2, IH))
        score, = tensors(nc, ctx, cp_score=(P, 2, TP))
        top, = tensors(nc, ctx, cp_top=(P, 2, 8))
        ps = ctx.enter_context(nc.psum_tensor("cp_ps", [P, 4, 512], F32))
        weighed, multiplied, rectified, added, cut, found, replaced, masked, final = (sem("cp_" + n) for n in (
            "w", "mm", "relu", "add", "cut", "max", "rep", "mask", "final"))
        block = ctx.enter_context(nc.Block())
        steps = [(i, h) for i in range(2) for h in range(IH)]
        width = lambda i: P * (i + 1)
        share, tail = shares(tiles[:-TAIL], len(steps)), tiles[-TAIL:]

        @block.sync
        def _(sp):
            for n in tiles:
                k.proj.load(sp, n + WSLOTS)

        @block.tensor
        def _(pe):
            for n, (i, h) in enumerate(steps):
                if n >= 4:
                    pe.wait_ge(rectified, n - 3)
                half = slice(h % 2 * HD, h % 2 * HD + HD)
                pe.matmul(ps[:, n % 4, 0:width(i)], k.att[half, IQ0 + h // 2, i * P:(i + 1) * P],
                          k.ikd[half, 0:width(i)], start=True, stop=True).then_inc(multiplied, 1)
                for tile in share[n]:
                    k.proj.multiply(pe, tile)
            for tile in tail:
                k.proj.multiply(pe, tile)

        @block.scalar
        def _(act):
            for n, (i, h) in enumerate(steps):
                act.wait_ge(multiplied, n + 1)
                if n >= 4:
                    act.wait_ge(added, n - 3)
                act.activation(r[:, n % 4, 0:width(i)], ps[:, n % 4, 0:width(i)], ACT.Relu,
                               scale=HD ** -0.5).then_inc(rectified, 1)
                for tile in share[n]:
                    k.proj.evacuate(act, tile)
            for tile in tail:
                k.proj.evacuate(act, tile)

        @block.vector
        def _(dve):
            dve.tensor_scalar(iw[:], k.mnat[:, :, IW_P:IW_P + IH], IH ** -0.5, None, ALU.mult).then_inc(weighed, 1)
            dve.wait_ge(weighed, 1)
            for n, (i, h) in enumerate(steps):
                dve.wait_ge(rectified, n + 1)
                s = score[:, i, 0:width(i)]
                if h == 0:
                    dve.tensor_scalar(s, r[:, n % 4, 0:width(i)], iw[:, i, h:h + 1], None, ALU.mult
                                      ).then_inc(added, 1)
                else:
                    dve.wait_ge(added, n)
                    dve.scalar_tensor_tensor(out=s, in0=r[:, n % 4, 0:width(i)], scalar=iw[:, i, h:h + 1], in1=s,
                                             op0=ALU.mult, op1=ALU.add).then_inc(added, 1)
                for tile in share[n]:
                    k.proj.convolve(dve, tile)
            for step in range(SEL_P // 8):
                for i in range(2):
                    s = score[:, i, 0:width(i)]
                    n = 2 * step + i
                    if step == 0:
                        dve.wait_ge(cut, i + 1)
                    else:
                        dve.wait_ge(replaced, n - 1)
                    dve.max(top[:, i, :], s).then_inc(found, 1)
                    dve.wait_ge(found, n + 1)
                    dve.match_replace(s, top[:, i, :], s, LOW).then_inc(replaced, 1)
            for i in range(2):
                dve.wait_ge(replaced, SEL_P // 4 - 1 + i)
                dve.tensor_scalar(k.negp[:, i, 0:width(i)], score[:, i, 0:width(i)], LOW, NEG,
                                  ALU.not_equal, ALU.mult).then_inc(masked, 1)
            for tile in tail:
                k.proj.convolve(dve, tile)

        @block.gpsimd
        def _(pool):
            for tile in tiles:
                k.proj.tails(pool, tile)
            for i in range(2):
                pool.wait_ge(added, IH * (i + 1))
                s = score[:, i, i * P:(i + 1) * P]
                pool.affine_select(out=s, in_=s, compare_op=ALU.is_ge, fill=-1.0e38, base=0,
                                   pattern=[[-1, P]], channel_multiplier=1).then_inc(cut, 1)
            for i in range(2):
                pool.wait_ge(masked, i + 1)
                s = k.negp[:, i, i * P:(i + 1) * P]
                pool.affine_select(out=s, in_=s, compare_op=ALU.is_ge, fill=NEG, base=0,
                                   pattern=[[-1, P]], channel_multiplier=1).then_inc(final, 1)
            pool.wait_ge(final, 2)


def score_sample(nc, k):
    with ExitStack() as ctx:
        sem = signals(nc, ctx, "cs_")
        ikt, iqd, r, wsel = tensors(
            nc, ctx, cs_ikt=(P, 2, 512), cs_iqd=(P, TS, TS * IH), cs_r=(TS * IH, NKS),
            cs_wsel=(TS * IH, TS))
        tr = ctx.enter_context(nc.psum_tensor("cs_tr", [P, 2, 512], F32))
        small = ctx.enter_context(nc.psum_tensor("cs_small", [P, 512], F32))
        ps = ctx.enter_context(nc.psum_tensor("cs_ps", [P, 3, 512], F32))
        cleared, spread, diag, weighed, turned, copied, scored, rectified, summed, read = (sem(n) for n in (
            "clr", "spread", "diag", "w", "turn", "copy", "score", "relu", "sum", "read"))
        block = ctx.enter_context(nc.Block())

        ik = k.paged[:].rearrange("p (a d) -> p a d", d=HD)

        @block.tensor
        def _(pe):
            for h in range(IH):
                pe.matmul(small[:, h * TS:(h + 1) * TS], k.selhi if h % 2 else k.sello,
                               k.att[:, IQ0 + h // 2, TP:T], start=True, stop=True)
            pe.matmul(small[0:TS * IH, 128:128 + TS], k.iwsel, k.misc[:, TP:T], start=True, stop=True).then_inc(spread, 1)
            pe.wait_ge(k.ik_loaded, 16 * TS * PAGES)
            pe.wait_ge(diag, TS)

            def scores(b):
                pe.wait_ge(copied, b + 1)
                for half in range(2):
                    rows = slice(half * HD, half * HD + HD)
                    mm = pe.matmul(ps[0:TS * IH, half, :], iqd[rows, b, :], ikt[rows, b % 2, :],
                                   start=b == 0, stop=b == TS - 1)
                mm = pe.matmul(ps[0:TS * IH, 2, 0:1], iqd[0:HD, b, :], k.misc[0:HD, TP + b:TP + b + 1],
                               start=b == 0, stop=b == TS - 1)
                mm.then_inc(scored, 1)

            for b in range(TS + 1):
                if b < TS:
                    if b >= 2:
                        pe.wait_ge(copied, b - 1)
                    for j in range(PAGES // 2):
                        at = b * PAGES + 2 * j
                        mm = pe.transpose(tr[:, b % 2, j * P:(j + 1) * P],
                                          ik[:, at:at + 2, :].rearrange("p a d -> p (a d)"), k.ident)
                    mm.then_inc(turned, 1)
                if b:
                    scores(b - 1)
            pe.wait_ge(rectified, 1)
            pe.wait_ge(weighed, 2)
            for a, n in ((0, 512), (512, 512), (1024, 1)):
                mm = pe.matmul(ps[0:TS, a // 512, 0:n], wsel[:], r[:, a:a + n], start=True, stop=True)
            mm.then_inc(summed, 1)

        @block.scalar
        def _(act):
            for b in range(TS):
                act.wait_ge(turned, b + 1)
                if b >= 2:
                    act.wait_ge(scored, b - 1)
                act.activation(ikt[:, b % 2, :], tr[:, b % 2, :], ACT.Copy).then_inc(copied, 1)
            act.wait_ge(scored, TS)
            for half in range(2):
                act.activation(r[:, 0:PAST].rearrange("p (j a s) -> p j a s", a=2, s=PG)[:, :, half, :],
                               ps[0:TS * IH, half, :].rearrange("p (j s) -> p j s", s=PG), ACT.Relu, scale=HD ** -0.5)
            act.activation(r[:, PAST:NKS], ps[0:TS * IH, 2, 0:1], ACT.Relu, scale=HD ** -0.5).then_inc(rectified, 1)

        @block.vector
        def _(dve):
            dve.memset(iqd[:], 0.0).then_inc(cleared, 1)
            dve.wait_ge(cleared, 1)
            dve.wait_ge(spread, 1)
            for b in range(TS):
                dve.tensor_copy(iqd[:, b, b * IH:(b + 1) * IH],
                                small[:, 0:IH * TS].rearrange("p (h b) -> p h b", b=TS)[:, :, b]).then_inc(diag, 1)
            dve.tensor_scalar(wsel[:], small[0:TS * IH, 128:128 + TS], IH ** -0.5, None, ALU.mult).then_inc(weighed, 1)
            dve.wait_ge(weighed, 1)
            dve.tensor_tensor(wsel[:], wsel[:], k.own_ih, ALU.mult).then_inc(weighed, 1)
            dve.wait_ge(summed, 1)
            for a, n in ((0, 512), (512, 512), (1024, 1)):
                o = dve.tensor_copy(k.negs[:, a:a + n], ps[0:TS, a // 512, 0:n])
            o.then_inc(read, 1)
            dve.wait_ge(read, 1)


def attend_prompt(nc, k, tiles):
    NL, NPR, LAG_T, LAG_O = 3, 4, 2, 3
    with ExitStack() as ctx:
        sem = signals(nc, ctx)
        lg, pr, prt, st = tensors(nc, ctx, ap_l=(P, NL, TP), ap_p=(P, NPR, TP), ap_pt=(P, 2, TP), ap_st=(P, NPR, 4))
        psl = ctx.enter_context(nc.psum_tensor("ap_psl", [P, 2, 512], F32))
        pst = ctx.enter_context(nc.psum_tensor("ap_pst", [P, 2, 512], F32))
        pso = ctx.enter_context(nc.psum_tensor("ap_pso", [P, 2, 512], F32))
        logits, maxed, negated, expd, inverted, normed, turned, copied, mixed, out = (sem("ap_" + n) for n in (
            "logit", "max", "neg", "exp", "inv", "norm", "turn", "copy", "mix", "out"))
        top, = tensors(nc, ctx, cs_top=(TS, 8))
        found, replaced, masked = (sem("cs_" + n) for n in ("max", "rep", "mask"))
        block = ctx.enter_context(nc.Block())
        steps = [(i, j, half, r) for i in range(2) for j in range(2) for half in range(2) for r in range(REP)]
        N = len(steps)
        share = shares(tiles, N) + [[]] * LAG_O
        assert SEL_S // 8 == N
        width = lambda i: P * (i + 1)

        @block.sync
        def _(sp):
            for n in tiles:
                k.proj.load(sp, n + WSLOTS)
            sp.wait_ge(k.proj.saved, KC)
            sp.dma_start(k.o_conv_p[:], k.proj.tail_p[:]).then_inc(k.proj.stored, 16)
            sp.dma_start(k.o_conv_s[:], k.proj.tail_s[:]).then_inc(k.proj.stored, 16)
            sp.wait_ge(k.proj.stored, 32)

        @block.gpsimd
        def _(pool):
            for n in tiles:
                k.proj.tails(pool, n)

        @block.tensor
        def _(pe):
            for m in range(N + LAG_O):
                if m < N:
                    i, j, half, r = steps[m]
                    if m >= 2:
                        pe.wait_ge(maxed, m - 1)
                    rows = slice(half * HD, half * HD + HD)
                    o = psl[:, m % 2, 0:width(i)]
                    pe.matmul(o, k.att[rows, 4 * j + r, i * P:(i + 1) * P], k.att[rows, K0 + j, 0:width(i)],
                              start=True, stop=False)
                    pe.matmul(o, k.flip, k.hankel[:, 8 * j + 4 * half + r, TP - width(i):TP],
                              start=False, stop=True).then_inc(logits, 1)
                n = m - LAG_T
                if 0 <= n < N:
                    i = steps[n][0]
                    pe.wait_ge(normed, n + 1)
                    if n >= 2:
                        pe.wait_ge(copied, n - 1)
                    for c in range(i + 1):
                        mm = pe.transpose(pst[:, n % 2, c * P:(c + 1) * P], pr[:, n % NPR, c * P:(c + 1) * P], k.ident)
                    mm.then_inc(turned, 1)
                n = m - LAG_O
                if n >= 0:
                    i, j = steps[n][0:2]
                    pe.wait_ge(copied, n + 1)
                    if n >= 2:
                        pe.wait_ge(out, n - 1)
                    for c in range(i + 1):
                        mm = pe.matmul(pso[:, n % 2, 0:P], k.vnat[:, c, j * P:(j + 1) * P],
                                       prt[:, n % 2, c * P:(c + 1) * P], start=c == 0, stop=c == i)
                    mm.then_inc(mixed, 1)
                for tile in share[m]:
                    k.proj.multiply(pe, tile)

        @block.vector
        def _(dve):
            for m in range(N + 1):
                if m < N:
                    i = steps[m][0]
                    w = width(i)
                    dve.wait_ge(logits, m + 1)
                    if m >= NL:
                        dve.wait_ge(expd, m - NL + 1)
                    if m >= NPR:
                        dve.wait_ge(normed, m - NPR + 1)
                    s = st[:, m % NPR]
                    dve.tensor_tensor_reduce(lg[:, m % NL, 0:w], psl[:, m % 2, 0:w], k.negp[:, i, 0:w], 1.0, LOW,
                                             ALU.add, ALU.max, s[:, 0:1]).then_inc(maxed, 1)
                    dve.wait_ge(maxed, m + 1)
                    dve.tensor_scalar(s[:, 1:2], s[:, 0:1], -1.0, None, ALU.mult).then_inc(negated, 1)
                if m >= 1:
                    n = m - 1
                    w = width(steps[n][0])
                    s = st[:, n % NPR]
                    dve.wait_ge(expd, n + 1)
                    dve.reciprocal(s[:, 3:4], s[:, 2:3]).then_inc(inverted, 1)
                    dve.wait_ge(inverted, n + 1)
                    dve.tensor_scalar(pr[:, n % NPR, 0:w], pr[:, n % NPR, 0:w], s[:, 3:4], None, ALU.mult
                                      ).then_inc(normed, 1)
                if m < N:
                    if m:
                        dve.wait_ge(replaced, m)
                    dve.max(top[:], k.negs[:]).then_inc(found, 1)
                    dve.wait_ge(found, m + 1)
                    dve.match_replace(k.negs[:], top[:], k.negs[:], LOW).then_inc(replaced, 1)
                for tile in share[m]:
                    k.proj.convolve(dve, tile)
            dve.wait_ge(replaced, N)
            dve.tensor_scalar(k.negs[:], k.negs[:], LOW, NEG, ALU.not_equal, ALU.mult).then_inc(masked, 1)
            dve.wait_ge(masked, 1)

        @block.scalar
        def _(act):
            for m in range(N + LAG_O):
                if m < N:
                    w = width(steps[m][0])
                    act.wait_ge(negated, m + 1)
                    if m >= NPR:
                        act.wait_ge(turned, m - NPR + 1)
                    act.activation(pr[:, m % NPR, 0:w], lg[:, m % NL, 0:w], ACT.Exp, bias=st[:, m % NPR, 1:2],
                                   accum_out=st[:, m % NPR, 2:3]).then_inc(expd, 1)
                n = m - LAG_T
                if 0 <= n < N:
                    w = width(steps[n][0])
                    act.wait_ge(turned, n + 1)
                    if n >= 2:
                        act.wait_ge(mixed, n - 1)
                    act.activation(prt[:, n % 2, 0:w], pst[:, n % 2, 0:w], ACT.Copy).then_inc(copied, 1)
                n = m - LAG_O
                if n >= 0:
                    i, j, half, r = steps[n]
                    rows = slice(half * HD, half * HD + HD)
                    act.wait_ge(mixed, n + 1)
                    act.activation(k.yatt[rows, 4 * j + r, i * P:(i + 1) * P], pso[rows, n % 2, 0:P], ACT.Copy
                                   ).then_inc(out, 1)
                for tile in share[m]:
                    k.proj.evacuate(act, tile)
            act.wait_ge(out, N)


def time_steps(nc, k, tiles):
    NP_, ALL = 2 * SSDH, 2 * SSDH + TS
    with ExitStack() as ctx:
        sem = signals(nc, ctx)
        bias, alog, x, a, e, u, l, seg, both = tensors(nc, ctx, **{"ts_" + n: (P, ALL) for n in "bias alog x a e u l".split()},
                                                       ts_seg=(P, NP_), ts_both=(P, 2 * TS))
        spread, = tensors(nc, ctx, ts_spread=(P, D_INNER))
        ps = ctx.enter_context(nc.psum_tensor("ts_ps", [P, 512], F32))
        px = ctx.enter_context(nc.psum_tensor("ts_px", [P, 512], F32))
        c_loaded, cleared, step_v, step_a, cumulated, widened, last = (sem("ts_" + n) for n in (
            "c", "clear", "v", "a", "cum", "wide", "last"))
        block = ctx.enter_context(nc.Block())
        rows = slice(DT_P, P)

        @block.sync
        def _(sp):
            sp.dma_start(bias[:], k.d_dtb[:]).then_inc(c_loaded, 16)
            sp.dma_start(alog[:], k.d_alog[:]).then_inc(c_loaded, 16)
            sp.dma_start(spread[:], k.d_spread[:]).then_inc(c_loaded, 16)
            sp.dma_start(k.dskip[:], k.d_dskip[:]).then_inc(c_loaded, 16)
            for n in tiles:
                k.proj.load(sp, n + WSLOTS)

        @block.vector
        def _(dve):
            dve.memset(x[:], 0.0).then_inc(cleared, 1)
            dve.wait_ge(cleared, 1)
            dve.wait_ge(c_loaded, 64)
            dve.tensor_tensor(x[:, 0:NP_].rearrange("p (c h) -> p c h", c=2), k.mnat[:, :, DT_P:P],
                              bias[:, 0:NP_].rearrange("p (c h) -> p c h", c=2), ALU.add)
            dve.tensor_tensor(x[rows, NP_:ALL], k.misc[rows, TP:T], bias[rows, NP_:ALL], ALU.add).then_inc(step_v, 1)
            dve.wait_ge(step_a, 2)
            dve.tensor_scalar(u[:], e[:], 1.0, None, ALU.add).then_inc(step_v, 1)
            dve.wait_ge(step_v, 2)
            dve.scalar_tensor_tensor(out=a[:], in0=u[:], scalar=-1.0, in1=e[:], op0=ALU.add, op1=ALU.subtract
                                     ).then_inc(step_v, 1)
            dve.wait_ge(step_v, 3)
            dve.reciprocal(e[:], u[:]).then_inc(step_v, 1)
            dve.wait_ge(step_v, 4)
            dve.tensor_tensor(e[:], a[:], e[:], ALU.mult).then_inc(step_v, 1)
            dve.wait_ge(step_a, 3)
            dve.wait_ge(step_v, 5)
            dve.tensor_tensor(l[:], l[:], e[:], ALU.subtract).then_inc(step_v, 1)
            dve.wait_ge(step_v, 6)
            dve.scalar_tensor_tensor(out=k.dt[:], in0=x[:], scalar=0.0, in1=l[:], op0=ALU.max, op1=ALU.add
                                     ).then_inc(step_v, 1)
            dve.wait_ge(step_a, 4)
            dve.wait_ge(step_v, 7)
            dve.scalar_tensor_tensor(out=k.dA[:], in0=k.dt[:], scalar=-1.0, in1=alog[:], op0=ALU.mult, op1=ALU.mult
                                     ).then_inc(step_v, 1)
            dve.tensor_copy(both[rows, 0:TS], k.dt[rows, NP_:ALL]).then_inc(step_v, 1)
            dve.wait_ge(cumulated, 1)
            dve.tensor_scalar(k.nac[:], ps[:, 0:NP_], -1.0, None, ALU.mult).then_inc(step_v, 1)
            dve.wait_ge(step_v, 10)
            dve.tensor_tensor(seg[:], k.nac[:], ps[:, NP_:2 * NP_], ALU.add).then_inc(step_v, 1)
            dve.wait_ge(step_a, 6)
            dve.tensor_tensor(k.dec[:], seg[:], k.dt[:, 0:NP_], ALU.mult).then_inc(last, 1)
            dve.wait_ge(widened, 1)
            dve.tensor_copy(k.ex[:], px[:, 0:KI * 2 * TS].rearrange("p (c n) -> p c n", c=KI)).then_inc(last, 1)
            dve.wait_ge(last, 2)

        @block.scalar
        def _(act):
            act.wait_ge(step_v, 1)
            act.activation(a[:], x[:], ACT.Abs).then_inc(step_a, 1)
            act.wait_ge(step_a, 1)
            act.activation(e[:], a[:], ACT.Exp, scale=-1.0).then_inc(step_a, 1)
            act.wait_ge(step_v, 2)
            act.activation(l[:], u[:], ACT.Ln).then_inc(step_a, 1)
            act.wait_ge(c_loaded, 64)
            act.activation(alog[:], alog[:], ACT.Exp).then_inc(step_a, 1)
            act.wait_ge(step_v, 9)
            act.activation(both[rows, TS:2 * TS], k.dA[rows, NP_:ALL], ACT.Exp).then_inc(step_a, 1)
            act.wait_ge(step_v, 11)
            act.activation(seg[:], seg[:], ACT.Exp).then_inc(step_a, 1)
            act.activation(k.etot[:], ps[:, NP_:2 * NP_], ACT.Exp).then_inc(step_a, 1)
            for n in tiles:
                k.proj.evacuate(act, n)
            act.wait_ge(step_a, 7)

        @block.tensor
        def _(pe):
            for n in tiles:
                k.proj.multiply(pe, n)
            pe.wait_ge(step_v, 8)
            pe.matmul(ps[:, 0:NP_], k.tri, k.dA[:, 0:NP_], start=True, stop=True)
            pe.matmul(ps[:, NP_:2 * NP_], k.ones, k.dA[:, 0:NP_], start=True, stop=True).then_inc(cumulated, 1)
            pe.wait_ge(step_v, 9)
            pe.wait_ge(step_a, 5)
            for c in range(KI):
                mm = pe.matmul(px[:, c * 2 * TS:(c + 1) * 2 * TS], spread[rows, c * P:(c + 1) * P], both[rows, :],
                               start=True, stop=True, tile_position=(DT_P, 0))
            mm.then_inc(widened, 1)


def ssd_chunk(nc, k, c):
    t0 = c * P
    with ExitStack() as ctx:
        sem = signals(nc, ctx, f"sc{c}_")
        xdt, xdec, bnat, cb, lm, em, mx, ea, ce = tensors(
            nc, ctx, **{f"sc{c}_{n}": s for n, s in dict(
                xdt=(P, D_INNER), xdec=(P, D_INNER), bnat=(P, GROUPS, P), cb=(P, GROUPS, P), lm=(P, 2, 4, P),
                em=(P, 2, 4, P), mx=(P, 2, 4, P), ea=(P, 2, 4, P), ce=(P, 2, 4, P)).items()})
        if c:
            sq, = tensors(nc, ctx, sn_sq=(P, 2, 2, T))
        tr = ctx.enter_context(nc.psum_tensor(f"sc{c}_tr", [P, 2, 512], F32))
        pl = ctx.enter_context(nc.psum_tensor(f"sc{c}_pl", [P, 2, 4, P], F32))
        py = ctx.enter_context(nc.psum_tensor(f"sc{c}_py", [P, 2, 512], F32))
        ph = ctx.enter_context(nc.psum_tensor(f"sc{c}_ph", [P, 512], F32))
        (turned, drained_v, drained_a, crossed, crossed_out, cumulated, lm_ready, ea_ready, em_ready, mixed,
         carried, y_done, y_skip, y_out, h_done, h_scaled, h_out) = (sem(n) for n in (
             "turn", "drv", "dra", "cross", "crossout", "cum", "lm", "ea", "em", "mix", "ce", "y", "yskip", "yout", "h",
             "hsc", "hout"))
        squared, normsummed, sums_out, stored = (sem(n) for n in ("nsq", "nsum", "nout", "store"))
        block = ctx.enter_context(nc.Block())
        heads = lambda a, h0, n: a[:, c * SSDH + h0:c * SSDH + h0 + n]

        @block.tensor
        def _(pe):
            for n in range(6):
                if n >= 2:
                    pe.wait_ge(drained_v, n - 1)
                for i in range(4):
                    mm = pe.transpose(tr[:, n % 2, i * P:(i + 1) * P], k.xbc[:, 4 * n + i, t0:t0 + P], k.ident)
                mm.then_inc(turned, 1)
            for n in range(2):
                pe.wait_ge(drained_a, n + 1)
                for i in range(4):
                    g = 4 * n + i
                    mm = pe.matmul(tr[:, n, i * P:(i + 1) * P], k.xbc[:, KI + g, t0:t0 + P],
                                   k.xbc[:, KI + GROUPS + g, t0:t0 + P], start=True, stop=True)
                mm.then_inc(crossed, 1)

            def outputs(g):
                pe.wait_ge(mixed, g + 1)
                if c:
                    pe.wait_ge(carried, g + 1)
                if g >= 2:
                    pe.wait_ge(y_skip, g - 1)
                for r in range(4):
                    h = 4 * g + r
                    o = py[r % 2 * HD:r % 2 * HD + HD, g % 2, r // 2 * P:(r // 2 + 1) * P]
                    mm = pe.matmul(o, xdt[:, h * HD:(h + 1) * HD], mx[:, g % 2, r, :], start=True, stop=c == 0)
                    if c:
                        mm = pe.matmul(o, k.hT[:, h * HD:(h + 1) * HD], ce[:, g % 2, r, :], start=False, stop=True)
                mm.then_inc(y_done, 1)

            def norm_sum(g):
                if not c or not 0 <= g < GROUPS:
                    return
                pe.wait_ge(squared, g + 1)
                if g < 2:
                    pe.wait_ge(crossed_out, 2)
                else:
                    pe.wait_ge(sums_out, g - 1)
                for i in range(2):
                    mm = pe.matmul(tr[:, g % 2, 0:T], k.ones, sq[:, g % 2, i, :], start=i == 0, stop=i == 1)
                mm.then_inc(normsummed, 1)

            def cumulate(g):
                if g == GROUPS:
                    return
                if g >= 2:
                    pe.wait_ge(lm_ready, g - 1)
                    if c:
                        pe.wait_ge(ea_ready, g - 1)
                for r in range(4):
                    dah = heads(k.dA, 4 * g + r, 1).broadcast_to([P, P])
                    mm = pe.matmul(pl[:, g % 2, r, :], dah, k.tri, start=True, stop=True)
                mm.then_inc(cumulated, 1)

            cumulate(0)
            for g in range(GROUPS):
                norm_sum(g - 3)
                if g:
                    outputs(g - 1)
                cumulate(g + 1)
                if g:
                    pe.wait_ge(h_out, g)
                else:
                    pe.wait_ge(drained_v, 4)
                pe.matmul(ph[:, 0:4 * HD], bnat[:, g, :], xdec[:, g * 4 * HD:(g + 1) * 4 * HD],
                          start=True, stop=True).then_inc(h_done, 1)
            outputs(GROUPS - 1)
            for g in range(GROUPS - 3, GROUPS):
                norm_sum(g)

        @block.scalar
        def _(act):
            for n in range(2):
                act.wait_ge(turned, 5 + n)
                act.activation(bnat[:, 4 * n:4 * n + 4, :].rearrange("p g n -> p (g n)"), tr[:, n, :], ACT.Copy
                               ).then_inc(drained_a, 1)
            for n in range(2):
                act.wait_ge(crossed, n + 1)
                act.activation(cb[:, 4 * n:4 * n + 4, :].rearrange("p g n -> p (g n)"), tr[:, n, :], ACT.Copy
                               ).then_inc(crossed_out, 1)
            def square(g):
                if c and 0 <= g < GROUPS:
                    act.wait_ge(y_out, g + 1)
                    if g >= 2:
                        act.wait_ge(normsummed, g - 1)
                    act.activation(sq[:, g % 2], k.Y[:, 2 * g:2 * g + 2, :], ACT.Square).then_inc(squared, 1)

            def sums(g):
                if c and 0 <= g < GROUPS:
                    act.wait_ge(normsummed, g + 1)
                    act.activation(k.rms[:, g, :], tr[:, g % 2, 0:T], ACT.Copy).then_inc(sums_out, 1)

            for g in range(GROUPS):
                act.wait_ge(lm_ready, g + 1)
                if c:
                    if g >= 2:
                        act.wait_ge(carried, g - 1)
                    act.activation(ea[:, g % 2], pl[:, g % 2], ACT.Exp).then_inc(ea_ready, 1)
                if g >= 2:
                    act.wait_ge(mixed, g - 1)
                for r in range(4):
                    e = act.activation(em[:, g % 2, r, :], lm[:, g % 2, r, :], ACT.Exp, bias=heads(k.nac, 4 * g + r, 1))
                e.then_inc(em_ready, 1)
                if c == 0:
                    act.wait_ge(h_done, g + 1)
                    act.activation(k.hT[:, g * 4 * HD:(g + 1) * 4 * HD], ph[:, 0:4 * HD], ACT.Copy).then_inc(h_out, 1)
                sums(g - 4)
                square(g - 2)
            for g in range(GROUPS, GROUPS + 4):
                sums(g - 4)
                square(g - 2)
            if c:
                act.wait_ge(sums_out, GROUPS)

        @block.vector
        def _(dve):
            if c == 0:
                dve.tensor_copy(k.Y[:, :, TP:T], k.ys[:])
            for n in range(4):
                dve.wait_ge(turned, n + 1)
                for out, f in ((xdt, k.dt), (xdec, k.dec)):
                    o = dve.tensor_tensor(out[:, n * 512:(n + 1) * 512].rearrange("p (h d) -> p h d", d=HD),
                                          tr[:, n % 2, :].rearrange("p (h d) -> p h d", d=HD),
                                          heads(f, 8 * n, 8).unsqueeze(2).broadcast_to([P, 8, HD]), ALU.mult)
                o.then_inc(drained_v, 1)

            def finish(g):
                dve.wait_ge(y_done, g + 1)
                if g:
                    dve.wait_ge(y_out, g)
                for i in range(2):
                    o = dve.scalar_tensor_tensor(out=k.Y[:, 2 * g + i, t0:t0 + P], in0=k.xbc[:, 2 * g + i, t0:t0 + P],
                                                 scalar=k.dskip[:, 2 * g + i:2 * g + i + 1],
                                                 in1=py[:, g % 2, i * P:(i + 1) * P], op0=ALU.mult, op1=ALU.add)
                o.then_inc(y_skip, 1)
                if c:
                    hg = k.hT[:, g * 4 * HD:(g + 1) * 4 * HD]
                    dve.wait_ge(h_done, g + 1)
                    dve.tensor_tensor(hg.rearrange("p (h d) -> p h d", d=HD), hg.rearrange("p (h d) -> p h d", d=HD),
                                      heads(k.etot, 4 * g, 4).unsqueeze(2).broadcast_to([P, 4, HD]), ALU.mult
                                      ).then_inc(h_scaled, 1)
                    dve.wait_ge(h_scaled, g + 1)
                    dve.tensor_tensor(hg, hg, ph[:, 0:4 * HD], ALU.add).then_inc(h_out, 1)
                dve.wait_ge(y_skip, g + 1)
                yg = k.Y[:, 2 * g:2 * g + 2, t0:t0 + P]
                dve.tensor_tensor(yg, yg, k.zs[:, 2 * g:2 * g + 2, t0:t0 + P], ALU.mult).then_inc(y_out, 1)

            for g in range(GROUPS):
                dve.wait_ge(cumulated, g + 1)
                if g >= 2:
                    dve.wait_ge(em_ready, g - 1)
                dve.tensor_tensor(lm[:, g % 2], pl[:, g % 2], k.negt.unsqueeze(1).broadcast_to([P, 4, P]), ALU.add
                                  ).then_inc(lm_ready, 1)
                if g == 0:
                    dve.wait_ge(crossed_out, 2)
                if g:
                    finish(g - 1)
                if c:
                    dve.wait_ge(ea_ready, g + 1)
                    ct = k.xbc[:, KI + GROUPS + g, t0:t0 + P].unsqueeze(1).broadcast_to([P, 4, P])
                    dve.tensor_tensor(ce[:, g % 2], ea[:, g % 2], ct, ALU.mult).then_inc(carried, 1)
                dve.wait_ge(em_ready, g + 1)
                dve.tensor_tensor(mx[:, g % 2], em[:, g % 2], cb[:, g, :].unsqueeze(1).broadcast_to([P, 4, P]),
                                  ALU.mult).then_inc(mixed, 1)
            finish(GROUPS - 1)
            dve.wait_ge(y_out, GROUPS)

        if c:
            @block.sync
            def _(sp):
                sp.wait_ge(h_out, GROUPS)
                sp.dma_start(k.o_ssm_p[:], k.hT[:]).then_inc(stored, 16)
                sp.wait_ge(stored, 16)


class SampleState:
    SLOTS, UNITS, CT, GT = 3, 2 * TS, KI // 2, GROUPS // 2

    def __init__(self, nc, ctx, k):
        self.k = k
        self.h, self.dtx, self.y, self.junk, self.skip = tensors(
            nc, ctx, ss_h=(P, self.SLOTS, KI, NST), ss_dtx=(P, KI, TS), ss_y=(P, KI, TS), ss_junk=(P, 4, NST),
            ss_skip=(P, KI, TS))
        self.pb = ctx.enter_context(nc.psum_tensor("ss_pb", [P, self.GT, NST], F32))
        self.pc = ctx.enter_context(nc.psum_tensor("ss_pc", [P, self.GT, NST], F32))
        sem = signals(nc, ctx, "ss_")
        self.loaded = [sem(f"ld{s}") for s in range(self.SLOTS)]
        self.stored = [sem(f"st{s}") for s in range(self.SLOTS)]
        self.scaled, self.b_ready, self.c_ready, self.faded, self.updated, self.read, self.closing = (
            sem(n) for n in ("dtx", "b", "c", "fade", "upd", "read", "close"))
        self.new = k.xbc[:, 0:KI, SAMP0:CV:4]

    def load(self, sp, b):
        s = b % self.SLOTS
        if b >= self.SLOTS:
            sp.wait_ge(self.stored[s], 16 * (b // self.SLOTS))
            sp.wait_ge(self.read, (b - self.SLOTS + 1) * KI)
        sp.dma_start(self.h[:, s], self.k.d_state[b]).then_inc(self.loaded[s], 16)

    def store(self, sp, b):
        sp.wait_ge(self.updated, KI * (b + 1))
        sp.dma_start(self.k.o_ssm_s[b], self.h[:, b % self.SLOTS]).then_inc(self.stored[b % self.SLOTS], 16)

    def all_stored(self, sp):
        for s in range(self.SLOTS):
            sp.wait_ge(self.stored[s], 16 * len(range(s, TS, self.SLOTS)))

    def spread(self, pe, u):
        k, at = self.k, SAMP0 + 4 * (u // 2)
        for out, first, ready, free in ((self.pb, KI, self.b_ready, self.updated),
                                        (self.pc, KI + GROUPS, self.c_ready, self.read)):
            if u:
                pe.wait_ge(free, u * self.CT)
            for i in range(self.GT):
                g = first + u % 2 * self.GT + i
                mm = pe.matmul(out[:, i, :], k.xbc[:, g, at:at + 1].broadcast_to([P, P]), k.ident,
                               start=True, stop=True)
            mm.then_inc(ready, 1)

    def fade(self, act, u):
        b, k = u // 2, self.k
        act.wait_ge(self.loaded[b % self.SLOTS], 16 * (b // self.SLOTS + 1))
        for i in range(self.CT):
            c = u % 2 * self.CT + i
            h = self.h[:, b % self.SLOTS, c, :]
            act.activation(h, h, ACT.Copy, scale=k.ex[:, c, TS + b:TS + b + 1]).then_inc(self.faded, 1)

    def update(self, dve, u):
        b, k = u // 2, self.k
        if u == 0:
            dve.tensor_tensor(self.dtx[:], self.new, k.ex[:, :, 0:TS], ALU.mult).then_inc(self.scaled, 1)
            dve.wait_ge(self.scaled, 1)
        dve.wait_ge(self.b_ready, u + 1)
        for i in range(self.CT):
            c = u % 2 * self.CT + i
            h = self.h[:, b % self.SLOTS, c, :]
            dve.wait_ge(self.faded, u * self.CT + i + 1)
            dve.scalar_tensor_tensor(out=h, in0=self.pb[:, i // 2, :], scalar=self.dtx[:, c, b:b + 1], in1=h,
                                     op0=ALU.mult, op1=ALU.add).then_inc(self.updated, 1)
        dve.wait_ge(self.c_ready, u + 1)
        for i in range(self.CT):
            c, n = u % 2 * self.CT + i, u * self.CT + i
            dve.wait_ge(self.updated, n + 1)
            if n >= 4:
                dve.wait_ge(self.read, n - 3)
            dve.tensor_tensor_reduce(self.junk[:, n % 4], self.h[:, b % self.SLOTS, c, :], self.pc[:, i // 2, :],
                                     1.0, 0.0, ALU.mult, ALU.add, self.y[:, c, b:b + 1]).then_inc(self.read, 1)

    def finish(self, dve):
        k = self.k
        dve.tensor_tensor(self.skip[:], self.new, k.dskip[:].unsqueeze(2).broadcast_to([P, KI, TS]), ALU.mult
                          ).then_inc(self.closing, 1)
        dve.wait_ge(self.closing, 1)
        dve.wait_ge(self.read, TS * KI)
        dve.tensor_tensor(self.skip[:], self.skip[:], self.y[:], ALU.add).then_inc(self.closing, 1)
        dve.wait_ge(self.closing, 2)
        dve.tensor_tensor(k.ys[:], self.skip[:], k.zs[:, :, TP:T], ALU.mult).then_inc(self.closing, 1)
        dve.wait_ge(self.closing, 3)


def attend_sample(nc, k):
    NG, GP = 4, 4
    with ExitStack() as ctx:
        sem = signals(nc, ctx, "as_")
        kt, qd, pr, prt = tensors(nc, ctx, as_kt=(P, 2, 4 * P),
                                      as_qd=(P, TS, 2, P), as_p=(P, NKS), as_pt=(P, PAGES, P))
        pd, pdt, st, rel = tensors(nc, ctx, as_pd=(P, TS), as_pdt=(TS, P), as_st=(P, 8), as_rel=(NB, P))
        hot = pr[0:NB, :]
        tr = ctx.enter_context(nc.psum_tensor("as_tr", [P, 2, 512], F32))
        pl = ctx.enter_context(nc.psum_tensor("as_pl", [P, 3, 512], F32))
        po = pl[:, 2, :]
        by_sp = [sem(f"lsp{s}") for s in range(NG)]
        by_pool = [sem(f"lpool{s}") for s in range(NG)]
        (c_loaded, cleared, diag, turned, copied, logits, maxed, negated, expd, normed, newed, p_turned,
         p_copied, mixed, out, o_turned, placed) = (sem(n) for n in (
             "c", "clr", "diag", "turn", "copy", "logit", "max", "neg", "exp", "norm", "new", "pturn", "pcopy",
             "mix", "out", "oturn", "placed"))
        ssd = SampleState(nc, ctx, k)
        EARLY = 12
        gates = LastGates(nc, ctx, k)
        block = ctx.enter_context(nc.Block())
        flat = qd[:].rearrange("p b j n -> p (b j n)")
        kv = k.paged[:].rearrange("p (g i n) -> p g i n", g=NG, i=GP)
        assert PAGES * TS // GP % NG == 0
        VK = PAGES * TS // GP
        after = [[]] * VK + [[0, 1]] + shares(range(2, N_LAST), TS)
        turn = [t for t, gs in enumerate(after) for _ in gs]
        weights_at = [VK + NG + 1 if t == VK else VK + NG + 2 * (t - VK) for t in turn]
        spans = ((0, 512), (512, 512), (PAST, 1))

        def load(eng, loaded, half, visit):
            if NG <= visit < VK + NG:
                eng.wait_ge(turned, 2 * (visit - NG + 1))
            elif visit >= VK + NG:
                eng.wait_ge(mixed, visit - VK - NG + 1)
            for i in (2 * half, 2 * half + 1):
                if visit < VK:
                    cache, at = k.d_ck, (visit % 2 * GP + i) * PAGES + visit // 2
                else:
                    cache, at = k.d_cv, (visit - VK) * GP + i
                page = eng.value_load(k.pages[0:1, at:at + 1], min_val=0, max_val=k.n_pool - 1)
                eng.dma_start(kv[:, visit % NG, i:i + 1, :], cache[bass.ds(page, 1)].rearrange("a s n -> s a n")
                              ).then_inc(loaded[visit % NG], 16)

        def arrived(pe, visit):
            pe.wait_ge(by_sp[visit % NG], 32 * (visit // NG + 1))
            pe.wait_ge(by_pool[visit % NG], 32 * (visit // NG + 1))

        @block.sync
        def _(sp):
            sp.dma_start(hot, k.d_hots[:]).then_inc(c_loaded, 16)
            sp.dma_start(rel[:], k.d_relbh[:]).then_inc(c_loaded, 16)
            for b in range(ssd.SLOTS):
                load(sp, by_sp, 0, b)
                ssd.load(sp, b)
            store_at = {6 + 2 * b: b for b in range(6)} | {24: 6, 28: 7}
            load_at = {7 + 2 * i: ssd.SLOTS + i for i in range(TS - ssd.SLOTS)}
            for visit in range(ssd.SLOTS, 2 * VK):
                load(sp, by_sp, 0, visit)
                if visit in store_at:
                    ssd.store(sp, store_at[visit])
                if visit in load_at:
                    ssd.load(sp, load_at[visit])
                if VK - gates.SLOTS <= visit < VK:
                    gates.load(sp, visit - VK + gates.SLOTS)
                for g, at in enumerate(weights_at):
                    if visit == at:
                        gates.load(sp, g + gates.SLOTS)
            ssd.all_stored(sp)

        @block.gpsimd
        def _(pool):
            for visit in range(2 * VK):
                load(pool, by_pool, 1, visit)

        @block.tensor
        def _(pe):
            pe.wait_ge(c_loaded, 32)
            pe.wait_ge(diag, 16)
            for n, (a, w) in enumerate(spans):
                pe.matmul(pl[:, n, 0:w], rel[:], hot[:, a:a + w], start=True, stop=False)

            def products(n):
                page, pair = n // 4, n % 4
                pe.wait_ge(copied, n + 1)
                for i in range(2):
                    for j in range(2):
                        mm = pe.matmul(pl[:, page // 4, page % 4 * P:(page % 4 + 1) * P], qd[:, 2 * pair + i, j, :],
                                       kt[:, n % 2, (2 * i + j) * P:(2 * i + j + 1) * P], start=False, stop=False)
                mm.then_inc(logits, 1)

            for n in range(4 * PAGES + 1):
                if n < 4 * PAGES:
                    page, pair = n // 4, n % 4
                    visit = n // 2
                    if n % 2 == 0:
                        arrived(pe, visit)
                    if n >= 2:
                        pe.wait_ge(copied, n - 1)
                    for i in range(2):
                        for j in range(2):
                            mm = pe.transpose(tr[:, n % 2, (2 * i + j) * P:(2 * i + j + 1) * P],
                                              kv[:, visit % NG, 2 * (n % 2) + i, j * P:(j + 1) * P], k.ident)
                    mm.then_inc(turned, 1)
                if n:
                    products(n - 1)
                if n % 2 == 1 and n // 2 < EARLY:
                    ssd.spread(pe, n // 2)
            for b in range(TS):
                for j in range(2):
                    pe.matmul(pl[:, 2, 0:1], qd[:, b, j, :], k.att[:, K0 + j, TP + b:TP + b + 1], start=False, stop=False)
            for n, (a, w) in enumerate(spans):
                mm = pe.matmul(pl[:, n, 0:w], k.rep_h, k.negs[:, a:a + w], start=False, stop=True)
            mm.then_inc(logits, 1)
            for g in after[VK]:
                gates.multiply(pe, g)
            pe.wait_ge(normed, 1)
            for n in range(2):
                for i in range(4):
                    mm = pe.transpose(tr[:, n, i * P:(i + 1) * P], pr[:, (4 * n + i) * P:(4 * n + i + 1) * P], k.ident)
                mm.then_inc(p_turned, 1)
            pe.wait_ge(newed, 1)
            pe.wait_ge(p_copied, 1)
            pe.transpose(tr[0:TS, 0, 0:P], pd[:], k.ident).then_inc(p_turned, 1)
            pe.wait_ge(p_copied, 4)
            for b in range(TS):
                rows, heads = slice(b % 4 * 32, b % 4 * 32 + HEADS), slice(b * HEADS, (b + 1) * HEADS)
                o = po[rows, b // 4 * 2 * P:(b // 4 + 1) * 2 * P]
                for part in range(2):
                    visit = VK + 2 * b + part
                    arrived(pe, visit)
                    for i in range(GP):
                        mm = pe.matmul(o, prt[:, GP * part + i, heads], kv[:, visit % NG, i, :],
                                       start=part + i == 0, stop=False, tile_position=(0, b % 4 * 32))
                    if part == 0:
                        mm.then_inc(mixed, 1)
                mm = pe.matmul(o, pdt[:, heads], k.vnew[:], start=False, stop=True, tile_position=(0, b % 4 * 32))
                mm.then_inc(mixed, 1)
                if EARLY + b < ssd.UNITS:
                    ssd.spread(pe, EARLY + b)
                for g in after[VK + 1 + b]:
                    gates.multiply(pe, g)
            pe.wait_ge(out, 4)
            for i in range(4):
                mm = pe.transpose(tr[:, 0, i * P:(i + 1) * P], pr[:, i * P:(i + 1) * P], k.ident)
            mm.then_inc(o_turned, 1)

        @block.scalar
        def _(act):
            for n in range(4 * PAGES):
                act.wait_ge(turned, n + 1)
                if n >= 2:
                    act.wait_ge(logits, n - 1)
                act.activation(kt[:, n % 2, :], tr[:, n % 2, :], ACT.Copy).then_inc(copied, 1)
                if n % 2 == 1 and n // 2 < EARLY:
                    ssd.fade(act, n // 2)
            for g in after[VK]:
                gates.evacuate(act, g)
            act.wait_ge(negated, 1)
            act.activation(pr[:, 0:PAST].rearrange("p (a n) -> p a n", n=512), pl[:, 0:2, :], ACT.Exp,
                           bias=st[:, 3:4], accum_out=st[:, 4:5])
            act.activation(pr[:, PAST:NKS], pl[:, 2, 0:1], ACT.Exp, bias=st[:, 3:4], accum_out=st[:, 5:6]
                           ).then_inc(expd, 1)
            for n in range(2):
                act.wait_ge(p_turned, n + 1)
                act.activation(prt[:, 4 * n:4 * n + 4, :], tr[:, n, :].rearrange("p (a n) -> p a n", n=P), ACT.Copy
                               ).then_inc(p_copied, 1)
            act.wait_ge(p_turned, 3)
            act.activation(pdt[:], tr[0:TS, 0, 0:P], ACT.Copy).then_inc(p_copied, 2)
            for b in range(TS):
                if EARLY + b < ssd.UNITS:
                    ssd.fade(act, EARLY + b)
                for g in after[VK + 1 + b]:
                    gates.evacuate(act, g)

        @block.vector
        def _(dve):
            dve.memset(qd[:], 0.0).then_inc(cleared, 1)
            dve.wait_ge(cleared, 1)
            for j in range(2):
                for half in range(2):
                    for r in range(REP):
                        rows = slice(half * HD, half * HD + HD)
                        at = j * P + 8 * j + 4 * half + r
                        dve.tensor_copy(flat[rows, at:at + (TS - 1) * (2 * P + HEADS) + 1:2 * P + HEADS],
                                        k.att[rows, 4 * j + r, TP:T]).then_inc(diag, 1)
            for u in range(EARLY):
                ssd.update(dve, u)
            dve.wait_ge(logits, 4 * PAGES + 1)
            dve.tensor_reduce(st[:, 0:1], pl[:, 0:2, :], AX.XY, ALU.max)
            dve.tensor_copy(st[:, 1:2], pl[:, 2, 0:1]).then_inc(maxed, 1)
            dve.wait_ge(maxed, 1)
            dve.tensor_tensor(st[:, 2:3], st[:, 0:1], st[:, 1:2], ALU.max).then_inc(maxed, 1)
            dve.wait_ge(maxed, 2)
            dve.tensor_scalar(st[:, 3:4], st[:, 2:3], -1.0, None, ALU.mult).then_inc(negated, 1)
            dve.wait_ge(expd, 1)
            dve.tensor_tensor(st[:, 6:7], st[:, 4:5], st[:, 5:6], ALU.add).then_inc(maxed, 1)
            dve.wait_ge(maxed, 3)
            dve.reciprocal(st[:, 7:8], st[:, 6:7]).then_inc(maxed, 1)
            dve.wait_ge(maxed, 4)
            dve.tensor_scalar(pr[:], pr[:], st[:, 7:8], None, ALU.mult).then_inc(normed, 1)
            dve.wait_ge(normed, 1)
            dve.tensor_scalar(pd[:], k.own_h, pr[:, PAST:NKS], None, ALU.mult).then_inc(newed, 1)
            for u in range(EARLY, ssd.UNITS):
                ssd.update(dve, u)
            ssd.finish(dve)
            dve.wait_ge(mixed, 2 * TS)
            for q in range(4):
                rows = slice(32 * q, 32 * q + HEADS)
                dve.tensor_copy(pr[rows, 0:4 * P], po[rows, :]).then_inc(out, 1)
            dve.wait_ge(o_turned, 1)
            o4 = tr[:, 0, :].rearrange("p (s j q c) -> p s j q c", s=2, j=2, q=4)
            for j in range(2):
                for half in range(2):
                    rows = slice(half * HD, half * HD + HD)
                    at = 8 * j + 4 * half
                    dve.tensor_copy(k.yatt[rows, 4 * j:4 * j + 4, TP:T].rearrange("p r (s q) -> p s q r", s=2),
                                    o4[rows, :, j, :, at:at + REP]).then_inc(placed, 1)
            dve.wait_ge(placed, 4)


def merge(nc, k):
    KB, SLOTS = KI + KD, 3
    with ExitStack() as ctx:
        sem = signals(nc, ctx, "mg_")
        w, wo, merged, part = tensors(nc, ctx, mg_w=(P, SLOTS, KB * P), mg_wo=(P, 4, KD * P), mg_m=(P, KD, T),
                                      mg_part=(P, 2, 2, T))
        gn, sq = tensors(nc, ctx, mg_g=(P, KI), mg_sq=(P, 2, T))
        pa = ctx.enter_context(nc.psum_tensor("mg_pa", [P, 2, 512], F32))
        pb = ctx.enter_context(nc.psum_tensor("mg_pb", [P, 2, 512], F32))
        po = ctx.enter_context(nc.psum_tensor("mg_po", [P, 2, 512], F32))
        pn = ctx.enter_context(nc.psum_tensor("mg_pn", [P, 512], F32))
        w_loaded = [sem(f"w{s}") for s in range(SLOTS)]
        wo_loaded = [sem(f"wo{s}") for s in range(4)]
        multiplied, gated, summed, out_done, added = (sem(n) for n in ("mm", "gate", "sum", "out", "add"))
        squared, square_summed, rms_ready = (sem(n) for n in ("sq", "sqsum", "rms2"))
        g_loaded, rooted, inverted, normed = (sem(n) for n in ("g", "root", "inv", "norm"))
        block = ctx.enter_context(nc.Block())

        @block.sync
        def _(sp):
            sp.dma_start(gn[:], k.d_gssd[:]).then_inc(g_loaded, 16)
            for n in range(KD):
                if n >= SLOTS:
                    sp.wait_ge(multiplied, n - SLOTS + 1)
                sp.dma_start(w[:, n % SLOTS, :], k.d_w_ab[n]).then_inc(w_loaded[n % SLOTS], 16)
            for n in range(KD):
                if n >= 4:
                    sp.wait_ge(out_done, n - 3)
                sp.dma_start(wo[:, n % 4, :], k.d_w_out[n]).then_inc(wo_loaded[n % 4], 16)

        @block.tensor
        def _(pe):
            def branch(n, out, columns, rhs):
                for c in columns:
                    if n == 0 and out is pa and c % 2 == 0:
                        pe.wait_ge(normed, c // 2 + 1)
                    mm = pe.matmul(out[:, n % 2, 0:T], w[:, n % SLOTS, c * P:(c + 1) * P], rhs(c),
                                   start=c == columns[0], stop=c == columns[-1])
                return mm

            def attention(n):
                pe.wait_ge(w_loaded[n % SLOTS], 16 * (n // SLOTS + 1))
                if n >= 2:
                    pe.wait_ge(gated, 2 * (n - 1))
                branch(n, pb, range(KI, KB), lambda c: k.yatt[:, c - KI, :])

            attention(0)
            attention(1)
            for n in range(KD):
                if n >= 2:
                    attention(n)
                branch(n, pa, range(KI), lambda c: k.Y[:, c, :]).then_inc(multiplied, 1)
            def square_sum(n):
                pe.wait_ge(squared, n + 1)
                pe.matmul(pn[:, 0:T], k.ones, sq[:, n % 2, :], start=n == 0, stop=n == KD - 1
                          ).then_inc(square_summed, 1)

            pe.wait_ge(summed, KD)
            for n in range(KD):
                pe.wait_ge(wo_loaded[n % 4], 16 * (n // 4 + 1))
                if n >= 2:
                    pe.wait_ge(added, n - 1)
                for c in range(KD):
                    mm = pe.matmul(po[:, n % 2, 0:T], wo[:, n % 4, c * P:(c + 1) * P], merged[:, c, :],
                                   start=c == 0, stop=c == KD - 1)
                mm.then_inc(out_done, 1)
                if n >= 2:
                    square_sum(n - 2)
            for n in range(KD - 2, KD):
                square_sum(n)

        @block.scalar
        def _(act):
            for g in range(GROUPS):
                act.activation(k.rms[:, g, :], k.rms[:, g, :], ACT.Sqrt, scale=1.0 / (2 * P), bias=k.eps
                               ).then_inc(rooted, 1)
            for n in range(KD):
                act.wait_ge(added, n + 1)
                if n >= 2:
                    act.wait_ge(square_summed, n - 1)
                act.activation(sq[:, n % 2, :], k.xT[:, n, :], ACT.Square).then_inc(squared, 1)
            act.wait_ge(square_summed, KD)
            act.activation(k.rms2[:], pn[:, 0:T], ACT.Sqrt, scale=1.0 / D_MODEL, bias=k.eps).then_inc(rms_ready, 1)
            act.wait_ge(rms_ready, 1)

        @block.vector
        def _(dve):
            dve.wait_ge(g_loaded, 16)
            for g in range(GROUPS):
                dve.wait_ge(rooted, g + 1)
                dve.reciprocal(k.rms[:, g, :], k.rms[:, g, :]).then_inc(inverted, 1)
                dve.wait_ge(inverted, g + 1)
                for i in (2 * g, 2 * g + 1):
                    o = dve.scalar_tensor_tensor(out=k.Y[:, i, :], in0=k.Y[:, i, :], scalar=gn[:, i:i + 1],
                                                 in1=k.rms[:, g, :], op0=ALU.mult, op1=ALU.mult)
                o.then_inc(normed, 1)
            for n in range(KD):
                dve.wait_ge(multiplied, n + 1)
                if n >= 2:
                    dve.wait_ge(summed, n - 1)
                dve.tensor_tensor(part[:, n % 2, 0], pa[:, n % 2, 0:T], k.gate[:, n, :], ALU.mult).then_inc(gated, 1)
                dve.tensor_tensor(part[:, n % 2, 1], pb[:, n % 2, 0:T], k.gate[:, KD + n, :], ALU.mult
                                  ).then_inc(gated, 1)
                dve.wait_ge(gated, 2 * n + 2)
                dve.tensor_tensor(merged[:, n, :], part[:, n % 2, 0], part[:, n % 2, 1], ALU.add).then_inc(summed, 1)
            for n in range(KD):
                dve.wait_ge(out_done, n + 1)
                dve.tensor_tensor(k.xT[:, n, :], k.xT[:, n, :], po[:, n % 2, 0:T], ALU.add).then_inc(added, 1)
            dve.wait_ge(added, KD)


def peer_queries(nc, k):
    NT = 2 * PH
    with ExitStack() as ctx:
        sem = signals(nc, ctx, "pq_")
        g2, w = tensors(nc, ctx, pq_g=(P, KD), pq_w=(P, WSLOTS, KD * P))
        ps = ctx.enter_context(nc.psum_tensor("pq_ps", [P, WSLOTS, 512], F32))
        w_loaded = [sem(f"w{s}") for s in range(WSLOTS)]
        g_loaded, k_loaded, inverted, normed, multiplied, evacuated = (sem(n) for n in ("g", "keys", "inv", "norm", "mm", "evac"))
        block = ctx.enter_context(nc.Block())

        @block.sync
        def _(sp):
            sp.dma_start(g2[:], k.d_g2[:]).then_inc(g_loaded, 16)
            for n in range(NT):
                if n >= WSLOTS:
                    sp.wait_ge(multiplied, n - WSLOTS + 1)
                sp.dma_start(w[:, n % WSLOTS, :], k.d_wq[n]).then_inc(w_loaded[n % WSLOTS], 16)
                if n == WSLOTS - 1:
                    sp.dma_start(k.keys[:], k.d_keys[:]).then_inc(k_loaded, 16)
            sp.wait_ge(k_loaded, 16)

        @block.scalar
        def _(act):
            for n in range(NT):
                act.wait_ge(multiplied, n + 1)
                act.activation(k.pq[:, n, :], ps[:, n % WSLOTS, 0:T], ACT.Copy).then_inc(evacuated, 1)
            act.wait_ge(evacuated, NT)

        @block.tensor
        def _(pe):
            for n in range(NT):
                pe.wait_ge(w_loaded[n % WSLOTS], 16 * (n // WSLOTS + 1))
                if n >= WSLOTS:
                    pe.wait_ge(evacuated, n - WSLOTS + 1)
                for c in range(KD):
                    if n == 0:
                        pe.wait_ge(normed, c + 1)
                    mm = pe.matmul(ps[:, n % WSLOTS, 0:T], w[:, n % WSLOTS, c * P:(c + 1) * P], k.hN[:, c, :],
                                   start=c == 0, stop=c == KD - 1)
                mm.then_inc(multiplied, 1)

        @block.vector
        def _(dve):
            dve.reciprocal(k.rms2[:], k.rms2[:]).then_inc(inverted, 1)
            dve.wait_ge(inverted, 1)
            dve.wait_ge(g_loaded, 16)
            for c in range(KD):
                dve.scalar_tensor_tensor(out=k.hN[:, c, :], in0=k.xT[:, c, :], scalar=g2[:, c:c + 1],
                                         in1=k.rms2[:], op0=ALU.mult, op1=ALU.mult).then_inc(normed, 1)


def peer(nc, k):
    RING = 8
    PER = PH * TOPK
    SPER = PER * TS // P
    TILES = ((0, P), (P, P), (TP, TS))
    with ExitStack() as ctx:
        sem = signals(nc, ctx, "pe_")
        s, v, cand, eq, tv, fa, fb, e1, e2, idf, gsm = tensors(
            nc, ctx, pe_s=(P, 2 * PH, PK), pe_v=(P, 2 * PH, TOPK), pe_cand=(P, PH, TOPK * TOPK),
            pe_eq=(P, PER, TOPK), pe_tv=(P, PH, TOPK), pe_fa=(P, PER), pe_fb=(P, PER), pe_e1=(P, PER),
            pe_e2=(P, PER), pe_idf=(P, 2 * PH, TOPK), pe_gs=(P, PH))
        uv, hnat, a, gl, wt, dg, y = tensors(
            nc, ctx, pe_uv=(P, RING, 2 * D_MODEL), pe_hnat=(P, 3, D_MODEL), pe_a=(P, RING), pe_gl=(P, RING),
            pe_w=(P, RING), pe_dg=(P, RING, P), pe_y=(P, D_MODEL))
        gw, gws, hrep = tensors(nc, ctx, pe_gw=(P, 3, PER), pe_gws=(P, SPER), pe_hrep=(P, KD, P))
        ints = lambda n, *shape, dt=U32: ctx.enter_context(nc.sbuf_tensor(n, list(shape), dt))
        iv, tp, pa, idx, idxs = (ints("pe_iv", P, 2 * PH, TOPK), ints("pe_tp", P, PH, TOPK),
                                      ints("pe_pa", P, 2, PER), ints("pe_idx", P, 3, PER, dt=I32),
                                 ints("pe_idxs", P, SPER, dt=I32))
        ps = ctx.enter_context(nc.psum_tensor("pe_ps", [P, 4, 4, P], F32))
        ph = ctx.enter_context(nc.psum_tensor("pe_ph", [P, KD, P], F32))
        acc = ctx.enter_context(nc.psum_tensor("pe_acc", [P, KD, P], F32))
        repeated = sem("rep")
        gathered = [sem(f"ga{i}") for i in range(RING)]
        (scored, s_read, h_turned, h_read, step, subtracted, chosen, to_dram, moved, exped, indexed, dotted, gelued, weighed,
         diagonal, accumulated, y_read, y_out) = (sem(n) for n in (
             "score", "sread", "hturn", "hread", "step", "sub", "chosen", "todram", "moved", "exp", "index", "dot", "gelu",
             "w", "diag", "acc", "yread", "yout"))
        block = ctx.enter_context(nc.Block())
        BEFORE = (0, PER, 2 * PER)
        LOOPS = (PER // RING, PER // RING, SPER // RING)
        CHOICES = ((0, 0, 1), (0, 1, 3), (0, 3, PH), (1, 0, PH), (2, 0, PH))
        FIRST = sum(n == 0 for n, _, _ in CHOICES)
        TURNS = ((0, 1), (1, 5), (5, 10), (10, LOOPS[0]))
        PACE = (2, 1, 1, 1)

        @block.tensor
        def _(pe):
            def scores(n):
                t0, m = TILES[n]
                if n:
                    pe.wait_ge(s_read, n + FIRST - 1)
                for i in range(2 * PH):
                    mm = pe.matmul(ps[0:m, i // 4, i % 4, :], k.pq[:, i, t0:t0 + m], k.keys[:, i, :],
                                   start=True, stop=True)
                    if n == 0 and i % 4 == 3 or i == 2 * PH - 1 and n:
                        mm.then_inc(scored, 1)

            scores(0)
            for n in range(3):
                if n:
                    pe.wait_ge(h_read, n)
                if n == 2:
                    pe.wait_ge(repeated, KD)
                for c in range(KD):
                    h = k.hN[:, c, n * P:(n + 1) * P] if n < 2 else hrep[:, c, :]
                    mm = pe.matmul(ph[:, c, :], h, k.ident, start=True, stop=True)
                mm.then_inc(h_turned, 1)
            for n, (t0, m) in enumerate(TILES):
                if n:
                    pe.wait_ge(y_read, n)
                for c in range(KD):
                    pe.matmul(acc[0:m, c, :], k.xT[:, c, t0:t0 + m], k.ident, start=c % 4 == 0, stop=False,
                              skip_group_check=True)

                def steps(i):
                    for r in range(RING):
                        pe.wait_ge(diagonal, BEFORE[n] + i * RING + r + 1)
                        lhsT = dg[:, r, :] if n < 2 else dg[:, r, 0:TS]
                        for half in range(2):
                            mm = pe.matmul(acc[0:m, 4 * half:4 * half + 4, :], lhsT,
                                           uv[:, r, D_MODEL + half * 512:D_MODEL + (half + 1) * 512],
                                           start=False, stop=False, skip_group_check=True)
                        mm.then_inc(accumulated, 1)
                if n == 0:
                    for c, turns in enumerate(TURNS):
                        if c >= FIRST - 1:
                            scores(c - FIRST + 2)
                        with pe.Fori(*turns) as i:
                            steps(i)
                elif n == 1:
                    with pe.Fori(0, LOOPS[n]) as i:
                        steps(i)
                else:
                    steps(0)

        @block.scalar
        def _(act):
            def exponents(c):
                n, h0, h1 = CHOICES[c]
                g = gw[0:TILES[n][1], n, h0 * TOPK:h1 * TOPK]
                act.wait_ge(subtracted, c + 1)
                act.activation(g, g, ACT.Exp).then_inc(exped, 1)

            for n in range(3):
                act.wait_ge(h_turned, n + 1)
                act.activation(hnat[:, n, :], ph[:].rearrange("p c d -> p (c d)"), ACT.Copy).then_inc(h_read, 1)
            exponents(0)
            for n, (t0, m) in enumerate(TILES):
                if n < 2:
                    act.wait_ge(chosen, 1 + FIRST * n)
                else:
                    act.wait_ge(moved, 32)

                def steps(i):
                    for r in range(RING):
                        at = BEFORE[n] + i * RING + r
                        act.wait_ge(dotted, at + 1)
                        act.activation(gl[:, r:r + 1], a[:, r:r + 1], ACT.Gelu_apprx_tanh).then_inc(gelued, 1)
                        act.wait_ge(gelued, at + 1)
                        g = gw[:, n, bass.ds(i * RING + r, 1)] if n < 2 else gws[:, bass.ds(i * RING + r, 1)]
                        act.activation(wt[:, r:r + 1], gl[:, r:r + 1], ACT.Copy, scale=g).then_inc(weighed, 1)
                        act.wait_ge(weighed, at + 1)
                        if n < 2:
                            act.activation(dg[:, r, :], k.ident, ACT.Copy, scale=wt[:, r:r + 1]).then_inc(diagonal, 1)
                        else:
                            act.activation(dg[:, r, 0:TS], k.own_h, ACT.Copy, scale=wt[:, r:r + 1]
                                           ).then_inc(diagonal, 1)
                if n == 0:
                    for c, turns in enumerate(TURNS):
                        with act.Fori(*turns) as i:
                            steps(i)
                        exponents(c + 1)
                        if c < FIRST - 1:
                            act.wait_ge(chosen, c + 2)
                elif n == 1:
                    with act.Fori(0, LOOPS[n]) as i:
                        steps(i)
                else:
                    steps(0)
                act.wait_ge(accumulated, BEFORE[n] + LOOPS[n] * RING)
                if n:
                    act.wait_ge(y_out, 16 * n)
                act.activation(y[0:m, :], acc[0:m].rearrange("p c d -> p (c d)"), ACT.Copy).then_inc(y_read, 1)
                act.wait_ge(y_read, n + 1)
                act.dma_start(k.o_y[t0:t0 + m, :], y[0:m, :]).then_inc(y_out, 16)
            act.wait_ge(y_out, 48)

        @block.gpsimd
        def _(pool):
            for c in range(KD):
                pool.tensor_copy(hrep[:, c, :].rearrange("p (b i) -> p b i", b=TS),
                                 k.hN[:, c, TP:T].unsqueeze(2).broadcast_to([P, TS, P // TS])).then_inc(repeated, 1)
            for n in range(3):
                if n == 2:
                    pool.wait_ge(moved, 32)

                for i in range(LOOPS[n] * RING):
                    at = BEFORE[n] + i
                    r = at % RING
                    for c, (tile, h0, h1) in enumerate(CHOICES[0:-1]):
                        if (tile, h0 * TOPK) == (n, i):
                            pool.wait_ge(indexed, c + 1)
                    if at >= RING:
                        pool.wait_ge(accumulated, at - RING + 1)
                    src = idx[:, n, i:i + 1] if n < 2 else idxs[:, i:i + 1]
                    pool.indirect_dma_start(uv[:, r, :], None, k.d_uv[:], bass.IndirectOffsetOnAxis(
                        ap=src, axis=0)).then_inc(gathered[r], 16)

        @block.sync
        def _(sp):
            sp.wait_ge(chosen, len(CHOICES))
            sp.dma_start(k.s_idx[:], idx[0:TS, 2, :]).then_inc(to_dram, 16)
            sp.dma_start(k.s_gw[:], gw[0:TS, 2, :]).then_inc(to_dram, 16)
            sp.wait_ge(to_dram, 32)
            sp.dma_start(idxs[:], k.s_idx.rearrange("b (p n) -> (b p) n", n=SPER)).then_inc(moved, 16)
            sp.dma_start(gws[:], k.s_gw.rearrange("b (p n) -> (b p) n", n=SPER)).then_inc(moved, 16)

        @block.vector
        def _(dve):
            done = 0

            def one(instruction):
                nonlocal done
                instruction.then_inc(step, 1)
                done += 1

            def settled():
                dve.wait_ge(step, done)

            def largest(lists, rest, values, places, read=None):
                for half in range(2):
                    c8 = slice(8 * half, 8 * half + 8)
                    for n, (x, o) in enumerate(zip(lists, values)):
                        one(dve.max(o[:, c8], x))
                        if n % 4 == 3:
                            yield
                    settled()
                    for n, (x, o, p) in enumerate(zip(lists, values, places)):
                        one(dve.max_index(p[:, c8], o[:, c8], x))
                        if n % 4 == 3:
                            yield
                    if half == 0:
                        settled()
                        for n, (x, y, o) in enumerate(zip(lists, rest, values)):
                            ins = dve.match_replace(y, o[:, c8], x, LOW)
                            if read is not None and n == len(lists) - 1:
                                ins.then_inc(read, 1)
                                dve.wait_ge(read, reads + 1)
                            else:
                                one(ins)
                            if n % 4 == 3:
                                yield
                        settled()
                        lists = rest

            reads = 0

            def choose(c):
                nonlocal reads
                n, h0, h1 = CHOICES[c]
                m, H, N = TILES[n][1], h1 - h0, (h1 - h0) * TOPK
                halves, at = range(2 * h0, 2 * h1), slice(h0 * TOPK, h1 * TOPK)
                dve.wait_ge(scored, PH // 2 + n if n else (h1 + 1) // 2)
                yield from largest([ps[0:m, i // 4, i % 4, :] for i in halves], [s[0:m, i, :] for i in halves],
                                   [v[0:m, i, :] for i in halves], [iv[0:m, i, :] for i in halves], s_read)
                reads += 1
                settled()
                v4 = v[0:m, 2 * h0:2 * h1].rearrange("p (h c) i -> p h c i", c=2)
                one(dve.tensor_tensor(cand[0:m, h0:h1].rearrange("p h (i j) -> p h i j", j=TOPK),
                                      v4[:, :, 0, :].unsqueeze(3).broadcast_to([m, H, TOPK, TOPK]),
                                      v4[:, :, 1, :].unsqueeze(2).broadcast_to([m, H, TOPK, TOPK]), ALU.add))
                yield
                settled()
                sums = [cand[0:m, h, :] for h in range(h0, h1)]
                yield from largest(sums, sums, [tv[0:m, h, :] for h in range(h0, h1)],
                                   [tp[0:m, h, :] for h in range(h0, h1)])
                settled()
                dve.tensor_tensor(gw[0:m, n, at].rearrange("p (h i) -> p h i", h=H), tv[0:m, h0:h1],
                                  tv[0:m, h0:h1, 0:1].broadcast_to([m, H, TOPK]), ALU.subtract
                                  ).then_inc(subtracted, 1)
                flat = tp[0:m, h0:h1].rearrange("p h i -> p (h i)")
                one(dve.tensor_single_scalar(pa[0:m, 0, at], flat, 4, ALU.logical_shift_right))
                one(dve.tensor_single_scalar(pa[0:m, 1, at], flat, TOPK - 1, ALU.bitwise_and))
                one(dve.tensor_copy(idf[0:m, 2 * h0:2 * h1], iv[0:m, 2 * h0:2 * h1]))
                settled()
                one(dve.tensor_copy(fa[0:m, at], pa[0:m, 0, at]))
                one(dve.tensor_copy(fb[0:m, at], pa[0:m, 1, at]))
                yield
                i4 = idf[0:m, 2 * h0:2 * h1].rearrange("p (h c) i -> p h c i", c=2)
                for which, (f, e) in enumerate(((fa, e1), (fb, e2))):
                    settled()
                    one(dve.tensor_tensor(eq[0:m, at], f[0:m, at].unsqueeze(2).broadcast_to([m, N, TOPK]),
                                          k.iota[0:m].unsqueeze(1).broadcast_to([m, N, TOPK]), ALU.is_equal))
                    yield
                    settled()
                    e4 = eq[0:m, at].rearrange("p (h i) j -> p h i j", h=H)
                    one(dve.tensor_tensor(e4, e4, i4[:, :, which, :].unsqueeze(2).broadcast_to([m, H, TOPK, TOPK]),
                                          ALU.mult))
                    yield
                    settled()
                    one(dve.tensor_reduce(e[0:m, at], eq[0:m, at], AX.X, ALU.add))
                    yield
                settled()
                dve.scalar_tensor_tensor(out=idx[0:m, n, at], in0=e1[0:m, at], scalar=float(PK), in1=e2[0:m, at],
                                         op0=ALU.mult, op1=ALU.add).then_inc(indexed, 1)
                dve.wait_ge(indexed, c + 1)
                dve.wait_ge(subtracted, c + 1)

            def weights(c):
                n, h0, h1 = CHOICES[c]
                m, H = TILES[n][1], h1 - h0
                if c:
                    dve.wait_ge(chosen, c)
                dve.wait_ge(exped, c + 1)
                g3 = gw[0:m, n, h0 * TOPK:h1 * TOPK].rearrange("p (h i) -> p h i", h=H)
                one(dve.tensor_reduce(gsm[0:m, 0:H], g3, AX.X, ALU.add))
                settled()
                one(dve.reciprocal(gsm[0:m, 0:H], gsm[0:m, 0:H]))
                settled()
                dve.tensor_tensor(g3, g3, gsm[0:m, 0:H].unsqueeze(2).broadcast_to([m, H, TOPK]), ALU.mult
                                  ).then_inc(chosen, 1)

            def dot(n, i, r, fresh=False):
                at = BEFORE[n] + i * RING + r
                dve.wait_ge(gathered[r], (BEFORE[n] // RING + i + 1) * 16)
                if not fresh:
                    dve.wait_ge(gelued, at - RING + 1)
                dve.tensor_tensor_reduce(uv[:, r, 0:D_MODEL], uv[:, r, 0:D_MODEL], hnat[:, n, :], 1.0, 0.0,
                                         ALU.mult, ALU.add, a[:, r:r + 1]).then_inc(dotted, 1)

            for _ in choose(0):
                pass
            weights(0)
            dve.wait_ge(h_read, 3)
            for c, (first, end) in enumerate(TURNS):
                rest = choose(c + 1)
                for i in range(first, end):
                    for r in range(RING):
                        dot(0, i, r, i == 0)
                        for _ in range(PACE[c]):
                            next(rest, None)
                for _ in rest:
                    pass
                if c < FIRST - 1:
                    weights(c + 1)
            weights(FIRST)
            weights(FIRST + 1)
            with dve.Fori(0, LOOPS[1]) as i:
                for r in range(RING):
                    dot(1, i, r)
            for r in range(RING):
                dot(2, 0, r)


def attend(nc, k, ctx):
    k.att, k.ikd, k.vnat, k.vnew, k.paged = tensors(
        nc, ctx, att=(P, N_ATT, T), ikd=(P, T), vnat=(P, 2, 2 * P), vnew=(TS, 2 * P), paged=(P, TS * PAGES * HD))
    k.pages = ctx.enter_context(nc.sbuf_tensor("pages", [1, TS * PAGES], I32))
    k.negs, k.xn = tensors(nc, ctx, negs=(TS, NKS), xn=(P, KD, T))
    k.ik_loaded = signals(nc, ctx)("ik_loaded")
    with ExitStack() as projection:
        k.proj = Projection(nc, projection, k)
        ends = [Z0, Z0 + 6, Z0 + 14, END - BANKS, END]
        part = [list(range(a, b)) for a, b in zip(ends, ends[1:])]
        norm_in(nc, k)
        project_attention(nc, k)
        with ExitStack() as inner:
            k.hankel, k.negp = tensors(nc, inner, hankel=(P, HEADS, TP), negp=(P, 2, TP))
            prepare_attention(nc, k, part[0])
            choose_prompt(nc, k, part[1])
            score_sample(nc, k)
            attend_prompt(nc, k, part[2])
        time_steps(nc, k, part[3])
    attend_sample(nc, k)


def build(nc, ins, outs):
    k = Kept()
    (k.d_alog, k.d_cb, k.d_cik, k.d_ck, k.d_cst, k.d_cv, k.d_cw, k.d_cx, k.d_dskip, k.d_dtb, k.d_g1, k.d_g2,
     k.d_gqk, k.d_gssd, k.d_hot, k.d_hots, k.d_keys, k.d_old, k.d_pages, k.d_rel, k.d_relbh, k.d_spread,
     k.d_state, k.d_uv, k.d_w_ab, k.d_w_in, k.d_w_out, k.d_wq, k.d_xT)\
        = (ins[n] for n in IN_NAMES)
    (k.o_conv_p, k.o_conv_s, k.o_k, k.o_v, k.o_ik, k.o_y, k.o_ssm_p, k.o_ssm_s)\
        = (outs[n] for n in OUTS)
    k.n_pool = k.d_ck.shape[0]
    k.s_idx = nc.dram_tensor("s_idx", [TS, PH * TOPK], I32, kind="Internal").ap()
    k.s_gw = nc.dram_tensor("s_gw", [TS, PH * TOPK], F32, kind="Internal").ap()
    k.s_table = nc.dram_tensor("s_table", [HEADS, BIAS_N], F32, kind="Internal").ap()
    with ExitStack() as ctx:
        k.xT, k.cst, k.cx, k.rms2 = tensors(nc, ctx, xT=(P, KD, T), cst=(P, C_END), cx=(P, CX_N), rms2=(P, T))
        k.ident, k.ones, k.flip, k.tri, k.block, k.negt, k.sello, k.selhi = (
            k.cst[:, a:a + P] for a in range(0, C_END, P))
        k.eps, k.eps64 = k.cx[:, 0:1], k.cx[:, 1:2]
        k.iota, k.own_ih, k.own_h = k.cx[:, 16:32], k.cx[0:TS * IH, 32:40], k.cx[:, 40:48]
        k.iwsel, k.rep_h = k.cx[:, 64:128], k.cx[0:TS, 128:256]
        with ExitStack() as first:
            k.gate, k.yatt, k.misc, k.mnat, k.zs, k.xbc = tensors(
                nc, first, gate=(P, 2 * KD, T), yatt=(P, KD, T), misc=(P, T), mnat=(P, 2, P), zs=(P, KI, T),
                xbc=(P, KC, CV))
            k.dt, k.dA, k.nac, k.dec, k.etot, k.ex, k.dskip, k.ys = tensors(
                nc, first, dt=(P, 72), dA=(P, 72), nac=(P, 64), dec=(P, 64), etot=(P, 64), ex=(P, KI, 2 * TS),
                dskip=(P, KI), ys=(P, KI, TS))
            with ExitStack() as attention:
                attend(nc, k, attention)
            k.Y, k.rms = tensors(nc, first, Y=(P, KI, T), rms=(P, GROUPS, T))
            with ExitStack() as ssd:
                k.hT, = tensors(nc, ssd, hT=(P, D_INNER))
                ssd_chunk(nc, k, 0)
                ssd_chunk(nc, k, 1)
            merge(nc, k)
        k.hN, k.pq, k.keys = tensors(nc, ctx, hN=(P, KD, T), pq=(P, 2 * PH, T), keys=(P, 2 * PH, PK))
        peer_queries(nc, k)
        peer(nc, k)


OUTS = dict(o_conv_p=(P, KC, 3), o_conv_s=(P, KC, TS, 3), o_k=(P, 2, T), o_v=(P, 2, T), o_ik=(HD, T),
            o_y=(T, D_MODEL), o_ssm_p=(P, SSDH * HD), o_ssm_s=(TS, P, KI, NST))


def constants():
    c = np.zeros((P, C_END), np.float32)
    i = np.arange(P)
    c[:, C_ID:C_ID + P] = np.eye(P)
    c[:, C_ONES:C_ONES + P] = 1
    c[:, C_J:C_J + P] = np.eye(P)[::-1]
    c[:, C_TRI:C_TRI + P] = i[:, None] <= i[None]
    c[:, C_BLK:C_BLK + P] = i[:, None] // HD == i[None] // HD
    c[:, C_NEGT:C_NEGT + P] = np.where(i[:, None] <= i[None], 0, NEG)
    c[:, C_SELLO:C_SELLO + P] = i[:, None] == i[None] % HD
    c[:, C_SELHI:C_SELHI + P] = i[:, None] == HD + i[None] % HD
    x = np.zeros((P, CX_N), np.float32)
    x[:, 0], x[:, 1] = EPS, EPS * HD
    b = np.arange(TS)
    x[:, 16:32] = np.arange(TOPK)
    x[:, 32:40] = i[:, None] // IH == b
    x[:, 40:48] = i[:, None] // HEADS == b
    x[IW_P:IW_P + IH, 64:128] = np.arange(IH)[:, None] == np.arange(TS * IH)[None] % IH
    x[0:TS, 128:256] = b[:, None] == i[None] // HEADS
    return c, x


def bucket(dist):
    import math
    n = np.maximum(dist, 0)
    nf = np.maximum(n, 1).astype(np.float32)
    large = 16 + (np.log(nf / np.float32(16)) / np.float32(math.log(128 / 16)) * np.float32(16)).astype(np.int32)
    return np.where(n < 16, n, np.minimum(large, 31))


def kernel(x_prompt, x_sample, cache_k, cache_v, cache_idx_k, state_ssm, state_conv, page_table, rel_bias,
           norm1_g, w_in, conv_w, conv_b, dt_bias, a_log, d_skip, ssd_norm_g, q_norm_g, k_norm_g,
           w_branch_a, w_branch_b, w_out, norm2_g, peer_wq, peer_keys, peer_u, peer_v):
    import concourse.bacc as bacc
    from concourse.bass_utils import run_bass_kernel_spmd

    A = np.ascontiguousarray
    npa = np.asarray

    def chan(v):
        v = npa(v)
        v = v.reshape(*v.shape[:-1], v.shape[-1] // P, P)
        return A(np.moveaxis(v, (-1, -2), (0, 1)))

    def tiles(w):
        w = npa(w)
        return A(w.reshape(w.shape[0] // P, P, w.shape[1] // P, P).transpose(2, 1, 0, 3).reshape(
            w.shape[1] // P, P, w.shape[0]))

    def per_head(v):
        v = npa(v)[0]
        o = np.zeros((P, 2 * SSDH + TS), np.float32)
        o[:, :2 * SSDH] = np.tile(v, 2)[None]
        o[DT_P:, 2 * SSDH:] = v[:, None]
        return o

    spread = np.zeros((P, D_INNER), np.float32)
    spread[DT_P:] = np.arange(SSDH)[:, None] == np.arange(D_INNER)[None] // HD
    w = npa(w_in)[0]
    edges = np.cumsum((0, D_INNER, CONV_DIM, SSDH, HEADS * HD, KVH * HD, KVH * HD, IH * HD, HD, IH,
                       D_MODEL, D_MODEL))
    z, xbc, dt, q, kk, v, iq, ik, iw, ga, gb = (w[:, a:b] for a, b in zip(edges, edges[1:]))
    q = q.reshape(D_MODEL, 2, 2, REP, HD).transpose(0, 1, 3, 2, 4).reshape(D_MODEL, HEADS * HD)
    gap = np.zeros((D_MODEL, DT_P - IW_P - IH), np.float32)
    d_w_in = tiles(np.concatenate([q, kk, v, iq, ik, iw, gap, dt, z, xbc, ga, gb], axis=1))
    w_b = npa(w_branch_b)[0].reshape(2, 2, REP, HD, D_MODEL).transpose(0, 2, 1, 3, 4).reshape(HEADS * HD, D_MODEL)
    x = np.concatenate([npa(x_prompt)[0], npa(x_sample)[:, 0]], axis=0)
    d_cst, d_cx = constants()
    hot = (bucket(TP - 1 - np.arange(BIAS_N))[None] == np.arange(NB)[:, None]).astype(np.float32)
    arrays = dict(
        d_xT=chan(x), d_cst=d_cst, d_cx=d_cx, d_g1=chan(npa(norm1_g)[0]), d_w_in=d_w_in,
        d_cw=chan(npa(conv_w)[0]), d_cb=chan(npa(conv_b)[0]), d_old=chan(npa(state_conv)[0]),
        d_gqk=A(np.tile(np.stack([npa(q_norm_g)[0], npa(k_norm_g)[0]], axis=1), (2, 1))),
        d_rel=A(npa(rel_bias)), d_hot=hot,
        d_dtb=per_head(dt_bias), d_alog=per_head(a_log), d_spread=spread,
        d_dskip=chan(np.repeat(npa(d_skip)[0], HD)), d_gssd=chan(npa(ssd_norm_g)[0]),
        d_pages=A(npa(page_table).reshape(1, -1)), d_cik=A(npa(cache_idx_k)[0]),
        d_ck=A(npa(cache_k)[0].reshape(-1, PG, KVH * HD)), d_cv=A(npa(cache_v)[0].reshape(-1, PG, KVH * HD)),
        d_hots=(bucket(PAST - np.arange(NKS))[None] == np.arange(NB)[:, None]).astype(np.float32),
        d_relbh=A(np.tile(npa(rel_bias), (1, TS))),
        d_w_ab=tiles(np.concatenate([npa(w_branch_a)[0], w_b], axis=0)), d_w_out=tiles(npa(w_out)[0]),
        d_g2=chan(npa(norm2_g)[0]), d_wq=tiles(npa(peer_wq)[0]),
        d_keys=A(npa(peer_keys)[0].transpose(3, 1, 0, 2).reshape(PK, 2 * PH, PK)),
        d_uv=A(np.concatenate([npa(peer_u)[0], npa(peer_v)[0]], axis=1)),
        d_state=A(npa(state_ssm)[0].reshape(TS, KI, P, NST).transpose(0, 2, 1, 3)),
    )
    nc = bacc.Bacc("TRN2", target_bir_lowering=False, num_devices=1)
    ins = {n: nc.dram_tensor(n, list(a.shape), mybir.dt.from_np(a.dtype), kind="ExternalInput").ap()
           for n, a in arrays.items()}
    outs = {n: nc.dram_tensor(n, list(s), F32, kind="ExternalOutput").ap() for n, s in OUTS.items()}
    build(nc, ins, outs)
    r = run_bass_kernel_spmd(nc, [arrays], core_ids=[0]).results[0]

    def rows(o, n):
        return o.reshape(P, n, -1).transpose(2, 1, 0).reshape(-1, n * P)

    kn, vn, ikn = rows(r["o_k"], 2), rows(r["o_v"], 2), r["o_ik"].T
    heads = lambda a: A(a.reshape(-1, KVH, HD))
    conv_p = r["o_conv_p"].transpose(2, 1, 0).reshape(3, CONV_DIM)
    conv_s = r["o_conv_s"].transpose(2, 3, 1, 0).reshape(TS, 3, CONV_DIM)
    y = r["o_y"]
    ssm_p = r["o_ssm_p"].T.reshape(SSDH, HD, NST)
    ssm_s = r["o_ssm_s"].transpose(0, 2, 1, 3).reshape(TS, SSDH, HD, NST)
    return (A(y[None, :TP]), A(y[TP:, None]),
            heads(kn[:TP])[None, None], heads(vn[:TP])[None, None], A(ikn[:TP])[None, None],
            A(ssm_p)[None, None], A(conv_p)[None, None],
            A(heads(kn[TP:])[None, :, None]), A(heads(vn[TP:])[None, :, None]), A(ikn[TP:][None, :, None]),
            A(ssm_s)[None], A(conv_s)[None])
```
